# Optimizing a Trainium2 kernel written in Bass

```python
import jax, jax.numpy as jnp
from jax import lax
import numpy as np
import math
import jax
import jax.numpy as jnp

D_MODEL = 1024
BATCH = 1
SEQ = 1024
DEPTH = 2

CHUNK = 64
RW_HEAD_DIM = 64
RW_WIDTH = D_MODEL // 2
RW_HEADS = RW_WIDTH // RW_HEAD_DIM
DECAY_LORA = 64
AAA_LORA = 64
AT_HEAD_DIM = 64
AT_WIDTH = D_MODEL // 2
AT_HEADS = AT_WIDTH // AT_HEAD_DIM
LEFT_CHUNKS = 8
BAND_CHUNKS = LEFT_CHUNKS + 1
REL_CLIP = 2 * CHUNK
SG_CHUNK = 128
SG_WIDTH = D_MODEL
SG_GROUPS = 8
SG_GROUP_DIM = SG_WIDTH // SG_GROUPS
SHIFT_WIDTH = 3 * RW_WIDTH + DECAY_LORA + AAA_LORA
EVEN_IN = SHIFT_WIDTH + RW_WIDTH + 4 * AT_WIDTH
EVEN_MIX = RW_WIDTH + AT_WIDTH
ODD_IN = 3 * SG_WIDTH
RMS_EPS = 1e-6
LN_EPS = 1e-5
GN_EPS = 64e-5
NEG_INF = -1e30


def rmsnorm(x, g):
    x32 = x.astype(jnp.float32)
    y = x32 * lax.rsqrt(jnp.mean(x32 * x32, axis=-1, keepdims=True) + RMS_EPS)
    return (y * g.astype(jnp.float32)).astype(x.dtype)

def token_shift(p, mu):
    p_prev = jnp.pad(p, ((0, 0), (1, 0), (0, 0)))[:, :-1]
    return p + (p_prev - p) * mu

def rwkv7_mix(p_r, p_k, p_v, p_wd, p_ad, w0, w2, a0, a2, k_k, k_a, r_k, lnx_g, lnx_b):
    B, S, W = p_r.shape
    H, N = RW_HEADS, RW_HEAD_DIM
    f32 = jnp.float32
    r = p_r.astype(f32)
    k = p_k.astype(f32)
    v = p_v.astype(f32)
    w = -jax.nn.softplus(-(w0.astype(f32) + jnp.tanh(p_wd.astype(f32)) @ w2.astype(f32))) - 0.5
    decay = jnp.exp(-jnp.exp(w))
    a = jax.nn.sigmoid(a0.astype(f32) + p_ad.astype(f32) @ a2.astype(f32))
    heads = lambda t: t.reshape(B, S, H, N)
    kk = heads(k * k_k.astype(f32))
    kk = kk / jnp.maximum(jnp.sqrt(jnp.sum(kk * kk, axis=-1, keepdims=True)), 1e-12)
    k = k * (1.0 + (a - 1.0) * k_a.astype(f32))
    r_h, k_h, v_h, a_h = heads(r), heads(k), heads(v), heads(a)
    tm = lambda t: jnp.moveaxis(t, 1, 0)

    def step(state, inp):
        r_t, w_t, k_t, v_t, a_t, b_t = inp
        sa = jnp.einsum('bhvk,bhk->bhv', state, a_t)
        state = (state * w_t[:, :, None, :]
                 + sa[..., None] * b_t[:, :, None, :]
                 + v_t[..., None] * k_t[:, :, None, :])
        y_t = jnp.einsum('bhvk,bhk->bhv', state, r_t)
        return state, y_t

    s0 = jnp.zeros((B, H, N, N), f32)
    _, y = lax.scan(step, s0, (tm(r_h), tm(heads(decay)), tm(k_h), tm(v_h), tm(-kk), tm(kk * a_h)))
    y = jnp.moveaxis(y, 0, 1)
    mu = jnp.mean(y, axis=-1, keepdims=True)
    var = jnp.mean(jnp.square(y - mu), axis=-1, keepdims=True)
    y = ((y - mu) * lax.rsqrt(var + GN_EPS)).reshape(B, S, W)
    y = y * lnx_g.astype(f32) + lnx_b.astype(f32)
    bonus = jnp.sum(r_h * k_h * r_k.astype(f32), axis=-1, keepdims=True) * v_h
    y = y + bonus.reshape(B, S, W)
    return y.astype(p_r.dtype)

def chunk_attention(q, k, v, bias_table):
    B, S, W = q.shape
    H, Dh, L = AT_HEADS, AT_HEAD_DIM, CHUNK
    NC = S // L
    to_chunks = lambda t: t.reshape(B, NC, L, H, Dh).transpose(0, 3, 1, 2, 4)
    pad = ((0, 0), (0, 0), (LEFT_CHUNKS, 0), (0, 0), (0, 0))
    qc = to_chunks(q)
    kp = jnp.pad(to_chunks(k), pad)
    vp = jnp.pad(to_chunks(v), pad)
    qi = jnp.arange(L)
    kj = jnp.arange(BAND_CHUNKS * L)
    rel = LEFT_CHUNKS * L + qi[:, None] - kj[None, :]
    idx = jnp.clip(rel, -REL_CLIP, REL_CLIP) + REL_CLIP
    bias = bias_table[:, idx].astype(jnp.float32)
    scale = 1.0 / np.sqrt(Dh)

    def one_chunk(args):
        q_blk, c = args
        kb = lax.dynamic_slice_in_dim(kp, c, BAND_CHUNKS, axis=2).reshape(B, H, BAND_CHUNKS * L, Dh)
        vb = lax.dynamic_slice_in_dim(vp, c, BAND_CHUNKS, axis=2).reshape(B, H, BAND_CHUNKS * L, Dh)
        s = jnp.einsum('bhqd,bhkd->bhqk', q_blk, kb).astype(jnp.float32) * scale + bias
        valid = kj >= (LEFT_CHUNKS - c) * L
        s = jnp.where(valid[None, None, None, :], s, NEG_INF)
        p = jax.nn.softmax(s, axis=-1)
        return jnp.einsum('bhqk,bhkd->bhqd', p.astype(vb.dtype), vb)

    out = lax.map(one_chunk, (jnp.moveaxis(qc, 2, 0), jnp.arange(NC)))
    return out.transpose(1, 0, 3, 2, 4).reshape(B, S, W)

def spatial_gating(u, v, ln_g, ln_b, sg_w, sg_b):
    B, S, W = u.shape
    NB = S // SG_CHUNK
    v32 = v.astype(jnp.float32)
    mu = jnp.mean(v32, axis=-1, keepdims=True)
    var = jnp.mean(jnp.square(v32 - mu), axis=-1, keepdims=True)
    v = ((v32 - mu) * lax.rsqrt(var + LN_EPS) * ln_g.astype(jnp.float32)
         + ln_b.astype(jnp.float32)).astype(u.dtype)
    pos = jnp.arange(SG_CHUNK)
    mask = (pos[None, :] // CHUNK) <= (pos[:, None] // CHUNK)
    w = sg_w * mask[None].astype(sg_w.dtype)
    vb = v.reshape(B, NB, SG_CHUNK, SG_GROUPS, SG_GROUP_DIM)
    sv = jnp.einsum('gij,bnjgc->bnigc', w, vb) + sg_b.T[None, None, :, :, None]
    return u * sv.reshape(B, S, W)

def even_layer(h, g, w_in, shift_mu, w0, w2, a0, a2, k_k, k_a, r_k, lnx_g, lnx_b, att_bias, w_out):
    p = rmsnorm(h, g) @ w_in
    p_shift = token_shift(p[..., :SHIFT_WIDTH], shift_mu)
    p_r, p_k, p_v, p_wd, p_ad = jnp.split(
        p_shift, [RW_WIDTH, 2 * RW_WIDTH, 3 * RW_WIDTH, 3 * RW_WIDTH + DECAY_LORA], axis=-1)
    rest = p[..., SHIFT_WIDTH:]
    gate_a, q_b, k_b, v_b, gate_b = jnp.split(
        rest, [RW_WIDTH, RW_WIDTH + AT_WIDTH, RW_WIDTH + 2 * AT_WIDTH, RW_WIDTH + 3 * AT_WIDTH], axis=-1)
    y_a = rwkv7_mix(p_r, p_k, p_v, p_wd, p_ad, w0, w2, a0, a2, k_k, k_a, r_k, lnx_g, lnx_b)
    y_a = y_a * jax.nn.silu(gate_a)
    y_b = chunk_attention(q_b, k_b, v_b, att_bias) * jax.nn.silu(gate_b)
    return h + jnp.concatenate([y_a, y_b], axis=-1) @ w_out

def odd_layer(h, g, w_in, ln_g, ln_b, sg_w, sg_b, w_out):
    p = rmsnorm(h, g) @ w_in
    u, v, gate = jnp.split(p, [SG_WIDTH, 2 * SG_WIDTH], axis=-1)
    y = spatial_gating(jax.nn.gelu(u), jax.nn.gelu(v), ln_g, ln_b, sg_w, sg_b)
    return h + (y * jax.nn.silu(gate)) @ w_out

def first_inputs(seed: int = 0) -> dict:
    key = jax.random.key(seed)
    ks = jax.random.split(key, 24)
    ne = (DEPTH + 1) // 2
    no = DEPTH // 2
    nrm = lambda k, shape, s: jax.random.normal(k, shape, jnp.float32) * s
    return {
        "x": nrm(ks[0], (BATCH, SEQ, D_MODEL), 1.0),
        "norm_g": 1.0 + nrm(ks[1], (DEPTH, D_MODEL), 0.01),
        "w_in_e": nrm(ks[2], (ne, D_MODEL, EVEN_IN), D_MODEL ** -0.5),
        "shift_mu": jax.random.uniform(ks[3], (ne, SHIFT_WIDTH), jnp.float32),
        "rw_w0": jax.random.uniform(ks[4], (ne, RW_WIDTH), jnp.float32, -4.0, 1.0),
        "rw_w2": nrm(ks[5], (ne, DECAY_LORA, RW_WIDTH), 0.5 * DECAY_LORA ** -0.5),
        "rw_a0": nrm(ks[6], (ne, RW_WIDTH), 0.1),
        "rw_a2": nrm(ks[7], (ne, AAA_LORA, RW_WIDTH), 0.5 * AAA_LORA ** -0.5),
        "rw_kk": 0.85 + nrm(ks[8], (ne, RW_WIDTH), 0.02),
        "rw_ka": 1.0 + nrm(ks[9], (ne, RW_WIDTH), 0.02),
        "rw_rk": nrm(ks[10], (ne, RW_HEADS, RW_HEAD_DIM), 0.1),
        "rw_lnx_g": 1.0 + nrm(ks[11], (ne, RW_WIDTH), 0.01),
        "rw_lnx_b": nrm(ks[12], (ne, RW_WIDTH), 0.01),
        "att_bias": nrm(ks[13], (ne, AT_HEADS, 2 * REL_CLIP + 1), 0.1),
        "w_out_e": nrm(ks[14], (ne, EVEN_MIX, D_MODEL), 0.5 * EVEN_MIX ** -0.5),
        "w_in_o": nrm(ks[15], (no, D_MODEL, ODD_IN), D_MODEL ** -0.5),
        "sg_ln_g": 1.0 + nrm(ks[16], (no, SG_WIDTH), 0.01),
        "sg_ln_b": nrm(ks[17], (no, SG_WIDTH), 0.01),
        "sg_w": nrm(ks[18], (no, SG_GROUPS, SG_CHUNK, SG_CHUNK), SG_CHUNK ** -0.5),
        "sg_b": 1.0 + nrm(ks[19], (no, SG_GROUPS, SG_CHUNK), 0.01),
        "w_out_o": nrm(ks[20], (no, SG_WIDTH, D_MODEL), 0.5 * SG_WIDTH ** -0.5),
        "final_g": 1.0 + nrm(ks[21], (D_MODEL,), 0.01),
    }

def first_block(x, norm_g, w_in_e, shift_mu, rw_w0, rw_w2, rw_a0, rw_a2, rw_kk, rw_ka, rw_rk,
              rw_lnx_g, rw_lnx_b, att_bias, w_out_e, w_in_o, sg_ln_g, sg_ln_b, sg_w, sg_b,
              w_out_o, final_g):
    h = x
    for layer in range(DEPTH):
        i = layer // 2
        if layer % 2 == 0:
            h = even_layer(h, norm_g[layer], w_in_e[i], shift_mu[i], rw_w0[i], rw_w2[i], rw_a0[i],
                           rw_a2[i], rw_kk[i], rw_ka[i], rw_rk[i], rw_lnx_g[i], rw_lnx_b[i],
                           att_bias[i], w_out_e[i])
        else:
            h = odd_layer(h, norm_g[layer], w_in_o[i], sg_ln_g[i], sg_ln_b[i], sg_w[i], sg_b[i],
                          w_out_o[i])
    return rmsnorm(h, final_g)


_first_inputs = first_inputs


def first_inputs(seed=0):
    import zlib

    import numpy as np

    out = dict(_first_inputs(seed))
    spreads = {}
    factors = {'norm_g': 8.0,
     'rw_w2': 50.824,
     'rw_a0': 5.278,
     'rw_kk': 64.0,
     'rw_ka': 8.0,
     'rw_lnx_g': 64.0,
     'rw_lnx_b': 64.0,
     'att_bias': 64.0,
     'sg_ln_g': 64.0,
     'sg_ln_b': 64.0,
     'sg_b': 64.0,
     'final_g': 30.11,
     'rw_w0': 8.0}
    for name, (base, spread) in spreads.items():
        noise = np.random.default_rng([zlib.crc32(name.encode()), seed]).standard_normal(out[name].shape)
        drawn = base * np.exp(spread * noise) if base else spread * noise
        out[name] = __import__('jax').numpy.asarray(drawn.astype(out[name].dtype))
    for name, factor in factors.items():
        out[name] = (out[name] * factor).astype(out[name].dtype)
    return out


_narrow_inputs = first_inputs


def first_inputs(seed=0):

    out = dict(_narrow_inputs(seed))
    wider = {'rw_kk': 12.0,
     'rw_lnx_g': 12.0,
     'rw_lnx_b': 12.0,
     'att_bias': 12.0,
     'sg_ln_g': 12.0,
     'sg_ln_b': 12.0,
     'sg_b': 12.0,
     'final_g': 6.16}
    for name, times in wider.items():
        mean = out[name].mean()
        out[name] = (mean + times * (out[name] - mean)).astype(out[name].dtype)
    return out


DEPTH_2 = 1

HEAD_DIM = 64
BLOCK = 128
EPS = 1e-6
A_Q_HEADS = 8
A_KV_HEADS = 2
A_GROUP = A_Q_HEADS // A_KV_HEADS
A_WIDTH = A_Q_HEADS * HEAD_DIM
WINDOW = 128
B_WIDTH = D_MODEL // 2
CONV_WIDTH = 31
C_HEADS = 4
C_WIDTH = C_HEADS * 2 * HEAD_DIM
N_BRANCH = 3

A_Q_COLS = A_WIDTH
A_K_COLS = A_KV_HEADS * HEAD_DIM
A_V_COLS = A_KV_HEADS * HEAD_DIM
A_G_COLS = A_WIDTH
B_GLU_COLS = 2 * B_WIDTH
B_G_COLS = B_WIDTH
C_Q_COLS = C_WIDTH
C_K_COLS = C_WIDTH
C_V_COLS = C_WIDTH
C_G_COLS = C_WIDTH
MERGE_COLS = N_BRANCH * D_MODEL
SPLITS = (A_Q_COLS, A_K_COLS, A_V_COLS, A_G_COLS, B_GLU_COLS, B_G_COLS,
          C_Q_COLS, C_K_COLS, C_V_COLS, C_G_COLS, MERGE_COLS)
IN_WIDTH = sum(SPLITS)


def rms_norm(x, g):
    xf = x.astype(jnp.float32)
    y = xf * lax.rsqrt(jnp.mean(xf * xf, axis=-1, keepdims=True) + EPS)
    return (y * g.astype(jnp.float32)).astype(x.dtype)

def sliding_window_attention(q, k, v, sinks):
    B, T, _, d = q.shape
    nb = T // BLOCK
    qb = q.reshape(B, nb, BLOCK, A_KV_HEADS, A_GROUP, d)

    def band(t):
        tb = t.reshape(B, nb, BLOCK, A_KV_HEADS, d)
        prev = jnp.concatenate([jnp.zeros_like(tb[:, :1]), tb[:, :-1]], axis=1)
        return jnp.concatenate([prev, tb], axis=2)

    kw, vw = band(k), band(v)
    s = jnp.einsum('bnqkgd,bnskd->bnkgqs', qb, kw,
                   preferred_element_type=jnp.float32) * (d ** -0.5)
    qi = jnp.arange(BLOCK)[:, None] + BLOCK
    kj = jnp.arange(2 * BLOCK)[None, :]
    rel = qi - kj
    local = (rel >= 0) & (rel < WINDOW)
    kabs = jnp.arange(nb)[:, None, None] * BLOCK - BLOCK + kj[None]
    mask = local[None] & (kabs >= 0)
    s = jnp.where(mask[None, :, None, None], s, -jnp.inf)
    sink = sinks.astype(jnp.float32).reshape(1, 1, A_KV_HEADS, A_GROUP, 1, 1)
    m = jnp.maximum(jnp.max(s, axis=-1, keepdims=True), sink)
    p = jnp.exp(s - m)
    p = p / (jnp.sum(p, axis=-1, keepdims=True) + jnp.exp(sink - m))
    o = jnp.einsum('bnkgqs,bnskd->bnqkgd', p.astype(v.dtype), vw)
    return o.reshape(B, T, A_Q_HEADS * d)

def conformer_conv(glu_in, conv_w, conv_b, ln_g, ln_b):
    a, b = jnp.split(glu_in, 2, axis=-1)
    u = a * jax.nn.sigmoid(b)
    u = lax.conv_general_dilated(
        u, conv_w[:, None, :], window_strides=(1,),
        padding=[(CONV_WIDTH - 1, 0)],
        dimension_numbers=('NWC', 'WIO', 'NWC'),
        feature_group_count=B_WIDTH) + conv_b
    uf = u.astype(jnp.float32)
    mu = jnp.mean(uf, axis=-1, keepdims=True)
    var = jnp.mean(jnp.square(uf - mu), axis=-1, keepdims=True)
    un = (uf - mu) * lax.rsqrt(var + EPS) * ln_g.astype(jnp.float32) + ln_b.astype(jnp.float32)
    return jax.nn.silu(un).astype(u.dtype)

def differential_attention(q, k, v, lam, lam_init, subln_g):
    B, T, H, _, d = q.shape
    nb = T // BLOCK
    qb = jnp.moveaxis(q.reshape(B, nb, BLOCK, H, 2, d), 1, 0)
    kpos = jnp.arange(T)

    def one_block(args):
        q_blk, n = args
        s = jnp.einsum('bqhcd,bshcd->bhcqs', q_blk, k,
                       preferred_element_type=jnp.float32) * (d ** -0.5)
        qpos = n * BLOCK + jnp.arange(BLOCK)
        causal = kpos[None, :] <= qpos[:, None]
        a = jax.nn.softmax(jnp.where(causal, s, -jnp.inf), axis=-1)
        diff = a[:, :, 0] - lam * a[:, :, 1]
        return jnp.einsum('bhqs,bshe->bqhe', diff.astype(v.dtype), v)

    o = lax.map(one_block, (qb, jnp.arange(nb)))
    o = jnp.moveaxis(o, 0, 1).reshape(B, T, H, 2 * d)
    o = rms_norm(o, subln_g) * (1.0 - lam_init)
    return o.reshape(B, T, H * 2 * d)

def second_inputs(seed: int = 0) -> dict:
    key = jax.random.key(seed)
    ks = jax.random.split(key, 24)
    f = jnp.float32
    nrm = lambda k, shape, s: jax.random.normal(k, shape, f) * s
    L, D = DEPTH_2, D_MODEL
    return {
        "x": nrm(ks[0], (BATCH, SEQ, D), 1.0),
        "norm_g": 1.0 + nrm(ks[1], (L, D), 0.02),
        "w_in": nrm(ks[2], (L, D, IN_WIDTH), D ** -0.5),
        "attn_q_norm_g": 1.0 + nrm(ks[3], (L, HEAD_DIM), 0.02),
        "attn_k_norm_g": 1.0 + nrm(ks[4], (L, HEAD_DIM), 0.02),
        "attn_sinks": nrm(ks[5], (L, A_Q_HEADS), 0.5),
        "w_o_attn": nrm(ks[6], (L, A_WIDTH, D), A_WIDTH ** -0.5),
        "conv_w": nrm(ks[7], (L, CONV_WIDTH, B_WIDTH), CONV_WIDTH ** -0.5),
        "conv_b": nrm(ks[8], (L, B_WIDTH), 0.02),
        "conv_norm_g": 1.0 + nrm(ks[9], (L, B_WIDTH), 0.02),
        "conv_norm_b": nrm(ks[10], (L, B_WIDTH), 0.02),
        "w_o_conv": nrm(ks[11], (L, B_WIDTH, D), B_WIDTH ** -0.5),
        "diff_q_norm_g": 1.0 + nrm(ks[12], (L, HEAD_DIM), 0.02),
        "diff_k_norm_g": 1.0 + nrm(ks[13], (L, HEAD_DIM), 0.02),
        "lambda_q": nrm(ks[14], (L, 2, HEAD_DIM), 0.1),
        "lambda_k": nrm(ks[15], (L, 2, HEAD_DIM), 0.1),
        "diff_subln_g": 1.0 + nrm(ks[16], (L, 2 * HEAD_DIM), 0.02),
        "w_o_diff": nrm(ks[17], (L, C_WIDTH, D), C_WIDTH ** -0.5),
        "w_out": nrm(ks[18], (L, D, D), D ** -0.5),
    }

def second_block(x, norm_g, w_in, attn_q_norm_g, attn_k_norm_g, attn_sinks, w_o_attn,
              conv_w, conv_b, conv_norm_g, conv_norm_b, w_o_conv,
              diff_q_norm_g, diff_k_norm_g, lambda_q, lambda_k, diff_subln_g, w_o_diff,
              w_out):
    B, T, D = x.shape
    split_points = [int(s) for s in np.cumsum(SPLITS)[:-1]]
    for l in range(DEPTH_2):
        h = rms_norm(x, norm_g[l])
        z = jnp.einsum('btd,de->bte', h, w_in[l])
        aq, ak, av, ag, bglu, bg, cq, ck, cv, cg, mg = jnp.split(z, split_points, axis=-1)

        aq = rms_norm(aq.reshape(B, T, A_Q_HEADS, HEAD_DIM), attn_q_norm_g[l])
        ak = rms_norm(ak.reshape(B, T, A_KV_HEADS, HEAD_DIM), attn_k_norm_g[l])
        av = av.reshape(B, T, A_KV_HEADS, HEAD_DIM)
        ya = sliding_window_attention(aq, ak, av, attn_sinks[l]) * jax.nn.silu(ag)
        ya = ya @ w_o_attn[l]

        yb = conformer_conv(bglu, conv_w[l], conv_b[l], conv_norm_g[l], conv_norm_b[l])
        yb = (yb * jax.nn.silu(bg)) @ w_o_conv[l]

        lam_init = 0.8 - 0.6 * math.exp(-0.3 * l)
        e = jnp.exp(jnp.sum(lambda_q[l].astype(jnp.float32) * lambda_k[l].astype(jnp.float32), axis=-1))
        lam = e[0] - e[1] + lam_init
        cq = rms_norm(cq.reshape(B, T, C_HEADS, 2, HEAD_DIM), diff_q_norm_g[l])
        ck = rms_norm(ck.reshape(B, T, C_HEADS, 2, HEAD_DIM), diff_k_norm_g[l])
        cv = cv.reshape(B, T, C_HEADS, 2 * HEAD_DIM)
        yc = differential_attention(cq, ck, cv, lam, lam_init, diff_subln_g[l]) * jax.nn.silu(cg)
        yc = yc @ w_o_diff[l]

        gates = jax.nn.sigmoid(mg).reshape(B, T, N_BRANCH, D)
        merged = gates[:, :, 0] * ya + gates[:, :, 1] * yb + gates[:, :, 2] * yc
        x = x + merged @ w_out[l]
    return x


_first_inputs_2 = second_inputs


def second_inputs(seed=0):
    import zlib

    import numpy as np

    out = dict(_first_inputs_2(seed))
    spreads = {}
    factors = {'norm_g': 4.44,
     'attn_q_norm_g': 8.0,
     'attn_k_norm_g': 8.0,
     'attn_sinks': 8.0,
     'conv_b': 8.0,
     'conv_norm_g': 8.0,
     'conv_norm_b': 8.0,
     'diff_q_norm_g': 8.0,
     'diff_k_norm_g': 8.0,
     'diff_subln_g': 8.0}
    for name, (base, spread) in spreads.items():
        noise = np.random.default_rng([zlib.crc32(name.encode()), seed]).standard_normal(out[name].shape)
        drawn = base * np.exp(spread * noise) if base else spread * noise
        out[name] = jnp.asarray(drawn.astype(out[name].dtype))
    for name, factor in factors.items():
        out[name] = (out[name] * factor).astype(out[name].dtype)
    return out


_narrow_inputs_2 = second_inputs


def second_inputs(seed=0):

    out = dict(_narrow_inputs_2(seed))
    wider = {'attn_sinks': 12.0, 'conv_norm_g': 5.47, 'conv_norm_b': 5.13, 'diff_subln_g': 4.62}
    for name, times in wider.items():
        mean = out[name].mean()
        out[name] = (mean + times * (out[name] - mean)).astype(out[name].dtype)
    return out


DEPTH_3 = 1

MIX_WIDTH = D_MODEL
ATTN_WIDTH = MIX_WIDTH // 2
POOL_WIDTH = MIX_WIDTH - ATTN_WIDTH
N_HEADS = ATTN_WIDTH // HEAD_DIM
POOL_WINDOWS = (2, 4, 8, 16)
N_POOL_GROUPS = len(POOL_WINDOWS)
POOL_GROUP = POOL_WIDTH // N_POOL_GROUPS
D_FF = 4 * D_MODEL
PLE_DIM = 256
Q_BLOCK = 128
DN_ALPHA = float((2 * DEPTH_3) ** 0.25)
DN_BETA = float((8 * DEPTH_3) ** -0.25)
PROJ_WIDTH = 3 * ATTN_WIDTH + POOL_WIDTH


def layer_norm(x, g, b):
    xf = x.astype(jnp.float32)
    mu = jnp.mean(xf, axis=-1, keepdims=True)
    var = jnp.mean(jnp.square(xf - mu), axis=-1, keepdims=True)
    y = (xf - mu) * lax.rsqrt(var + LN_EPS)
    return (y * g.astype(jnp.float32) + b.astype(jnp.float32)).astype(x.dtype)

def stick_breaking_attention(q, k, v):
    B, H, S, Dh = q.shape
    n_blk = S // Q_BLOCK
    scale = 1.0 / math.sqrt(Dh)
    q_blocks = q.reshape(B, H, n_blk, Q_BLOCK, Dh).transpose(2, 0, 1, 3, 4)
    starts = jnp.arange(n_blk, dtype=jnp.int32) * Q_BLOCK
    k_pos = jnp.arange(S, dtype=jnp.int32)
    kf = k.astype(jnp.float32)
    vf = v.astype(jnp.float32)

    def one_block(args):
        q_blk, start = args
        z = jnp.einsum("bhqd,bhkd->bhqk", q_blk.astype(jnp.float32), kf) * scale
        q_pos = start + jnp.arange(Q_BLOCK, dtype=jnp.int32)
        mask = k_pos[None, :] < q_pos[:, None]
        log_not = jnp.where(mask, jax.nn.log_sigmoid(-z), 0.0)
        suffix = lax.cumsum(log_not, axis=3, reverse=True) - log_not
        weights = jnp.where(mask, jnp.exp(jax.nn.log_sigmoid(z) + suffix), 0.0)
        return jnp.einsum("bhqk,bhkd->bhqd", weights, vf)

    out = lax.map(one_block, (q_blocks, starts))
    return out.transpose(1, 2, 0, 3, 4).reshape(B, H, S, Dh)

def multiscale_pool(u, w_pool, pool_scale):
    B, S, _ = u.shape
    uf = u.astype(jnp.float32)
    csum = jnp.cumsum(uf, axis=1)
    pos = jnp.arange(S, dtype=jnp.int32)
    diffs = []
    for g, w in enumerate(POOL_WINDOWS):
        sl = slice(g * POOL_GROUP, (g + 1) * POOL_GROUP)
        cg = csum[..., sl]
        lag = jnp.pad(cg, ((0, 0), (w, 0), (0, 0)))[:, :S]
        count = jnp.minimum(pos + 1, w).astype(jnp.float32)[None, :, None]
        diffs.append((cg - lag) / count - uf[..., sl])
    d = jnp.stack(diffs, axis=2)
    y = jnp.einsum("bsgc,gcd->bsgd", d, w_pool.astype(jnp.float32))
    return y.reshape(B, S, POOL_WIDTH) * pool_scale.astype(jnp.float32)

def third_inputs(seed: int = 0) -> dict:
    key = jax.random.key(seed)
    ks = jax.random.split(key, 24)
    nrm = lambda k, shape, s: jax.random.normal(k, shape, jnp.float32) * s
    L = DEPTH_3
    x = jax.random.normal(ks[0], (BATCH, SEQ, D_MODEL), jnp.float32)
    p = jax.random.normal(ks[1], (L, BATCH, SEQ, PLE_DIM), jnp.float32)
    emb_ln_g = 1.0 + nrm(ks[2], (D_MODEL,), 0.02)
    emb_ln_b = nrm(ks[3], (D_MODEL,), 0.02)
    col_scale = jnp.concatenate([
        jnp.ones((2 * ATTN_WIDTH,), jnp.float32),
        jnp.full((ATTN_WIDTH + POOL_WIDTH,), DN_BETA, jnp.float32)])
    w_in = nrm(ks[4], (L, D_MODEL, PROJ_WIDTH), D_MODEL ** -0.5) * col_scale
    attn_out_g = 1.0 + nrm(ks[5], (L, ATTN_WIDTH), 0.02)
    w_pool = nrm(ks[6], (L, N_POOL_GROUPS, POOL_GROUP, POOL_GROUP), POOL_GROUP ** -0.5 * DN_BETA)
    pool_scale = 1.0 + nrm(ks[7], (L, POOL_WIDTH), 0.02)
    w_out = nrm(ks[8], (L, MIX_WIDTH, D_MODEL), MIX_WIDTH ** -0.5 * DN_BETA)
    ln1_g = 1.0 + nrm(ks[9], (L, D_MODEL), 0.02)
    ln1_b = nrm(ks[10], (L, D_MODEL), 0.02)
    w_up = nrm(ks[11], (L, D_MODEL, D_FF), D_MODEL ** -0.5 * DN_BETA)
    w_down = nrm(ks[12], (L, D_FF, D_MODEL), D_FF ** -0.5 * DN_BETA)
    ln2_g = 1.0 + nrm(ks[13], (L, D_MODEL), 0.02)
    ln2_b = nrm(ks[14], (L, D_MODEL), 0.02)
    w_ple = nrm(ks[15], (L, PLE_DIM, D_MODEL), PLE_DIM ** -0.5 * DN_BETA)
    w_ple_gate = nrm(ks[16], (L, D_MODEL, D_MODEL), D_MODEL ** -0.5)
    ln3_g = 1.0 + nrm(ks[17], (L, D_MODEL), 0.02)
    ln3_b = nrm(ks[18], (L, D_MODEL), 0.02)
    return {"x": x, "p": p, "emb_ln_g": emb_ln_g, "emb_ln_b": emb_ln_b,
            "w_in": w_in, "attn_out_g": attn_out_g, "w_pool": w_pool, "pool_scale": pool_scale,
            "w_out": w_out, "ln1_g": ln1_g, "ln1_b": ln1_b, "w_up": w_up, "w_down": w_down,
            "ln2_g": ln2_g, "ln2_b": ln2_b, "w_ple": w_ple, "w_ple_gate": w_ple_gate,
            "ln3_g": ln3_g, "ln3_b": ln3_b}

def third_block(x, p, emb_ln_g, emb_ln_b, w_in, attn_out_g, w_pool, pool_scale, w_out,
              ln1_g, ln1_b, w_up, w_down, ln2_g, ln2_b, w_ple, w_ple_gate, ln3_g, ln3_b):
    B, S, D = x.shape
    dt = x.dtype
    x = layer_norm(x, emb_ln_g, emb_ln_b)
    for i in range(DEPTH_3):
        proj = x @ w_in[i]
        q, k, v, u = jnp.split(proj, [ATTN_WIDTH, 2 * ATTN_WIDTH, 3 * ATTN_WIDTH], axis=-1)
        to_heads = lambda t: t.reshape(B, S, N_HEADS, HEAD_DIM).transpose(0, 2, 1, 3)
        o = stick_breaking_attention(to_heads(q), to_heads(k), to_heads(v))
        o = o * lax.rsqrt(jnp.mean(o * o, axis=-1, keepdims=True) + RMS_EPS)
        o = o.transpose(0, 2, 1, 3).reshape(B, S, ATTN_WIDTH) * attn_out_g[i].astype(jnp.float32)
        pooled = multiscale_pool(u, w_pool[i], pool_scale[i])
        mixed = jnp.concatenate([o, pooled], axis=-1).astype(dt) @ w_out[i]
        x = layer_norm(DN_ALPHA * x + mixed, ln1_g[i], ln1_b[i])
        h = jnp.square(jax.nn.relu(x @ w_up[i])) @ w_down[i]
        x = layer_norm(DN_ALPHA * x + h, ln2_g[i], ln2_b[i])
        ple = (p[i] @ w_ple[i]) * jax.nn.sigmoid(x @ w_ple_gate[i])
        x = layer_norm(DN_ALPHA * x + ple, ln3_g[i], ln3_b[i])
    return x


_first_inputs_3 = third_inputs


def third_inputs(seed=0):
    import zlib

    import numpy as np

    out = dict(_first_inputs_3(seed))
    spreads = {}
    factors = {'emb_ln_g': 2.774,
     'emb_ln_b': 2.792,
     'attn_out_g': 34.875,
     'pool_scale': 42.191,
     'ln1_g': 7.969,
     'ln1_b': 8.075,
     'ln2_g': 7.829,
     'ln2_b': 8.179,
     'ln3_g': 8.266,
     'ln3_b': 8.353}
    for name, (base, spread) in spreads.items():
        noise = np.random.default_rng([zlib.crc32(name.encode()), seed]).standard_normal(out[name].shape)
        drawn = base * np.exp(spread * noise) if base else spread * noise
        out[name] = __import__('jax').numpy.asarray(drawn.astype(out[name].dtype))
    for name, factor in factors.items():
        out[name] = (out[name] * factor).astype(out[name].dtype)
    return out


_narrow_inputs_3 = third_inputs


def third_inputs(seed=0):

    out = dict(_narrow_inputs_3(seed))
    wider = {'attn_out_g': 4.06,
     'pool_scale': 4.07,
     'ln2_g': 3.09,
     'ln2_b': 3.1,
     'ln3_g': 3.24,
     'ln3_b': 3.23}
    for name, times in wider.items():
        mean = out[name].mean()
        out[name] = (mean + times * (out[name] - mean)).astype(out[name].dtype)
    return out


def setup_inputs(seed=0):
    out = dict(first_inputs(seed))
    for name, value in second_inputs(seed + 1).items():
        if name != "x":
            out[name + "_2"] = value
    for name, value in third_inputs(seed + 2).items():
        if name != "x":
            out[name + "_3"] = value
    return out


def reference(
    x, norm_g, w_in_e, shift_mu, rw_w0, rw_w2, rw_a0, rw_a2, rw_kk, rw_ka, rw_rk, rw_lnx_g,
    rw_lnx_b, att_bias, w_out_e, w_in_o, sg_ln_g, sg_ln_b, sg_w, sg_b, w_out_o, final_g,
    norm_g_2, w_in_2, attn_q_norm_g_2, attn_k_norm_g_2, attn_sinks_2, w_o_attn_2, conv_w_2,
    conv_b_2, conv_norm_g_2, conv_norm_b_2, w_o_conv_2, diff_q_norm_g_2, diff_k_norm_g_2,
    lambda_q_2, lambda_k_2, diff_subln_g_2, w_o_diff_2, w_out_2, p_3, emb_ln_g_3, emb_ln_b_3,
    w_in_3, attn_out_g_3, w_pool_3, pool_scale_3, w_out_3, ln1_g_3, ln1_b_3, w_up_3, w_down_3,
    ln2_g_3, ln2_b_3, w_ple_3, w_ple_gate_3, ln3_g_3, ln3_b_3,
):
    x = first_block(
        x, norm_g, w_in_e, shift_mu, rw_w0, rw_w2, rw_a0, rw_a2, rw_kk, rw_ka, rw_rk, rw_lnx_g,
        rw_lnx_b, att_bias, w_out_e, w_in_o, sg_ln_g, sg_ln_b, sg_w, sg_b, w_out_o, final_g,
    )
    x = second_block(
        x, norm_g_2, w_in_2, attn_q_norm_g_2, attn_k_norm_g_2, attn_sinks_2, w_o_attn_2,
        conv_w_2, conv_b_2, conv_norm_g_2, conv_norm_b_2, w_o_conv_2, diff_q_norm_g_2,
        diff_k_norm_g_2, lambda_q_2, lambda_k_2, diff_subln_g_2, w_o_diff_2, w_out_2,
    )
    return third_block(
        x, p_3, emb_ln_g_3, emb_ln_b_3, w_in_3, attn_out_g_3, w_pool_3, pool_scale_3, w_out_3,
        ln1_g_3, ln1_b_3, w_up_3, w_down_3, ln2_g_3, ln2_b_3, w_ple_3, w_ple_gate_3, ln3_g_3,
        ln3_b_3,
    )


_drawn_inputs = setup_inputs


def setup_inputs(seed=0):
    import zlib

    import numpy as np

    out = dict(_drawn_inputs(seed))
    spreads = {}
    factors = {'attn_sinks_2': 4.6, 'lambda_k_2': 8.0}
    for name, (base, spread) in spreads.items():
        noise = np.random.default_rng([zlib.crc32(name.encode()), seed]).standard_normal(out[name].shape)
        drawn = base * np.exp(spread * noise) if base else spread * noise
        out[name] = jnp.asarray(drawn.astype(out[name].dtype))
    for name, factor in factors.items():
        out[name] = (out[name] * factor).astype(out[name].dtype)
    return out
```

```python
import math
from contextlib import ExitStack

import concourse.bass as bass
import numpy as np
from concourse import mybir

F32 = mybir.dt.float32
ACT = mybir.ActivationFunctionType
ALU = mybir.AluOpType
AX = mybir.AxisListType

P = 128
SEQ = 1024
D = 1024
NT = SEQ // P
KD = D // P
HALF = 512
NEG = -1e30


class Step:

    def __init__(self, lane, index):
        self.lane, self.index, self.value = lane, index, None


class Lane:

    def __init__(self, sem, in_order):
        self.sem, self.in_order, self.items, self.waited_for = sem, in_order, [], set()

    def put(self, call, args, kw, after):
        step = Step(self, len(self.items))
        if not self.in_order and self.items:
            after = list(after) + [self.items[-1][4]]
        for s in after:
            if s is not None:
                s.lane.waited_for.add(s.index)
        self.items.append((call, args, kw, [s for s in after if s is not None], step))
        return step


class DmaLane:

    def __init__(self, sem):
        self.sem, self.count, self.waited_for = sem, 0, set()


class Ring:

    def __init__(self, buffers):
        self.free = [(b, []) for b in buffers]

    def take(self):
        return self.free.pop(0)

    def give(self, buffer, last_users):
        self.free.append((buffer, list(last_users)))


def emit(lane, engine):
    reached, count = {}, 0
    for call, args, kw, after, step in lane.items:
        need = {}
        for s in after:
            level = s.value
            if level > need.get(s.lane.sem, 0):
                need[s.lane.sem] = level
        for sem, level in need.items():
            if level > reached.get(sem, 0):
                engine.wait_ge(sem, level)
                reached[sem] = level
        if call is None:
            continue
        made = call(*args, **kw)
        if step.lane is not lane:
            made.then_inc(step.lane.sem, 16)
        elif step.index in lane.waited_for:
            made.then_inc(lane.sem, 1)


def count_values(lane):
    count = 0
    for call, _, _, _, step in lane.items:
        if call is not None and step.lane is lane:
            if step.index in lane.waited_for:
                count += 1
                step.value = count


_COLUMNS = [("norm_g", 0, 8), ("shift_mu", 0, 13), ("rw_w0", 0, 4), ("rw_a0", 0, 4), ("rw_kk", 0, 4), ("rw_ka", 0, 4),
            ("rw_rk", 0, 4), ("norm_g", 1, 8), ("norm_g_2", 0, 8), ("attn_q_norm_g_2", 0, 1),
            ("attn_k_norm_g_2", 0, 1), ("diff_q_norm_g_2", 0, 1), ("diff_k_norm_g_2", 0, 1), ("conv_b_2", 0, 4),
            ("conv_norm_g_2", 0, 4), ("conv_norm_b_2", 0, 4), ("diff_subln_g_2", 0, 1), ("attn_out_g_3", 0, 4),
            ("pool_scale_3", 0, 4), ("conv_w_2", 0, 124)]


def column_plan():
    plan, at = {}, 0
    for name, layer, n in _COLUMNS:
        plan[name + ("'" if layer else "")] = (at, n)
        at += n
    return plan


def channel_columns(inputs):
    out = []
    for name, layer, n in _COLUMNS:
        a = np.asarray(inputs[name])[layer]
        if name == "conv_w_2":
            out.append(a.reshape(31, 4, P).transpose(2, 1, 0).reshape(P, 124))
            continue
        a = a.reshape(-1)
        if a.size == 64:
            a = np.tile(a, 2)
        out.append(a.reshape(n, P).T)
    return np.ascontiguousarray(np.concatenate(out, axis=1))


BLOCKS = (1, 2, 3)


def build(nc, T, out):
    ctx = ExitStack()
    with ctx:
        def sb(name, shape):
            return ctx.enter_context(nc.sbuf_tensor(name, shape, F32))

        def sem(name):
            return ctx.enter_context(nc.semaphore(name))

        H = sb("H", [P, NT, D])
        XT = sb("XT", [P, KD, SEQ])
        MIX = sb("MIX", [P, KD, SEQ])
        WS = [sb(f"WS{i}", [P, 4096]) for i in range(2)]
        ident = sb("ident", [P, P])
        head_ones = sb("head_ones", [P, P])
        PAR = sb("PAR", [P, 512])
        STAT = sb("STAT", [P, 256])
        GTMP = sb("GTMP", [P, 1024])
        WORK_N = 18304
        WORK = sb("WORK", [P, WORK_N])
        banks = [ctx.enter_context(nc.psum_tensor(f"bank{i}", [P, HALF], F32)) for i in range(8)]

        lane_pe = Lane(sem("s_pe"), True)
        lane_dve = Lane(sem("s_dve"), False)
        lane_act = Lane(sem("s_act"), False)
        lane_pool = Lane(sem("s_pool"), False)
        lane_sp = Lane(sem("s_sp"), True)
        lanes = [lane_pe, lane_dve, lane_act, lane_pool]
        w_lane = {id(WS[i]): DmaLane(sem(f"s_w{i}")) for i in range(2)}
        dma_par = DmaLane(sem("s_par"))
        dma_x = DmaLane(sem("s_x"))
        dma_misc = DmaLane(sem("s_misc"))
        dma_out = DmaLane(sem("s_out"))

        psum = Ring(banks)
        wring = Ring(WS)

        def pe(call, *a, after=(), **kw):
            return lane_pe.put(call, a, kw, after)

        def dve(call, *a, after=(), **kw):
            return lane_dve.put(call, a, kw, after)

        def act(call, *a, after=(), **kw):
            return lane_act.put(call, a, kw, after)

        def pool(call, *a, after=(), **kw):
            return lane_pool.put(call, a, kw, after)

        def dma(dst, src, lane, after=()):
            step = Step(lane, 0)
            lane.count += 16
            step.value = lane.count
            for s in after:
                if s is not None:
                    s.lane.waited_for.add(s.index)
            lane_sp.items.append((nc.sync.dma_start, (dst, src), {}, [s for s in after if s is not None], step))
            return step

        V, S, G, E = nc.vector, nc.scalar, nc.gpsimd, nc.tensor

        def last(lane):
            return lane.items[-1][4] if lane.items else None

        def boundary():
            ends = []
            for ln in lanes:
                for item in reversed(ln.items):
                    if item[0] is not None:
                        ends.append(item[4])
                        break
            for ln in lanes + [lane_sp]:
                for s in ends:
                    s.lane.waited_for.add(s.index)
                ln.items.append((None, (), {}, list(ends), Step(ln, -1)))
            for ln in lanes:
                if not ln.in_order:
                    ln.items[-1] = (None, (), {}, list(ends), [s for s in ends if s.lane is ln][0])
            return ends

        par_at = {}
        par_used = [0]

        def par(name, ap2, cols):
            at = par_used[0]
            par_used[0] += cols
            assert par_used[0] <= 512
            dma(PAR[:, at:at + cols], ap2, dma_par)
            par_at[name] = at

        def col(name, c):
            return PAR[:, par_at[name] + c:par_at[name] + c + 1]

        def cols(name, c0, n, m):
            a = PAR[:, par_at[name] + c0:par_at[name] + c0 + n]
            return a.unsqueeze(2).to_broadcast([P, n, m])

        def area(spec):
            at, r = 0, {}
            for name, n in spec:
                r[name] = WORK[:, at:at + n]
                at += n
            assert at <= WORK_N, at
            return r

        x_in = [dma(H[:, t, :], T["x"][0, t * P:(t + 1) * P, :], dma_x) for t in range(NT)][-1]
        par("columns", T["channel_columns"], T["channel_columns"].shape[1])
        for n, (first, _) in column_plan().items():
            par_at[n] = par_at["columns"] + first
        par("sinks", T["attn_sinks_2"][0].partition_broadcast(P), 8)
        par("lq", T["lambda_q_2"][0].rearrange("a n -> (a n)").partition_broadcast(P), P)
        par("lk", T["lambda_k_2"][0].rearrange("a n -> (a n)").partition_broadcast(P), P)
        bias_far_at = par_used[0]
        par("bias_far", T["att_bias_far"].partition_broadcast(P), 8)
        par_ready = Step(dma_par, 0)
        par_ready.value = dma_par.count

        pool(G.memset, ident[:, :], 0.0)
        pool(G.affine_select, out=ident[:, :], in_=ident[:, :], compare_op=ALU.not_equal, fill=1.0,
             base=0, pattern=[[-1, P]], channel_multiplier=1)
        pool(G.memset, head_ones[:, :], 0.0)
        pool(G.memset, head_ones[0:64, 0:64], 1.0)
        consts_ready = pool(G.memset, head_ones[64:128, 64:128], 1.0)

        def eye(n=P):
            return ident[0:n, 0:n]

        def load_w(pieces, kt):
            slot, free = wring.take()
            width = sum(w for _, _, w in pieces)
            view = slot[:, 0:kt * width].rearrange("p (k n) -> p k n", k=kt)
            at = 0
            for src, c0, w in pieces:
                step = dma(view[:, :, at:at + w], src.rearrange("(k p) n -> p k n", p=P)[:, :, c0:c0 + w],
                           w_lane[id(slot)], after=free)
                at += w
            return slot, view, step

        def done_w(slot):
            wring.give(slot, [last(lane_pe)])

        def product_T(wv, wstep, src, kt, c0, evac, after=()):
            for half in range(2):
                bank, free = psum.take()
                for k in range(kt):
                    mm = pe(E.matmul, bank[:, :], wv[:, k, c0:c0 + P], src[:, k, half * HALF:(half + 1) * HALF],
                            start=k == 0, stop=k == kt - 1,
                            after=(list(free) + [wstep] + list(after)) if k == 0 else ())
                psum.give(bank, [evac(bank, half, mm)])

        def product_N(wv, wstep, src, kt, t, evac, after=(), n=HALF, c0=0):
            bank, free = psum.take()
            for k in range(kt):
                mm = pe(E.matmul, bank[:, 0:n], src[:, k, t * P:(t + 1) * P], wv[:, k, c0:c0 + n],
                        start=k == 0, stop=k == kt - 1,
                        after=(list(free) + [wstep] + list(after)) if k == 0 else ())
            psum.give(bank, [evac(bank, mm)])

        def transposes(srcs, after=()):
            bank, free = psum.take()
            for i, s in enumerate(srcs):
                st = pe(E.transpose, bank[:, i * P:(i + 1) * P], s, ident[:, :],
                        after=(list(free) + list(after) + [consts_ready]) if i == 0 else ())
            return bank, st

        turn = [0]

        def copy_out(dst, src, after):
            turn[0] += 1
            if turn[0] % 2:
                return act(S.activation, dst, src, ACT.Copy, after=after)
            return dve(V.tensor_copy, dst, src, after=after)

        def add_to_H(bank, t, c0, mm):
            return dve(V.tensor_tensor, H[:, t, c0:c0 + HALF], H[:, t, c0:c0 + HALF], bank[:, :], ALU.add,
                       after=[mm])

        def project_out(w, src, kt, after):
            for c0 in range(0, D, HALF):
                slot, wv, ws = load_w([(w, c0, HALF)], kt)
                for t in range(NT):
                    product_N(wv, ws, src, kt, t, lambda b, mm, t=t: add_to_H(b, t, c0, mm), after=after)
                done_w(slot)

        def rstd_of(dst, src, scale, eps):
            a = dve(V.tensor_scalar, dst, src, scale, eps, ALU.mult, ALU.add)
            b = act(S.activation, dst, dst, ACT.Sqrt, after=[a])
            return dve(V.reciprocal, dst, dst, after=[b])

        SS = STAT[:, 0:8]
        MV = STAT[:, 8:24].rearrange("p (t a) -> p t a", a=2)
        BST = STAT[:, 24:36]
        RS = STAT[:, 36:44]

        def rms_stats(junk, eps, after=()):
            for t in range(NT):
                a = act(S.activation, junk, H[:, t, :], ACT.Square, accum_out=SS[:, t:t + 1],
                        after=after if t == 0 else ())
            dve(V.tensor_copy, RS, SS, after=[a])
            return rstd_of(RS, RS, 1.0 / D, eps)

        def rms_to_XT(gname, w, after=()):
            r = rms_stats(w["junk"], 1e-6, after=after)
            tmp = Ring([w["xn0"], w["xn1"]])
            for t in range(NT):
                xn, free = tmp.take()
                a = act(S.activation, xn, H[:, t, :], ACT.Copy, scale=RS[:, t:t + 1], after=[r] + free)
                for half in range(2):
                    bank, tr = transposes([xn[:, (half * 4 + i) * P:(half * 4 + i + 1) * P] for i in range(4)],
                                          after=[a])
                    e = dve(V.tensor_tensor, XT[:, half * 4:half * 4 + 4, t * P:(t + 1) * P],
                            bank[:, :].rearrange("p (c n) -> p c n", c=4), cols(gname, half * 4, 4, P), ALU.mult,
                            after=[tr, par_ready])
                    psum.give(bank, [e])
                tmp.give(xn, [tr])
            return e

        def vector_of(name):
            return T[name] if len(T[name].shape) == 1 else T[name][0]

        def ln_H(gname, bname, w, after=()):
            g = dma(w["grow"], vector_of(gname).partition_broadcast(P), dma_misc, after=after)
            g = dma(w["brow"], vector_of(bname).partition_broadcast(P), dma_misc, after=after)
            for t in range(NT):
                dve(V.bn_stats, BST[:, 0:6], H[:, t, 0:HALF], after=after if t == 0 else ())
                dve(V.bn_stats, BST[:, 6:12], H[:, t, HALF:D])
                dve(V.bn_aggr, MV[:, t, :], BST)
            r = rstd_of(RS, MV[:, :, 1], 1.0, 1e-5)
            for t in range(NT):
                a = dve(V.tensor_scalar, H[:, t, :], H[:, t, :], MV[:, t, 0:1], RS[:, t:t + 1],
                        ALU.subtract, ALU.mult, after=[r])
                b = pool(G.tensor_tensor, H[:, t, :], H[:, t, :], w["grow"], ALU.mult, after=[a, g])
                b = dve(V.tensor_tensor, H[:, t, :], H[:, t, :], w["brow"], ALU.add, after=[b, g])
                yield t, b

        def H_to_XT(t, ready):
            for half in range(2):
                bank, tr = transposes([H[:, t, (half * 4 + i) * P:(half * 4 + i + 1) * P] for i in range(4)],
                                      after=[ready])
                e = copy_out(XT[:, half * 4:half * 4 + 4, t * P:(t + 1) * P],
                             bank[:, :].rearrange("p (c n) -> p c n", c=4), [tr])
                psum.give(bank, [e])
            return e

        def tile_pairs(buf):
            return buf.rearrange("p (t n) -> p t n", n=P)

        norm_area = [("junk", 1024), ("xn0", 1024), ("xn1", 1024)]

        def both():
            return [last(lane_dve), last(lane_act)]

        gate_tmp = Ring([GTMP[:, 0:HALF], GTMP[:, HALF:2 * HALF]])

        def gate_T(wdram, c_base, ys, func, after=()):
            slot, wv, ws = load_w([(wdram, c_base, HALF)], KD)
            for ct in range(4):
                def evac(bank, half, mm, ct=ct):
                    g, free = gate_tmp.take()
                    a = act(S.activation, g, bank[:, :], func, after=[mm] + free)
                    y = ys(ct)[:, half * HALF:(half + 1) * HALF]
                    m = pool(G.tensor_tensor, y, y, g, ALU.mult, after=[a] + list(after))
                    gate_tmp.give(g, [m])
                    return a
                product_T(wv, ws, XT, KD, ct * P, evac)
            done_w(slot)

        def rwkv():
            KAPPA = math.exp(-0.5)
            B4 = 1024
            spec = [("LT", B4), ("RAW", 1025), ("R", B4), ("K", B4), ("A", B4), ("SIG", B4), ("CS", B4), ("EX", B4),
                    ("KK", B4), ("T1", B4), ("BT", B4), ("KTL", B4), ("VN", B4), ("BN", B4), ("KN", B4), ("AN", B4),
                    ("LVL", 7 * P), ("MASK2", 2 * P), ("W2", 512),
                    ("ST", P), ("WC", 16), ("BON", 16)]
            w = area(spec)
            RA = MIX[:, 4:6, :].rearrange("p a (t b n) -> p (a t) b n", b=2, n=P)
            YN = tile_pairs(MIX[:, 6, :])
            row_mask = MIX[:, 7, :]
            LT, RAW = w["LT"], w["RAW"]
            pool(G.memset, row_mask, 1.0)
            pool(G.memset, row_mask.rearrange("p (c n) -> p c n", n=64)[:, :, 0:1], 0.0)
            pool(G.memset, RAW[:, 0:1], 0.0)
            lvl = w["LVL"].rearrange("p (m n) -> p m n", n=P)
            for i in range(6):
                m = 1 << i
                ng = P // (2 * m)
                pool(G.memset, lvl[:, i, :], 0.0)
                even = lvl[:, i, :].rearrange("p (g a b) -> p g a b", a=2, b=m)[:, :, 0, :]
                pool(G.memset, even, 1.0)
                pool(G.affine_select, out=even, in_=even, compare_op=ALU.is_ge, fill=0.0, base=-m,
                     pattern=[[-2 * m, ng], [0, m]], channel_multiplier=1)
                pool(G.affine_select, out=even, in_=even, compare_op=ALU.is_ge, fill=0.0, base=2 * m - 1,
                     pattern=[[2 * m, ng], [0, m]], channel_multiplier=-1)
            pool(G.memset, lvl[:, 6, :], 0.0)
            odd = lvl[:, 6, :].rearrange("p (g a) -> p g a", a=2)[:, :, 1]
            pool(G.affine_select, out=odd, in_=odd, compare_op=ALU.not_equal, fill=1.0, base=0,
                 pattern=[[-2, P // 2]], channel_multiplier=1)
            mask2 = w["MASK2"].rearrange("p (m n) -> p m n", n=P)
            pool(G.memset, w["MASK2"], 1.0)
            for i in range(2):
                pool(G.affine_select, out=mask2[:, i, :], in_=mask2[:, i, :], compare_op=ALU.is_ge, fill=0.0,
                     base=i - 1, pattern=[[1, P]], channel_multiplier=-1)
            masks_ready = pool(G.memset, mask2[0:64, :, 64:128], 0.0)
            WIN = T["w_in_e"][0]
            w2s = dma(w["W2"][0:64, :], T["rw_w2"][0], dma_misc)
            w2s = dma(w["W2"][64:128, :], T["rw_a2"][0], dma_misc)
            W2 = w["W2"]

            def shift_evac(dst, mu_col, tmp):
                def evac(bank, half, mm):
                    return act(S.activation, RAW[:, 1 + half * HALF:1 + (half + 1) * HALF], bank[:, :], ACT.Copy,
                               after=[mm, last(lane_dve), last(lane_pool)])
                def finish():
                    a = pool(G.tensor_tensor, tmp, RAW[:, 0:SEQ], RAW[:, 1:SEQ + 1], ALU.subtract,
                             after=[last(lane_act), masks_ready, last(lane_dve)])
                    return dve(V.scalar_tensor_tensor, dst, tmp, mu_col, RAW[:, 1:SEQ + 1], ALU.mult, ALU.add,
                               after=[a])
                return evac, finish

            slot, wv, ws = load_w([(WIN, 1536, P)], KD)
            evac, finish = shift_evac(LT, col("shift_mu", 12), w["EX"])
            product_T(wv, ws, XT, KD, 0, evac)
            done_w(slot)
            f = finish()
            lt_ready = act(S.activation, LT[0:64, :], LT[0:64, :], ACT.Tanh, after=[f])
            R, K, A, SIG, CS, EX, KK, T1 = (w[n] for n in ("R", "K", "A", "SIG", "CS", "EX", "KK", "T1"))
            BT, KTL, VN, BN, KN, AN = (w[n] for n in ("BT", "KTL", "VN", "BN", "KN", "AN"))
            ST, WC, BON = w["ST"], w["WC"], w["BON"]
            for c in range(4):
                yield
                slot, wv, ws = load_w([(WIN, g * 512 + c * P, P) for g in range(3)], KD)
                done = []
                for g, dst in ((0, R), (1, K), (2, T1)):
                    evac, finish = shift_evac(dst, col("shift_mu", g * 4 + c), EX)
                    product_T(wv, ws, XT, KD, g * P, evac, after=[last(lane_dve)])
                    done.append(finish())
                done_w(slot)
                for hf in range(2):
                    bank, tr = transposes([T1[:, (hf * 4 + i) * P:(hf * 4 + i + 1) * P] for i in range(4)], after=done)
                    psum.give(bank, [copy_out(VN[:, hf * HALF:(hf + 1) * HALF], bank[:, :], [tr])])
                for hf in range(2):
                    sl = slice(hf * HALF, (hf + 1) * HALF)
                    bank, free = psum.take()
                    mm = pe(E.matmul, bank[:, :], W2[0:64, c * P:(c + 1) * P], LT[0:64, sl], start=True, stop=True,
                            after=free + [lt_ready, w2s])
                    psum.give(bank, [act(S.activation, SIG[:, sl], bank[:, :], ACT.Sigmoid,
                                         bias=col("rw_w0", c), after=[mm, par_ready])])
                    bank, free = psum.take()
                    mm = pe(E.matmul, bank[:, :], W2[64:128, c * P:(c + 1) * P], LT[64:128, sl], start=True, stop=True,
                            after=free)
                    psum.give(bank, [act(S.activation, A[:, sl], bank[:, :], ACT.Sigmoid,
                                         bias=col("rw_a0", c), after=[mm])])
                a_ready = last(lane_act)
                cs = dve(V.tensor_tensor_scan, CS, row_mask, SIG, 0.0, ALU.mult, ALU.add, after=[a_ready, masks_ready])
                x = dve(V.tensor_scalar, KK, K, col("rw_kk", c), None, ALU.mult)
                x = act(S.activation, T1, KK, ACT.Square, after=[x, last(lane_pe)])
                for hf in range(2):
                    sl = slice(hf * HALF, (hf + 1) * HALF)
                    bank, free = psum.take()
                    mm = pe(E.matmul, bank[:, :], head_ones[:, :], T1[:, sl], start=True, stop=True, after=free + [x])
                    psum.give(bank, [act(S.activation, EX[:, sl], bank[:, :], ACT.Sqrt,
                                         after=[mm, last(lane_dve)])])
                x = dve(V.tensor_scalar, EX, EX, 1e-12, None, ALU.max, after=[last(lane_act)])
                x = dve(V.reciprocal, EX, EX)
                x = dve(V.tensor_tensor, KK, KK, EX, ALU.mult)
                dve(V.tensor_scalar, T1, A, 1.0, col("rw_ka", c), ALU.subtract, ALU.mult)
                x = dve(V.scalar_tensor_tensor, K, T1, 1.0, K, ALU.add, ALU.mult)
                y = dve(V.scalar_tensor_tensor, T1, R, col("rw_rk", c), K, ALU.mult, ALU.mult)
                bank, free = psum.take()
                for t in range(NT):
                    mm = pe(E.matmul, bank[:, 2 * t:2 * t + 2], T1[:, t * P:(t + 1) * P],
                            head_ones[:, 0:P:64], start=True, stop=True, after=(free + [y]) if t == 0 else ())
                psum.give(bank, [dve(V.tensor_copy, BON, bank[:, 0:16], after=[mm])])
                b = dve(V.tensor_tensor, T1, KK, A, ALU.mult)
                ex = act(S.activation, EX, CS, ACT.Exp, scale=-KAPPA, after=[b])
                dve(V.tensor_tensor, RA[:, :, 1, :], tile_pairs(R), tile_pairs(EX), ALU.mult, after=[ex])
                wc = dve(V.tensor_copy, WC, EX.rearrange("p (c n) -> p c n", n=64)[:, :, 63])
                dve(V.tensor_tensor, SIG, CS, SIG, ALU.subtract)
                ex = act(S.activation, EX, SIG, ACT.Exp, scale=-KAPPA, after=[last(lane_dve)])
                dve(V.scalar_tensor_tensor, RA[:, :, 0, :], tile_pairs(KK), -1.0, tile_pairs(EX), ALU.mult, ALU.mult,
                    after=[ex])
                ex = act(S.activation, EX, CS, ACT.Exp, scale=KAPPA, after=[last(lane_dve)])
                dve(V.tensor_tensor, BT, T1, EX, ALU.mult, after=[ex])
                dve(V.tensor_tensor, KTL, K, EX, ALU.mult)
                wcb = WC.unsqueeze(2).to_broadcast([P, 16, 64])
                dve(V.tensor_tensor, SIG.rearrange("p (c n) -> p c n", n=64), BT.rearrange("p (c n) -> p c n", n=64),
                    wcb, ALU.mult)
                ops = dve(V.tensor_tensor, A.rearrange("p (c n) -> p c n", n=64),
                          KTL.rearrange("p (c n) -> p c n", n=64), wcb, ALU.mult)
                for src, dst in ((tile_pairs(SIG), BN), (tile_pairs(A), KN), (RA[:, :, 0, :], AN)):
                    for hf in range(2):
                        bank, tr = transposes([src[:, hf * 4 + i, :] for i in range(4)], after=[ops])
                        psum.give(bank, [copy_out(dst[:, hf * HALF:(hf + 1) * HALF], bank[:, :], [tr])])
                x = dve(V.memset, ST, 0.0)
                mat = lambda b, i: b[:, i * HALF:(i + 1) * HALF]
                Am, AL, Fm, Gm, Ym = mat(R, 0), mat(R, 1), mat(K, 0), mat(K, 1), mat(A, 0)
                X0, U0, UU, WT = mat(A, 1)[:, 0:256], mat(A, 1)[:, 256:512], mat(SIG, 0)[:, 0:256], mat(SIG, 0)[:, 256:512]
                AKT = CS.rearrange("p (b m n) -> p b m n", b=4, m=2)
                ABT = EX.rearrange("p (b m n) -> p b m n", b=4, m=2)
                blk = lambda b: b.rearrange("p (b n) -> p b n", b=4)
                for grp in range(4):
                    yield
                    tiles = [(2 * grp + i, h) for h in range(2) for i in range(2)]
                    at = lambda t, h: (t - 2 * grp) * P + h * 64
                    before = both()
                    for hf in range(2):
                        bank, free = psum.take()
                        for q, (t, h) in enumerate(tiles[2 * hf:2 * hf + 2]):
                            pr = slice(h * 64, h * 64 + 64)
                            mm = pe(E.matmul, bank[:, q * P:(q + 1) * P], RA[pr, t, 0, :], BT[pr, t * P:(t + 1) * P],
                                    start=True, stop=True, after=(free + before) if q == 0 else ())
                        am = act(S.activation, Am[:, hf * 256:hf * 256 + 256], bank[:, 0:256], ACT.Copy, after=[mm] + before)
                        psum.give(bank, [am])
                    for dst, lhs in ((AKT, KTL), (ABT, BT)):
                        for hf in range(2):
                            bank, free = psum.take()
                            for q, (t, h) in enumerate(tiles[2 * hf:2 * hf + 2]):
                                pr = slice(h * 64, h * 64 + 64)
                                mm = pe(E.matmul, bank[:, q * 256:(q + 1) * 256], lhs[pr, t * P:(t + 1) * P],
                                        RA[pr, t, :, :], start=True, stop=True, after=free if q == 0 else ())
                            e = dve(V.tensor_tensor, dst[:, 2 * hf:2 * hf + 2, :, :],
                                    bank[:, :].rearrange("p (b m n) -> p b m n", b=2, m=2),
                                    mask2.unsqueeze(1).to_broadcast([P, 2, 2, P]), ALU.mult, after=[mm, masks_ready])
                            psum.give(bank, [e])
                    idb = ident.unsqueeze(1).to_broadcast([P, 4, P]) if False else ident[:, :].unsqueeze(1).to_broadcast([P, 4, P])
                    lv = lambda i: lvl[:, i, :].unsqueeze(1).to_broadcast([P, 4, P])
                    dve(V.tensor_tensor, blk(Fm), ABT[:, :, 0, :], lv(6), ALU.mult)
                    dve(V.tensor_tensor, blk(Fm), blk(Fm), idb, ALU.add)
                    dve(V.tensor_tensor, blk(Gm), blk(Am), lv(0), ALU.mult, after=[am])
                    fg = dve(V.tensor_tensor, blk(Gm), blk(Gm), idb, ALU.add)
                    for i in range(1, 6):
                        al = pool(G.tensor_tensor, blk(AL), blk(Am), lv(i), ALU.mult, after=[am, last(lane_pe)])
                        bank, free = psum.take()
                        for q in range(4):
                            sl = slice(q * P, (q + 1) * P)
                            mm = pe(E.matmul, bank[:, sl], AL[:, sl], Fm[:, sl], start=True, stop=True,
                                    after=(free + [al, fg]) if q == 0 else ())
                        ym = act(S.activation, Ym, bank[:, :], ACT.Copy, after=[mm])
                        psum.give(bank, [ym])
                        bank, free = psum.take()
                        for q in range(4):
                            sl = slice(q * P, (q + 1) * P)
                            mm = pe(E.matmul, bank[:, sl], Gm[:, sl], Ym[:, sl], start=True, stop=True,
                                    after=(free + [ym]) if q == 0 else ())
                        bank2, free = psum.take()
                        if i < 5:
                            for q in range(4):
                                sl = slice(q * P, (q + 1) * P)
                                mm2 = pe(E.matmul, bank2[:, sl], Ym[:, sl], Gm[:, sl], start=True, stop=True,
                                         after=free if q == 0 else ())
                        fg = dve(V.tensor_tensor, Fm, Fm, bank[:, :], ALU.add, after=[mm])
                        psum.give(bank, [fg])
                        if i < 5:
                            fg = dve(V.tensor_tensor, Gm, Gm, bank2[:, :], ALU.add, after=[mm2])
                        psum.give(bank2, [fg] + list(free))
                    bank, free = psum.take()
                    for q, (t, h) in enumerate(tiles):
                        mm = pe(E.matmul, bank[:, at(t, h):at(t, h) + 64], AKT[:, q, 0, :],
                                VN[:, t * P + h * 64:t * P + h * 64 + 64], start=True, stop=True,
                                after=(free + [fg]) if q == 0 else ())
                    x0 = act(S.activation, X0, bank[:, 0:256], ACT.Copy, after=[mm])
                    psum.give(bank, [x0])
                    bank, free = psum.take()
                    for q, (t, h) in enumerate(tiles):
                        mm = pe(E.matmul, bank[:, at(t, h):at(t, h) + 64], Fm[:, q * P:(q + 1) * P],
                                X0[:, at(t, h):at(t, h) + 64], start=True, stop=True,
                                after=(free + [x0]) if q == 0 else ())
                    psum.give(bank, [act(S.activation, U0, bank[:, 0:256], ACT.Copy, after=[mm])])
                    bank, free = psum.take()
                    for i in range(2):
                        t = 2 * grp + i
                        for h in range(2):
                            mm = pe(E.matmul, bank[:, (2 * i + h) * P:(2 * i + h + 1) * P],
                                    AN[:, t * P:(t + 1) * P], Fm[:, (2 * h + i) * P:(2 * h + i + 1) * P],
                                    start=True, stop=True, after=free if (i, h) == (0, 0) else ())
                    bv = bank[:, :].rearrange("p (i h n) -> p i h n", i=2, h=2)
                    wtv = WT.rearrange("p (i n) -> p i n", i=2)
                    act(S.activation, wtv[0:64], bv[0:64, :, 0, :], ACT.Copy, after=[mm])
                    wt = act(S.activation, wtv[64:128], bv[64:128, :, 1, :], ACT.Copy)
                    psum.give(bank, [wt])
                    for i in range(2):
                        t = 2 * grp + i
                        tc = slice(t * P, (t + 1) * P)
                        ui = UU[:, i * P:(i + 1) * P]
                        for ch in range(2):
                            rows = slice(ch * 64, ch * 64 + 64)
                            bank, free = psum.take()
                            mm = pe(E.matmul, bank[:, 0:P], WT[:, i * P:(i + 1) * P], ST, start=True, stop=True,
                                    after=free + [wt, last(lane_dve)])
                            ybank, free = psum.take()
                            mm2 = pe(E.matmul, ybank[:, 0:P], RA[:, t, 1, :], ST, start=True, stop=True, after=free)
                            u = dve(V.tensor_tensor, ui[rows, :], bank[rows, 0:P], U0[rows, i * P:(i + 1) * P],
                                    ALU.add, after=[mm, wt])
                            ycp = act(S.activation, YN[rows, t, :], ybank[rows, 0:P], ACT.Copy, after=[mm2])
                            psum.give(bank, [u])
                            psum.give(ybank, [ycp])
                            bank, free = psum.take()
                            pe(E.matmul, bank[:, 0:P], KN[rows, tc], VN[rows, tc], start=True, stop=False, after=free)
                            mm = pe(E.matmul, bank[:, 0:P], BN[rows, tc], ui[rows, :], start=False, stop=True,
                                    after=[u])
                            n = 2 * t + ch
                            for h in range(2):
                                pr = slice(h * 64, h * 64 + 64)
                                s = dve(V.scalar_tensor_tensor, ST[pr, pr], ST[pr, pr], WC[pr, n:n + 1],
                                        bank[pr, pr], ALU.mult, ALU.add, after=[mm, mm2])
                            psum.give(bank, [s])
                        bank, free = psum.take()
                        for h in range(2):
                            hs = slice(h * 64, h * 64 + 64)
                            pe(E.matmul, bank[:, hs], ABT[:, 2 * h + i, 1, :], ui[:, hs], start=True, stop=False,
                               after=free + [u] if h == 0 else ())
                            mm = pe(E.matmul, bank[:, hs], AKT[:, 2 * h + i, 1, :], VN[:, t * P + h * 64:t * P + h * 64 + 64],
                                    start=False, stop=True)
                        psum.give(bank, [dve(V.tensor_tensor, YN[:, t, :], YN[:, t, :], bank[:, 0:P], ALU.add,
                                             after=[mm, ycp])])
                gn = lambda b: b.rearrange("p (g n) -> p g n", n=64)
                Y2 = MIX[:, 6, :]
                sm = STAT[:, 48:64]
                sv = STAT[:, 64:80]
                dve(V.tensor_reduce, sm, gn(Y2), AX.X, ALU.add)
                dve(V.tensor_scalar, sm, sm, 1.0 / 64, None, ALU.mult)
                smb = sm.unsqueeze(2).to_broadcast([P, 16, 64])
                dve(V.tensor_tensor, gn(Y2), gn(Y2), smb, ALU.subtract)
                x = act(S.activation, R, Y2, ACT.Square, after=[last(lane_dve), last(lane_pe)])
                dve(V.tensor_reduce, sv, gn(R), AX.X, ALU.add, after=[x])
                rstd_of(sv, sv, 1.0 / 64, 64e-5)
                dve(V.tensor_tensor, gn(Y2), gn(Y2), sv.unsqueeze(2).to_broadcast([P, 16, 64]), ALU.mult)
                g = dma(K[:, 0:P], T["rw_lnx_g"][0, c * P:(c + 1) * P].partition_broadcast(P), dma_misc,
                        after=both() + [last(lane_pe)])
                g = dma(K[:, P:2 * P], T["rw_lnx_b"][0, c * P:(c + 1) * P].partition_broadcast(P), dma_misc)
                dve(V.tensor_tensor, YN, YN, K[:, 0:P].unsqueeze(1).to_broadcast([P, NT, P]), ALU.mult, after=[g])
                dve(V.tensor_tensor, YN, YN, K[:, P:2 * P].unsqueeze(1).to_broadcast([P, NT, P]), ALU.add)
                dve(V.tensor_tensor, gn(R), gn(VN), BON.unsqueeze(2).to_broadcast([P, 16, 64]), ALU.mult)
                x = dve(V.tensor_tensor, Y2, Y2, R, ALU.add)
                for hf in range(2):
                    bank, tr = transposes([YN[:, hf * 4 + i, :] for i in range(4)], after=[x])
                    psum.give(bank, [copy_out(MIX[:, c, hf * HALF:(hf + 1) * HALF], bank[:, :], [tr])])
                boundary()

        def band_attention():
            w = area([("QT", 4096), ("KT", 4096), ("VN", 4096), ("BIAS", 2048), ("FAR", 384), ("S0", 640), ("S1", 640),
                      ("PT0", 640), ("PT1", 640), ("O", 512)])
            QT = w["QT"].rearrange("p (c n) -> p c n", c=4)
            KT = w["KT"].rearrange("p (c n) -> p c n", c=4)
            VN = w["VN"].rearrange("p (t n) -> p t n", t=NT)
            BIAS = w["BIAS"].rearrange("p (h n) -> p h n", h=8)
            src = T["att_bias_wide"]
            diag = bass.AP(tensor=src.tensor, offset=P - 1, ap=[[8 * 384 - 1, P], [384, 8], [1, 256]])
            d2 = dma(BIAS, diag, dma_misc)
            b = pool(G.memset, BIAS[0:64, :, 192:256], NEG, after=[d2])
            pool(G.memset, w["FAR"], 0.0)
            bias_ready = pool(G.memset, w["FAR"][64:128, 0:64], NEG)
            WIN = T["w_in_e"][0]
            for c0, dst, scale in ((2176, QT, 0.125), (2688, KT, 1.0)):
                slot, wv, ws = load_w([(WIN, c0, HALF)], KD)
                for ct in range(4):
                    def evac(bank, half, mm, ct=ct):
                        return act(S.activation, dst[:, ct, half * HALF:(half + 1) * HALF], bank[:, :], ACT.Copy,
                                   scale=scale, after=[mm])
                    product_T(wv, ws, XT, KD, ct * P, evac)
                done_w(slot)
            slot, wv, ws = load_w([(WIN, 3200, HALF)], KD)
            for t in range(NT):
                product_N(wv, ws, XT, KD, t, lambda b, mm, t=t: copy_out(VN[:, t, :], b[:, :], [mm]))
            done_w(slot)
            qkv_ready = both()
            s_ring, pt_ring = Ring([w["S0"], w["S1"]]), Ring([w["PT0"], w["PT1"]])
            stat = STAT[:, 48:80].rearrange("p (a h) -> p a h", a=4)
            for i in range(NT):
                obank, ofree = psum.take()
                for h in range(8):
                    yield
                    pr, ct = slice(64 * (h % 2), 64 * (h % 2) + 64), h // 2
                    near, far = min(i, 1) + 1, max(min(i, 4) - 1, 0)
                    nk = near + far
                    k0 = i + 1 - nk
                    Sb, sfree = s_ring.take()
                    q = QT[pr, ct, i * P:(i + 1) * P]
                    if far:
                        bank, free = psum.take()
                        mm = pe(E.matmul, bank[:, 0:far * P], q, KT[pr, ct, k0 * P:(k0 + far) * P], start=True,
                                stop=True, after=free + qkv_ready)
                        off = (3 - far) * P
                        e = dve(V.scalar_tensor_tensor, Sb[:, 0:far * P], bank[:, 0:far * P],
                                PAR[:, bias_far_at + h:bias_far_at + h + 1], w["FAR"][:, off:off + far * P]
                                if far == 3 else w["FAR"][:, P:P + far * P], ALU.add, ALU.add,
                                after=[mm, bias_ready, par_ready] + sfree)
                        psum.give(bank, [e])
                    bank, free = psum.take()
                    mm = pe(E.matmul, bank[:, 0:near * P], q, KT[pr, ct, (k0 + far) * P:(i + 1) * P], start=True,
                            stop=True, after=free + qkv_ready)
                    e = dve(V.tensor_tensor, Sb[:, far * P:nk * P], bank[:, 0:near * P],
                            BIAS[:, h, (2 - near) * P:256], ALU.add, after=[mm, bias_ready] + sfree)
                    psum.give(bank, [e])
                    x = dve(V.tensor_reduce, stat[:, 0, h:h + 1], Sb[:, 0:nk * P], AX.X, ALU.max, negate=True)
                    x = act(S.activation, Sb[:, 0:nk * P], Sb[:, 0:nk * P], ACT.Exp, bias=stat[:, 0, h:h + 1],
                            accum_out=stat[:, 1, h:h + 1], after=[x])
                    PT, pfree = pt_ring.take()
                    for a0 in range(0, nk, 4):
                        n = min(4, nk - a0)
                        bank, tr = transposes([Sb[:, (a0 + j) * P:(a0 + j + 1) * P] for j in range(n)], after=[x])
                        e = copy_out(PT[:, a0 * P:(a0 + n) * P], bank[:, 0:n * P], [tr] + pfree)
                        psum.give(bank, [e])
                        es = both()
                    s_ring.give(Sb, [tr])
                    for j in range(nk):
                        mm = pe(E.matmul, obank[:, h * 64:(h + 1) * 64], PT[:, j * P:(j + 1) * P],
                                VN[:, k0 + j, h * 64:(h + 1) * 64], start=j == 0, stop=j == nk - 1,
                                after=(es + (ofree if h == 0 else [])) if j == 0 else ())
                    pt_ring.give(PT, [mm])
                x = dve(V.reciprocal, stat[:, 2, :], stat[:, 1, :], after=[x])
                x = dve(V.tensor_tensor, w["O"].rearrange("p (h n) -> p h n", h=8),
                        obank[:, :].rearrange("p (h n) -> p h n", h=8),
                        stat[:, 2, :].unsqueeze(2).to_broadcast([P, 8, 64]), ALU.mult, after=[mm, last(lane_pe)])
                psum.give(obank, [x])
                bank, tr = transposes([w["O"][:, j * P:(j + 1) * P] for j in range(4)], after=[x])
                psum.give(bank, [copy_out(MIX[:, 4:8, i * P:(i + 1) * P],
                                          bank[:, :].rearrange("p (c n) -> p c n", c=4), [tr])])

        def odd_layer():
            w = area([("VN", 8192), ("SGW", 1024), ("SGT", 1024), ("SGB", 1024), ("grow", 1024), ("brow", 1024),
                      ("junk", 1024), ("xn0", 1024), ("xn1", 1024)])
            sgw = dma(w["SGW"].rearrange("p (g j) -> p g j", g=8), T["sg_w"][0].rearrange("g i j -> i g j"), dma_misc)
            sgw = dma(w["SGB"], T["sg_b"][0].rearrange("g i -> (g i)").partition_broadcast(P), dma_misc)
            sgw = dma(w["grow"], T["sg_ln_g"][0].partition_broadcast(P), dma_misc)
            sgw = dma(w["brow"], T["sg_ln_b"][0].partition_broadcast(P), dma_misc)
            xt_ready = rms_to_XT("norm_g'", w)
            for hf in range(2):
                bank, tr = transposes([w["SGW"][:, (hf * 4 + i) * P:(hf * 4 + i + 1) * P] for i in range(4)], after=[sgw])
                psum.give(bank, [copy_out(w["SGT"][:, hf * HALF:(hf + 1) * HALF], bank[:, :], [tr])])
            sgt = w["SGT"].rearrange("p (g i) -> p g i", g=8)
            sgt_ready = pool(G.memset, sgt[64:128, :, 0:64], 0.0, after=both())
            WIN = T["w_in_o"][0]
            VN = w["VN"].rearrange("p (t n) -> p t n", t=NT)
            for c0 in (0, HALF):
                slot, wv, ws = load_w([(WIN, D + c0, HALF)], KD)
                for t in range(NT):
                    product_N(wv, ws, XT, KD, t, lambda b, mm, t=t: act(
                        S.activation, VN[:, t, c0:c0 + HALF], b[:, :], ACT.Gelu_apprx_tanh, after=[mm]),
                        after=[xt_ready])
                done_w(slot)
            v_ready = last(lane_act)
            for t in range(NT):
                dve(V.bn_stats, BST[:, 0:6], VN[:, t, 0:HALF], after=[v_ready])
                dve(V.bn_stats, BST[:, 6:12], VN[:, t, HALF:D])
                dve(V.bn_aggr, MV[:, t, :], BST)
            r = rstd_of(RS, MV[:, :, 1], 1.0, 1e-5)
            for t in range(NT):
                a = dve(V.tensor_scalar, VN[:, t, :], VN[:, t, :], MV[:, t, 0:1], RS[:, t:t + 1],
                        ALU.subtract, ALU.mult)
                b = pool(G.tensor_tensor, VN[:, t, :], VN[:, t, :], w["grow"], ALU.mult, after=[a, sgw])
                b = dve(V.tensor_tensor, VN[:, t, :], VN[:, t, :], w["brow"], ALU.add, after=[b])
                for hf in range(2):
                    bank, free = psum.take()
                    for g in range(4):
                        gg = hf * 4 + g
                        mm = pe(E.matmul, bank[:, g * P:(g + 1) * P], VN[:, t, gg * P:(gg + 1) * P], sgt[:, gg, :],
                                start=True, stop=True, after=(free + [b, sgt_ready]) if g == 0 else ())
                    e = dve(V.tensor_tensor, MIX[:, hf * 4:hf * 4 + 4, t * P:(t + 1) * P],
                            bank[:, :].rearrange("p (c n) -> p c n", c=4),
                            w["SGB"][:, hf * HALF:(hf + 1) * HALF].rearrange("p (c n) -> p c n", c=4), ALU.add,
                            after=[mm])
                    psum.give(bank, [e])
            mix_ready = last(lane_dve)
            for base, func in ((0, ACT.Gelu_apprx_tanh), (2 * D, ACT.Silu)):
                for c0 in (0, HALF):
                    gate_T(WIN, base + c0, lambda ct: MIX[:, c0 // P + ct, :], func, after=[last(lane_dve)])
            project_out(T["w_out_o"][0], MIX, KD, [last(lane_pool)])
            boundary()
            w = area([("grow", 1024), ("junk", 1024)])
            g = dma(w["grow"], T["final_g"].partition_broadcast(P), dma_misc)
            r = rms_stats(w["junk"], 1e-6)
            for t in range(NT):
                x = dve(V.scalar_tensor_tensor, H[:, t, :], H[:, t, :], RS[:, t:t + 1], w["grow"], ALU.mult, ALU.mult,
                        after=[r, g])
            boundary()

        Z2 = T["w_in_2"][0]
        AQ, AK, AV, AG, BG1, BG2, BG, CQ, CK, CV, CG, MG = (0, 512, 640, 768, 1280, 1792, 2304, 2816, 3328, 3840, 4352,
                                                            4864)

        def head_norm_evac(dst, bank, mm, gname, scale, tmp):
            (raw, sq), free = tmp.take()
            a = act(S.activation, raw, bank[:, :], ACT.Copy, after=[mm] + free)
            a = act(S.activation, sq, raw, ACT.Square, after=[a])
            b2, free = psum.take()
            m2 = pe(E.matmul, b2[:, :], head_ones[:, :], sq, start=True, stop=True, after=free + [a, consts_ready])
            d = dve(V.tensor_scalar, sq, b2[:, :], 1.0 / (64 * scale * scale), 1e-6 / (scale * scale), ALU.mult,
                    ALU.add, after=[m2])
            psum.give(b2, [d])
            a = act(S.activation, sq, sq, ACT.Sqrt, after=[d])
            d = dve(V.reciprocal, sq, sq, after=[a])
            d = dve(V.scalar_tensor_tensor, dst, raw, col(gname, 0), sq, ALU.mult, ALU.mult)
            tmp.give((raw, sq), [d])
            return a

        def merge(branch, w_o, Y, after):
            for c0 in (0, HALF):
                slot, wv, ws = load_w([(w_o, c0, HALF)], 4)
                slot2, wv2, ws2 = load_w([(Z2, MG + branch * D + c0, HALF)], KD)
                for ct in range(4):
                    mt = c0 // P + ct
                    held = {}

                    def evac_gate(bank, half, mm):
                        g, free = gate_tmp.take()
                        a = act(S.activation, g, bank[:, :], ACT.Sigmoid, after=[mm] + free)
                        held[half] = (g, a)
                        return a

                    def evac_y(bank, half, mm):
                        g, a = held[half]
                        dst = MIX[:, mt, half * HALF:(half + 1) * HALF]
                        if branch == 0:
                            d = dve(V.tensor_tensor, dst, g, bank[:, :], ALU.mult, after=[mm, a])
                            gate_tmp.give(g, [d])
                            return d
                        d = dve(V.tensor_tensor, g, g, bank[:, :], ALU.mult, after=[mm, a])
                        m = pool(G.tensor_tensor, dst, dst, g, ALU.add, after=[d])
                        gate_tmp.give(g, [m])
                        return d

                    product_T(wv2, ws2, XT, KD, ct * P, evac_gate)
                    product_T(wv, ws, Y, 4, ct * P, evac_y, after=after)
                done_w(slot)
                done_w(slot2)

        def window_attention():
            w = area([("QT", 4096), ("KT", 2048), ("VN", 1024), ("Y", 4096), ("MW", 256),
                      ("t0", 512), ("t1", 512), ("t2", 512), ("t3", 512),
                      ("S0", 512), ("S1", 512), ("PT0", 512), ("PT1", 512), ("O", 512)])
            QT = w["QT"].rearrange("p (c n) -> p c n", c=4)
            KT = w["KT"].rearrange("p (c n) -> p c n", c=2)
            VN = w["VN"].rearrange("p (t n) -> p t n", t=NT)
            Y = w["Y"].rearrange("p (c n) -> p c n", c=4)
            tmp = Ring([(w["t0"], w["t1"]), (w["t2"], w["t3"])])
            MW = w["MW"]
            pool(G.memset, MW, 0.0)
            pool(G.affine_select, out=MW, in_=MW, compare_op=ALU.is_ge, fill=NEG, base=P, pattern=[[-1, 256]],
                 channel_multiplier=1)
            mask = pool(G.affine_select, out=MW, in_=MW, compare_op=ALU.is_ge, fill=NEG, base=-1, pattern=[[1, 256]],
                        channel_multiplier=-1)
            slot, wv, ws = load_w([(Z2, AQ, HALF)], KD)
            for ct in range(4):
                product_T(wv, ws, XT, KD, ct * P, lambda b, half, mm, ct=ct: head_norm_evac(
                    QT[:, ct, half * HALF:(half + 1) * HALF], b, mm, "attn_q_norm_g_2", 0.125, tmp))
            done_w(slot)
            slot, wv, ws = load_w([(Z2, AK, 64), (Z2, AK, 64), (Z2, AK + 64, 64), (Z2, AK + 64, 64), (Z2, AV, P)], KD)
            for kv in range(2):
                product_T(wv, ws, XT, KD, kv * P, lambda b, half, mm, kv=kv: head_norm_evac(
                    KT[:, kv, half * HALF:(half + 1) * HALF], b, mm, "attn_k_norm_g_2", 1.0, tmp))
            for t in range(NT):
                product_N(wv, ws, XT, KD, t, lambda b, mm, t=t: copy_out(VN[:, t, :], b[:, 0:P], [mm]), n=P, c0=256)
            done_w(slot)
            ready = both()
            s_ring, pt_ring = Ring([w["S0"], w["S1"]]), Ring([w["PT0"], w["PT1"]])
            st = STAT[:, 48:96].rearrange("p (a h) -> p a h", a=6)
            sinks = PAR[:, par_at["sinks"]:par_at["sinks"] + 8]
            for i in range(NT):
                obank, ofree = psum.take()
                nk = min(i, 1) + 1
                n = nk * P
                for hp in range(4):
                    yield
                    Sb, sfree = s_ring.take()
                    S2 = Sb.rearrange("p (h n) -> p h n", h=2)
                    for h in range(2):
                        pr = slice(64 * h, 64 * h + 64)
                        bank, free = psum.take()
                        mm = pe(E.matmul, bank[:, 0:n], QT[pr, hp, i * P:(i + 1) * P],
                                KT[pr, hp // 2, (i + 1 - nk) * P:(i + 1) * P], start=True, stop=True,
                                after=free + ready)
                        e = dve(V.tensor_tensor, S2[:, h, 0:n], bank[:, 0:n], MW[:, 256 - n:256], ALU.add,
                                after=[mm, mask] + sfree)
                        psum.give(bank, [e])
                    hs = slice(2 * hp, 2 * hp + 2)
                    dve(V.tensor_reduce, st[:, 0, hs], S2[:, :, 0:n], AX.X, ALU.max)
                    dve(V.tensor_tensor, st[:, 0, hs], st[:, 0, hs], sinks[:, hs], ALU.max, after=[par_ready])
                    x = dve(V.tensor_scalar, st[:, 1, hs], st[:, 0, hs], -1.0, None, ALU.mult)
                    for h in range(2):
                        hh = 2 * hp + h
                        e = act(S.activation, S2[:, h, 0:n], S2[:, h, 0:n], ACT.Exp, bias=st[:, 1, hh:hh + 1],
                                accum_out=st[:, 2, hh:hh + 1], after=[x])
                    PT, pfree = pt_ring.take()
                    bank, tr = transposes([S2[:, h, j * P:(j + 1) * P] for h in range(2) for j in range(nk)], after=[e])
                    cp = copy_out(PT[:, 0:2 * n], bank[:, 0:2 * n], [tr] + pfree)
                    psum.give(bank, [cp])
                    s_ring.give(Sb, [tr])
                    for h in range(2):
                        hh = 2 * hp + h
                        for j in range(nk):
                            mm = pe(E.matmul, obank[:, hh * 64:(hh + 1) * 64], PT[:, (h * nk + j) * P:(h * nk + j + 1) * P],
                                    VN[:, i + 1 - nk + j, (hp // 2) * 64:(hp // 2) * 64 + 64], start=j == 0,
                                    stop=j == nk - 1, after=([cp] + ofree) if j == 0 else ())
                    pt_ring.give(PT, [mm])
                d = dve(V.tensor_tensor, st[:, 3, :], sinks, st[:, 0, :], ALU.subtract)
                a = act(S.activation, st[:, 4, :], st[:, 3, :], ACT.Exp, after=[d])
                dve(V.tensor_tensor, st[:, 4, :], st[:, 4, :], st[:, 2, :], ALU.add, after=[a])
                dve(V.reciprocal, st[:, 4, :], st[:, 4, :])
                x = dve(V.tensor_tensor, w["O"].rearrange("p (h n) -> p h n", h=8),
                        obank[:, :].rearrange("p (h n) -> p h n", h=8),
                        st[:, 4, :].unsqueeze(2).to_broadcast([P, 8, 64]), ALU.mult, after=[mm, last(lane_pe)])
                psum.give(obank, [x])
                bank, tr = transposes([w["O"][:, j * P:(j + 1) * P] for j in range(4)], after=[x])
                psum.give(bank, [copy_out(Y[:, :, i * P:(i + 1) * P], bank[:, :].rearrange("p (c n) -> p c n", c=4),
                                          [tr])])
            ready = both()
            gate_T(Z2, AG, lambda ct: Y[:, ct, :], ACT.Silu, after=ready)
            merge(0, T["w_o_attn_2"][0], Y, [last(lane_pool)])

        def conformer():
            W0 = 1056
            w = area([("U", 4 * W0), ("Y", 4096), ("ACC", 4096), ("t0", 512), ("t1", 512), ("SQ", 2048), ("MU", 1024),
                      ("RSD", 1024)])
            U = w["U"].rearrange("p (c n) -> p c n", c=4)
            Y = w["Y"].rearrange("p (c n) -> p c n", c=4)
            ACC = w["ACC"].rearrange("p (c n) -> p c n", c=4)
            pad = dve(V.memset, U[:, :, 0:30], 0.0)
            sg = Ring([w["t0"], w["t1"]])
            slot, wv, ws = load_w([(Z2, BG1, HALF)], KD)
            slot2, wv2, ws2 = load_w([(Z2, BG2, HALF)], KD)
            for ct in range(4):
                held = {}

                def evac_b(bank, half, mm):
                    g, free = sg.take()
                    a = act(S.activation, g, bank[:, :], ACT.Sigmoid, after=[mm] + free)
                    held[half] = (g, a)
                    return a

                def evac_a(bank, half, mm):
                    g, a = held[half]
                    d = dve(V.tensor_tensor, U[:, ct, 30 + half * HALF:30 + (half + 1) * HALF], g, bank[:, :],
                            ALU.mult, after=[mm, a])
                    sg.give(g, [d])
                    return d

                product_T(wv2, ws2, XT, KD, ct * P, evac_b)
                product_T(wv, ws, XT, KD, ct * P, evac_a)
            done_w(slot)
            done_w(slot2)
            for ct in range(4):
                yield
                tap = lambda j: col("conv_w_2", ct * 31 + j)
                dve(V.tensor_scalar, ACC[:, ct, :], U[:, ct, 0:SEQ], tap(0), col("conv_b_2", ct), ALU.mult, ALU.add)
                for j in range(1, 31):
                    dve(V.scalar_tensor_tensor, ACC[:, ct, :], U[:, ct, j:j + SEQ], tap(j), ACC[:, ct, :], ALU.mult,
                        ALU.add)
            ones = w["SQ"][:, 0:P]
            on = dve(V.memset, w["t0"][:, 0:P], 1.0)
            ones = w["t0"][:, 0:P]
            MU, RSD = w["MU"], w["RSD"]
            for half in range(2):
                sl = slice(half * HALF, (half + 1) * HALF)
                SQ = w["SQ"].rearrange("p (c n) -> p c n", c=4)
                bank, free = psum.take()
                for ct in range(4):
                    mm = pe(E.matmul, bank[:, :], ones, ACC[:, ct, sl], start=ct == 0, stop=ct == 3,
                            after=(free + [on]) if ct == 0 else ())
                d = dve(V.tensor_scalar, MU[:, sl], bank[:, :], 1.0 / 512, None, ALU.mult, after=[mm])
                psum.give(bank, [d])
                d = dve(V.tensor_tensor, ACC[:, :, sl], ACC[:, :, sl], MU[:, sl].unsqueeze(1).to_broadcast([P, 4, HALF]),
                        ALU.subtract)
                a = act(S.activation, SQ, ACC[:, :, sl], ACT.Square, after=[d, last(lane_pe)])
                bank, free = psum.take()
                for ct in range(4):
                    mm = pe(E.matmul, bank[:, :], ones, SQ[:, ct, :], start=ct == 0, stop=ct == 3,
                            after=(free + [a]) if ct == 0 else ())
                d = dve(V.tensor_scalar, RSD[:, sl], bank[:, :], 1.0 / 512, 1e-6, ALU.mult, ALU.add, after=[mm])
                psum.give(bank, [d])
                a = act(S.activation, RSD[:, sl], RSD[:, sl], ACT.Sqrt, after=[d])
                dve(V.reciprocal, RSD[:, sl], RSD[:, sl], after=[a])
                d = dve(V.tensor_tensor, ACC[:, :, sl], ACC[:, :, sl], RSD[:, sl].unsqueeze(1).to_broadcast([P, 4, HALF]),
                        ALU.mult)
            for ct in range(4):
                a = act(S.activation, Y[:, ct, :], ACC[:, ct, :], ACT.Silu, scale=col("conv_norm_g_2", ct),
                        bias=col("conv_norm_b_2", ct), after=[d])
            gate_T(Z2, BG, lambda ct: Y[:, ct, :], ACT.Silu, after=[a])
            merge(1, T["w_o_conv_2"][0], Y, [last(lane_pool)])

        def causal_mask(dst, fill_kept, fill_masked, strict):
            pool(G.memset, dst, fill_kept)
            return pool(G.affine_select, out=dst, in_=dst, compare_op=ALU.is_ge, fill=fill_masked,
                        base=-1 if strict else 0, pattern=[[-1, P]], channel_multiplier=1)

        def differential():
            w = area([("QT", 4096), ("KT", 4096), ("VN", 4096), ("MC", P),
                      ("t0", 512), ("t1", 512), ("P0", 1024), ("P1", 1024), ("PT", 1024), ("O", 512), ("L", 384)])
            Yb = w["QT"]
            QT = w["QT"].rearrange("p (c n) -> p c n", c=4)
            KT = w["KT"].rearrange("p (c n) -> p c n", c=4)
            VN = w["VN"].rearrange("p (t n) -> p t n", t=NT)
            tmp = Ring([(w["t0"], w["t1"])])
            mask = causal_mask(w["MC"], 0.0, NEG, False)
            lam_init = 0.8 - 0.6 * math.exp(-0.3 * 0)
            L = w["L"]
            lq = PAR[:, par_at["lq"]:par_at["lq"] + P]
            lk = PAR[:, par_at["lk"]:par_at["lk"] + P]
            d = dve(V.tensor_tensor, L[:, 0:P], lq, lk, ALU.mult, after=[par_ready])
            d = dve(V.tensor_reduce, L[:, P:P + 2], L[:, 0:P].rearrange("p (a n) -> p a n", a=2), AX.X, ALU.add)
            a = act(S.activation, L[:, P:P + 2], L[:, P:P + 2], ACT.Exp, after=[d])
            d = dve(V.tensor_tensor, L[:, 130:131], L[:, 129:130], L[:, 128:129], ALU.subtract, after=[a])
            d = dve(V.tensor_scalar, L[:, 130:131], L[:, 130:131], lam_init, None, ALU.subtract)
            neg_lam = L[:, 130:131]
            for c0, dst, gn, sc in ((CQ, QT, "diff_q_norm_g_2", 0.125), (CK, KT, "diff_k_norm_g_2", 1.0)):
                slot, wv, ws = load_w([(Z2, c0, HALF)], KD)
                for ct in range(4):
                    product_T(wv, ws, XT, KD, ct * P, lambda b, half, mm, ct=ct: head_norm_evac(
                        dst[:, ct, half * HALF:(half + 1) * HALF], b, mm, gn, sc, tmp))
                done_w(slot)
            slot, wv, ws = load_w([(Z2, CV, HALF)], KD)
            for t in range(NT):
                product_N(wv, ws, XT, KD, t, lambda b, mm, t=t: copy_out(VN[:, t, :], b[:, :], [mm]))
            done_w(slot)
            ready = both()
            st = STAT[:, 48:112].rearrange("p (a n) -> p a n", a=8)
            PP = [w["P0"], w["P1"]]
            PT = w["PT"]
            pt_free, pp_free = [], []
            for i in range(NT):
                obank, ofree = psum.take()
                n = (i + 1) * P
                for h in range(4):
                    yield
                    for c in range(2):
                        pr = slice(64 * c, 64 * c + 64)
                        q = QT[pr, h, i * P:(i + 1) * P]
                        parts = []
                        for k0 in range(0, n, HALF):
                            kn = min(HALF, n - k0)
                            bank, free = psum.take()
                            mm = pe(E.matmul, bank[:, 0:kn], q, KT[pr, h, k0:k0 + kn], start=True, stop=True,
                                    after=free + ready)
                            parts.append((bank, k0, kn, mm))
                        bank, k0, kn, mm = parts[-1]
                        dve(V.tensor_tensor, bank[:, kn - P:kn], bank[:, kn - P:kn], w["MC"], ALU.add,
                            after=[mm, mask])
                        for j, (bank, k0, kn, mm) in enumerate(parts):
                            d = dve(V.tensor_reduce, st[:, 0, j:j + 1], bank[:, 0:kn], AX.X, ALU.max, negate=True,
                                    after=[mm])
                        if len(parts) == 2:
                            d = dve(V.tensor_tensor, st[:, 0, 0:1], st[:, 0, 0:1], st[:, 0, 1:2], ALU.min)
                        for j, (bank, k0, kn, mm) in enumerate(parts):
                            a = act(S.activation, PP[c][:, k0:k0 + kn], bank[:, 0:kn], ACT.Exp, bias=st[:, 0, 0:1],
                                    accum_out=st[:, 1 + c, j:j + 1], after=[d] + pp_free)
                            psum.give(bank, [a])
                        if len(parts) == 2:
                            dve(V.tensor_tensor, st[:, 1 + c, 0:1], st[:, 1 + c, 0:1], st[:, 1 + c, 1:2], ALU.add,
                                after=[a])
                        dve(V.reciprocal, st[:, 3 + c, h:h + 1], st[:, 1 + c, 0:1], after=[a])
                    x = dve(V.tensor_scalar, st[:, 5, 0:1], st[:, 4, h:h + 1], st[:, 1, 0:1], neg_lam, ALU.mult, ALU.mult)
                    x = dve(V.scalar_tensor_tensor, PP[0][:, 0:n], PP[1][:, 0:n], st[:, 5, 0:1], PP[0][:, 0:n],
                            ALU.mult, ALU.add)
                    for a0 in range(0, i + 1, 4):
                        m = min(4, i + 1 - a0)
                        bank, tr = transposes([PP[0][:, (a0 + j) * P:(a0 + j + 1) * P] for j in range(m)], after=[x])
                        e = copy_out(PT[:, a0 * P:(a0 + m) * P], bank[:, 0:m * P], [tr] + pt_free)
                        psum.give(bank, [e])
                    pp_free = [tr]
                    es = both()
                    for j in range(i + 1):
                        mm = pe(E.matmul, obank[:, h * P:(h + 1) * P], PT[:, j * P:(j + 1) * P],
                                VN[:, j, h * P:(h + 1) * P], start=j == 0, stop=j == i,
                                after=(es + ofree) if j == 0 else ())
                    pt_free = [mm]
                O = w["O"].rearrange("p (h n) -> p h n", h=4)
                x = dve(V.tensor_tensor, O, obank[:, :].rearrange("p (h n) -> p h n", h=4),
                        st[:, 3, 0:4].unsqueeze(2).to_broadcast([P, 4, P]), ALU.mult, after=[mm, last(lane_pe)])
                psum.give(obank, [x])
                a = act(S.activation, w["t0"], w["O"], ACT.Square, after=[x])
                x = dve(V.tensor_reduce, st[:, 6, 0:4], w["t0"].rearrange("p (h n) -> p h n", h=4), AX.X, ALU.add,
                        after=[a])
                keep = 1.0 - lam_init
                x = rstd_of(st[:, 6, 0:4], st[:, 6, 0:4], 1.0 / (P * keep * keep), 1e-6 / (keep * keep))
                x = dve(V.tensor_tensor, O, O, st[:, 6, 0:4].unsqueeze(2).to_broadcast([P, 4, P]), ALU.mult)
                bank, tr = transposes([w["O"][:, j * P:(j + 1) * P] for j in range(4)], after=[x])
                e = dve(V.tensor_scalar, QT[:, :, i * P:(i + 1) * P], bank[:, :].rearrange("p (c n) -> p c n", c=4),
                        col("diff_subln_g_2", 0), None, ALU.mult, after=[tr])
                psum.give(bank, [e])
            ready = both()
            gate_T(Z2, CG, lambda ct: QT[:, ct, :], ACT.Silu, after=ready)
            merge(2, T["w_o_diff_2"][0], QT, [last(lane_pool)])

        ALPHA = float(2 ** 0.25)

        def ln_to_XT(gname, bname, w):
            for t, ready in ln_H(gname, bname, w, after=()):
                x = H_to_XT(t, ready)
            return x

        def residual_evac(bank, t, c0, mm):
            return dve(V.scalar_tensor_tensor, H[:, t, c0:c0 + HALF], H[:, t, c0:c0 + HALF], ALPHA, bank[:, :],
                       ALU.mult, ALU.add, after=[mm])

        def stick_breaking():
            w = area([("QT", 4096), ("KT", 4096), ("VN", 4096), ("MS", P), ("MN", P), ("ONE", 1024),
                      ("LN", 1024), ("Z", 1024), ("R", 1024), ("PT", 1024), ("O", 512)])
            QT = w["QT"].rearrange("p (c n) -> p c n", c=4)
            KT = w["KT"].rearrange("p (c n) -> p c n", c=4)
            VN = w["VN"].rearrange("p (t n) -> p t n", t=NT)
            causal_mask(w["MS"], 1.0, 0.0, True)
            causal_mask(w["MN"], 0.0, NEG, True)
            mask = pool(G.memset, w["ONE"], 1.0)
            WIN = T["w_in_3"][0]
            for c0, dst, scale in ((0, QT, 0.125), (512, KT, 1.0)):
                slot, wv, ws = load_w([(WIN, c0, HALF)], KD)
                for ct in range(4):
                    product_T(wv, ws, XT, KD, ct * P, lambda b, half, mm, ct=ct: act(
                        S.activation, dst[:, ct, half * HALF:(half + 1) * HALF], b[:, :], ACT.Copy, scale=scale,
                        after=[mm]))
                done_w(slot)
            slot, wv, ws = load_w([(WIN, 1024, HALF)], KD)
            for t in range(NT):
                product_N(wv, ws, XT, KD, t, lambda b, mm, t=t: copy_out(VN[:, t, :], b[:, :], [mm]))
            done_w(slot)
            ready = both()
            st = STAT[:, 48:64]
            LN, Z, R, PT = w["LN"], w["Z"], w["R"], w["PT"]
            pt_free = []
            for i in range(NT):
                obank, ofree = psum.take()
                n = (i + 1) * P
                for h in range(8):
                    yield
                    pr, ct = slice(64 * (h % 2), 64 * (h % 2) + 64), h // 2
                    q = QT[pr, ct, i * P:(i + 1) * P]
                    parts = []
                    for k0 in range(0, n, HALF):
                        kn = min(HALF, n - k0)
                        bank, free = psum.take()
                        mm = pe(E.matmul, bank[:, 0:kn], q, KT[pr, ct, k0:k0 + kn], start=True, stop=True,
                                after=free + ready)
                        parts.append((bank, k0, kn, mm))
                        act(S.activation, LN[:, k0:k0 + kn], bank[:, 0:kn], ACT.Abs, after=[mm, last(lane_dve)])
                    act(S.activation, LN[:, 0:n], LN[:, 0:n], ACT.Exp, scale=-1.0)
                    a = act(S.activation, LN[:, 0:n], LN[:, 0:n], ACT.Ln, bias=1.0)
                    for bank, k0, kn, mm in parts:
                        d = dve(V.scalar_tensor_tensor, R[:, k0:k0 + kn], bank[:, 0:kn], 0.0, LN[:, k0:k0 + kn],
                                ALU.max, ALU.add, after=[a])
                    dve(V.tensor_tensor, R[:, i * P:n], R[:, i * P:n], w["MS"], ALU.mult, after=[mask])
                    dve(V.tensor_tensor_scan, LN[:, 0:n][:, ::-1], w["ONE"][:, 0:n], R[:, 0:n][:, ::-1], 0.0, ALU.mult,
                        ALU.add)
                    for bank, k0, kn, mm in parts:
                        d = dve(V.tensor_tensor, Z[:, k0:k0 + kn], bank[:, 0:kn], LN[:, k0:k0 + kn], ALU.subtract,
                                after=[last(lane_pe)])
                        psum.give(bank, [d])
                    d = dve(V.tensor_tensor, Z[:, i * P:n], Z[:, i * P:n], w["MN"], ALU.add)
                    a = act(S.activation, Z[:, 0:n], Z[:, 0:n], ACT.Exp, after=[d])
                    for a0 in range(0, i + 1, 4):
                        m = min(4, i + 1 - a0)
                        bank, tr = transposes([Z[:, (a0 + j) * P:(a0 + j + 1) * P] for j in range(m)], after=[a])
                        e = copy_out(PT[:, a0 * P:(a0 + m) * P], bank[:, 0:m * P], [tr] + pt_free)
                        psum.give(bank, [e])
                    es = both()
                    for j in range(i + 1):
                        mm = pe(E.matmul, obank[:, h * 64:(h + 1) * 64], PT[:, j * P:(j + 1) * P],
                                VN[:, j, h * 64:(h + 1) * 64], start=j == 0, stop=j == i,
                                after=(es + ofree) if j == 0 else ())
                    pt_free = [mm]
                O = w["O"].rearrange("p (h n) -> p h n", h=8)
                a = act(S.activation, w["O"], obank[:, :], ACT.Copy, after=[mm, last(lane_pe)])
                psum.give(obank, [a])
                x = dve(V.tensor_tensor, R[:, 0:HALF], w["O"], w["O"], ALU.mult, after=[a])
                x = dve(V.tensor_reduce, st[:, 0:8], R[:, 0:HALF].rearrange("p (h n) -> p h n", h=8), AX.X, ALU.add)
                x = rstd_of(st[:, 0:8], st[:, 0:8], 1.0 / 64, 1e-6)
                x = dve(V.tensor_tensor, O, O, st[:, 0:8].unsqueeze(2).to_broadcast([P, 8, 64]), ALU.mult)
                bank, tr = transposes([w["O"][:, j * P:(j + 1) * P] for j in range(4)], after=[x])
                e = dve(V.tensor_tensor, MIX[:, 0:4, i * P:(i + 1) * P], bank[:, :].rearrange("p (c n) -> p c n", c=4),
                        cols("attn_out_g_3", 0, 4, P), ALU.mult, after=[tr])
                psum.give(bank, [e])

        def pooling():
            W0 = 1040
            w = area([("U", 4 * W0), ("S", 4 * W0), ("S2", 4 * W0), ("CNT", 64), ("WP", 512)])
            U = w["U"].rearrange("p (c n) -> p c n", c=4)
            buf = [w["S"].rearrange("p (c n) -> p c n", c=4), w["S2"].rearrange("p (c n) -> p c n", c=4)]
            CNT = w["CNT"].rearrange("p (g n) -> p g n", g=4)
            for b in (U, buf[0], buf[1]):
                pad = pool(G.memset, b[:, :, 0:16], 0.0)
            for g in range(4):
                win = 2 << g
                pool(G.memset, CNT[:, g, :], 1.0)
                for t in range(win - 1):
                    pool(G.memset, CNT[:, g, t:t + 1], float(np.float32(win / (t + 1))))
            cnt = last(lane_pool)
            wp = dma(w["WP"].rearrange("p (g d) -> p g d", g=4), T["w_pool_3"][0].rearrange("g c d -> c g d"), dma_misc)
            slot, wv, ws = load_w([(T["w_in_3"][0], 1536, HALF)], KD)
            for ct in range(4):
                product_T(wv, ws, XT, KD, ct * P, lambda b, half, mm, ct=ct: act(
                    S.activation, U[:, ct, 16 + half * HALF:16 + (half + 1) * HALF], b[:, :], ACT.Copy,
                    after=[mm, pad]))
            done_w(slot)
            yield
            u_ready = last(lane_act)
            for g in range(4):
                cur = U
                for lvl in range(g + 1):
                    sh = 1 << lvl
                    nxt = buf[lvl % 2]
                    d = dve(V.tensor_tensor, nxt[:, g, 16:16 + SEQ], cur[:, g, 16:16 + SEQ],
                            cur[:, g, 16 - sh:16 - sh + SEQ], ALU.add, after=[u_ready, cnt])
                    cur = nxt
                dst = buf[(g + 1) % 2][:, g, 16:16 + SEQ]
                win = 2 << g
                dve(V.tensor_scalar, dst, cur[:, g, 16:16 + SEQ], 1.0 / win, None, ALU.mult)
                dve(V.tensor_tensor, dst[:, 0:16], dst[:, 0:16], CNT[:, g, :], ALU.mult)
                d = dve(V.tensor_tensor, dst, dst, U[:, g, 16:16 + SEQ], ALU.subtract)
                for half in range(2):
                    bank, free = psum.take()
                    mm = pe(E.matmul, bank[:, :], w["WP"][:, g * P:(g + 1) * P],
                            dst[:, half * HALF:(half + 1) * HALF], start=True, stop=True, after=free + [d, wp])
                    psum.give(bank, [act(S.activation, MIX[:, 4 + g, half * HALF:(half + 1) * HALF], bank[:, :],
                                         ACT.Copy, scale=col("pool_scale_3", g), after=[mm])])

        def mlp():
            w = area([("HT", 8192)] + norm_area)
            HT = w["HT"].rearrange("p (c n) -> p c n", c=8)
            r2 = Ring([w["xn0"][:, 0:512], w["xn0"][:, 512:1024]])
            ht_free = []
            for grp in range(4):
                for c0 in (0, HALF):
                    slot, wv, ws = load_w([(T["w_up_3"][0], grp * D + c0, HALF)], KD)
                    for ct in range(4):
                        def evac(bank, half, mm, ct=ct):
                            tbuf, free = r2.take()
                            a = act(S.activation, tbuf, bank[:, :], ACT.Relu, after=[mm] + free)
                            m = pool(G.tensor_tensor, HT[:, c0 // P + ct, half * HALF:(half + 1) * HALF], tbuf, tbuf,
                                     ALU.mult, after=[a] + ht_free)
                            r2.give(tbuf, [m])
                            return a
                        product_T(wv, ws, XT, KD, ct * P, evac)
                    done_w(slot)
                ready = [last(lane_pool)]
                for c0 in (0, HALF):
                    slot, wv, ws = load_w([(T["w_down_3"][0][grp * D:(grp + 1) * D, :], c0, HALF)], KD)
                    for t in range(NT):
                        ev = residual_evac if grp == 0 else add_to_H
                        if grp == 0:
                            product_N(wv, ws, HT, KD, t, lambda b, mm, t=t: residual_evac(b, t, c0, mm), after=ready)
                        else:
                            product_N(wv, ws, HT, KD, t, lambda b, mm, t=t: dve(
                                V.tensor_tensor, H[:, t, c0:c0 + HALF], H[:, t, c0:c0 + HALF], bank_ap(b), ALU.add,
                                after=[mm]), after=ready)
                    done_w(slot)
                ht_free = [last(lane_pe)]

        def bank_ap(b):
            return b[:, :]

        def embed_gate():
            w = area([("PN", 2048), ("PTT", 2048), ("g0", 512), ("g1", 512), ("g2", 512), ("g3", 512)] )
            PN = w["PN"].rearrange("p (t n) -> p t n", t=NT)
            PTT = w["PTT"].rearrange("p (c n) -> p c n", c=2)
            pl = dma(PN, T["p_3"][0, 0].rearrange("(t p) n -> p t n", p=P), dma_misc)
            for c in range(2):
                for hf in range(2):
                    bank, tr = transposes([PN[:, hf * 4 + i, c * P:(c + 1) * P] for i in range(4)], after=[pl])
                    psum.give(bank, [copy_out(PTT[:, c, hf * HALF:(hf + 1) * HALF], bank[:, :], [tr])])
            ready = both()
            ring = Ring([w[f"g{i}"] for i in range(4)])
            for c0 in (0, HALF):
                slot, wv, ws = load_w([(T["w_ple_gate_3"][0], c0, HALF)], KD)
                slot2, wv2, ws2 = load_w([(T["w_ple_3"][0], c0, HALF)], 2)
                for t in range(NT):
                    held = {}

                    def evac_gate(b, mm):
                        g, free = ring.take()
                        a = act(S.activation, g, b[:, :], ACT.Sigmoid, after=[mm] + free)
                        held["g"] = (g, a)
                        return a

                    def evac_p(b, mm):
                        g, a = held["g"]
                        d = dve(V.tensor_tensor, g, g, b[:, :], ALU.mult, after=[mm, a])
                        h = H[:, t, c0:c0 + HALF]
                        d2 = dve(V.scalar_tensor_tensor, h, h, ALPHA, g, ALU.mult, ALU.add)
                        ring.give(g, [d2])
                        return d

                    product_N(wv, ws, XT, KD, t, evac_gate)
                    product_N(wv2, ws2, PTT, 2, t, evac_p, after=ready)
                done_w(slot)
                done_w(slot2)

        def run(gen):
            for _ in gen:
                pass

        def store_H(ready, src=None):
            for t in range(NT):
                st = dma(out[0, t * P:(t + 1) * P, :], H[:, t, :], dma_out, after=ready)
            lane_sp.items.append((None, (), {}, [st], Step(lane_sp, -1)))

        def block1():
            rms_to_XT("norm_g", area(norm_area))
            boundary()
            run(rwkv())
            boundary()
            run(band_attention())
            boundary()
            gate_T(T["w_in_e"][0], 1664, lambda ct: MIX[:, ct, :], ACT.Silu)
            gate_T(T["w_in_e"][0], 3712, lambda ct: MIX[:, 4 + ct, :], ACT.Silu)
            project_out(T["w_out_e"][0], MIX, KD, [last(lane_pool)])
            boundary()
            odd_layer()

        def block2():
            rms_to_XT("norm_g_2", area(norm_area))
            boundary()
            run(window_attention())
            boundary()
            run(conformer())
            boundary()
            run(differential())
            boundary()
            project_out(T["w_out_2"][0], MIX, KD, [])
            boundary()

        def block3():
            ln_area = [("grow", 1024), ("brow", 1024)]
            ln_to_XT("emb_ln_g_3", "emb_ln_b_3", area(ln_area))
            boundary()
            run(stick_breaking())
            boundary()
            run(pooling())
            boundary()
            for c0 in (0, HALF):
                slot, wv, ws = load_w([(T["w_out_3"][0], c0, HALF)], KD)
                for t in range(NT):
                    product_N(wv, ws, MIX, KD, t, lambda b, mm, t=t: residual_evac(b, t, c0, mm))
                done_w(slot)
            boundary()
            ln_to_XT("ln1_g_3", "ln1_b_3", area(ln_area))
            boundary()
            mlp()
            boundary()
            ln_to_XT("ln2_g_3", "ln2_b_3", area(ln_area))
            boundary()
            embed_gate()
            boundary()
            for _ in ln_H("ln3_g_3", "ln3_b_3", area(ln_area)):
                pass

        for ln in lanes:
            ln.items.append((None, (), {}, [x_in], last(ln) or x_in))
        for n in BLOCKS:
            (block1, block2, block3)[n - 1]()
        store_H([last(lane_dve), last(lane_act), last(lane_pool)])

        for ln in lanes + [lane_sp]:
            count_values(ln)
        block = ctx.enter_context(nc.Block())

        @block.sync
        def _(eng):
            emit(lane_sp, eng)

        @block.tensor
        def _(eng):
            emit(lane_pe, eng)

        @block.vector
        def _(eng):
            emit(lane_dve, eng)

        @block.scalar
        def _(eng):
            emit(lane_act, eng)

        @block.gpsimd
        def _(eng):
            emit(lane_pool, eng)


_NAMES = """x norm_g w_in_e shift_mu rw_w0 rw_w2 rw_a0 rw_a2 rw_kk rw_ka rw_rk rw_lnx_g rw_lnx_b att_bias w_out_e
w_in_o sg_ln_g sg_ln_b sg_w sg_b w_out_o final_g norm_g_2 w_in_2 attn_q_norm_g_2 attn_k_norm_g_2 attn_sinks_2
w_o_attn_2 conv_w_2 conv_b_2 conv_norm_g_2 conv_norm_b_2 w_o_conv_2 diff_q_norm_g_2 diff_k_norm_g_2 lambda_q_2
lambda_k_2 diff_subln_g_2 w_o_diff_2 w_out_2 p_3 emb_ln_g_3 emb_ln_b_3 w_in_3 attn_out_g_3 w_pool_3 pool_scale_3
w_out_3 ln1_g_3 ln1_b_3 w_up_3 w_down_3 ln2_g_3 ln2_b_3 w_ple_3 w_ple_gate_3 ln3_g_3 ln3_b_3""".split()


def kernel(**inputs):
    import concourse.bacc as bacc
    from concourse.bass_utils import run_bass_kernel_spmd

    nc = bacc.Bacc("TRN2", target_bir_lowering=False, num_devices=1)
    arrays, T = {}, {}
    arrays = {n: np.ascontiguousarray(inputs[n]) for n in _NAMES}
    arrays["channel_columns"] = channel_columns(inputs)
    rev = inputs["att_bias"][0][:, ::-1]
    wide = np.concatenate([np.repeat(rev[:, :1], P - 1, axis=1), rev], axis=1)
    arrays["att_bias_wide"] = np.ascontiguousarray(np.broadcast_to(wide, (P,) + wide.shape))
    arrays["att_bias_far"] = np.ascontiguousarray(rev[:, 0])
    for n, a in arrays.items():
        T[n] = nc.dram_tensor(n, a.shape, F32, kind="ExternalInput").ap()
    out = nc.dram_tensor("out", (1, SEQ, D), F32, kind="ExternalOutput").ap()
    build(nc, T, out)
    return run_bass_kernel_spmd(nc, [arrays], core_ids=[0]).results[0]["out"]
```

```python
import math
from contextlib import ExitStack

import concourse.bass as bass
import numpy as np
from concourse import mybir

F32 = mybir.dt.float32
F32R = mybir.dt.float32r
ACT = mybir.ActivationFunctionType
ALU = mybir.AluOpType
AX = mybir.AxisListType

P = 128
SEQ = 1024
D = 1024
NT = SEQ // P
KD = D // P
HALF = 512
NEG = -1e30


class Step:

    def __init__(self, lane, index):
        self.lane, self.index, self.value = lane, index, None


class Lane:

    def __init__(self, sem, in_order):
        self.sem, self.in_order, self.items, self.waited_for = sem, in_order, [], set()

    def put(self, call, args, kw, after):
        step = Step(self, len(self.items))
        if not self.in_order and self.items:
            after = list(after) + [self.items[-1][4]]
        for s in after:
            if s is not None:
                s.lane.waited_for.add(s.index)
        self.items.append((call, args, kw, [s for s in after if s is not None], step))
        return step


class DmaLane:

    def __init__(self, sem):
        self.sem, self.count, self.waited_for = sem, 0, set()


class Ring:

    def __init__(self, buffers):
        self.free = [(b, []) for b in buffers]

    def take(self):
        return self.free.pop(0)

    def give(self, buffer, last_users):
        self.free.append((buffer, list(last_users)))


def emit(lane, engine):
    reached, count = {}, 0
    for call, args, kw, after, step in lane.items:
        need = {}
        for s in after:
            level = s.value
            if level > need.get(s.lane.sem, 0):
                need[s.lane.sem] = level
        for sem, level in need.items():
            if level > reached.get(sem, 0):
                engine.wait_ge(sem, level)
                reached[sem] = level
        if call is None:
            continue
        made = call(*args, **kw)
        if step.lane is not lane:
            made.then_inc(step.lane.sem, 16)
        elif step.index in lane.waited_for:
            made.then_inc(lane.sem, 1)


def count_values(lane):
    count = 0
    for call, _, _, _, step in lane.items:
        if call is not None and step.lane is lane:
            if step.index in lane.waited_for:
                count += 1
                step.value = count


_COLUMNS = [("norm_g", 0, 8), ("shift_mu", 0, 13), ("rw_w0", 0, 4), ("rw_a0", 0, 4), ("rw_kk", 0, 4), ("rw_ka", 0, 4),
            ("rw_rk", 0, 4), ("norm_g", 1, 8), ("norm_g_2", 0, 8), ("attn_q_norm_g_2", 0, 1),
            ("attn_k_norm_g_2", 0, 1), ("diff_q_norm_g_2", 0, 1), ("diff_k_norm_g_2", 0, 1), ("conv_b_2", 0, 4),
            ("conv_norm_g_2", 0, 4), ("conv_norm_b_2", 0, 4), ("diff_subln_g_2", 0, 1), ("attn_out_g_3", 0, 4),
            ("pool_scale_3", 0, 4), ("conv_w_2", 0, 124)]


def column_plan():
    plan, at = {}, 0
    for name, layer, n in _COLUMNS:
        plan[name + ("'" if layer else "")] = (at, n)
        at += n
    return plan


def channel_columns(inputs):
    out = []
    for name, layer, n in _COLUMNS:
        a = np.asarray(inputs[name])[layer]
        if name == "conv_w_2":
            out.append(a.reshape(31, 4, P).transpose(2, 1, 0).reshape(P, 124))
            continue
        a = a.reshape(-1)
        if a.size == 64:
            a = np.tile(a, 2)
        out.append(a.reshape(n, P).T)
    return np.ascontiguousarray(np.concatenate(out, axis=1))


BLOCKS = (1, 2, 3)


def build(nc, T, out):
    ctx = ExitStack()
    with ctx:
        def sb(name, shape, scope=ctx, dtype=F32):
            return scope.enter_context(nc.sbuf_tensor(name, shape, dtype))

        def sem(name):
            return ctx.enter_context(nc.semaphore(name))

        H = sb("H", [P, NT, D])
        MIX = sb("MIX", [P, KD, SEQ])
        WS = [sb("WS0", [P, 4096])]
        ident = sb("ident", [P, P])
        head_ones = sb("head_ones", [P, P])
        PAR = sb("PAR", [P, 512])
        STAT = sb("STAT", [P, 256])
        until_mlp = ctx.enter_context(ExitStack())
        WS.append(sb("WS1", [P, 4096], until_mlp))
        XT = sb("XT", [P, KD, SEQ], until_mlp)
        GTMP = sb("GTMP", [P, 1024], until_mlp)
        WORK_N = 18304
        WORK = sb("WORK", [P, WORK_N], until_mlp)
        banks = [ctx.enter_context(nc.psum_tensor(f"bank{i}", [P, HALF], F32)) for i in range(8)]

        lane_pe = Lane(sem("s_pe"), True)
        lane_dve = Lane(sem("s_dve"), False)
        lane_act = Lane(sem("s_act"), False)
        lane_pool = Lane(sem("s_pool"), False)
        lane_sp = Lane(sem("s_sp"), True)
        lanes = [lane_pe, lane_dve, lane_act, lane_pool]
        w_lane = {id(WS[i]): DmaLane(sem(f"s_w{i}")) for i in range(2)}
        dma_par = DmaLane(sem("s_par"))
        dma_x = DmaLane(sem("s_x"))
        dma_x_tile = [DmaLane(sem(f"s_x{t}")) for t in range(NT)]
        dma_misc = DmaLane(sem("s_misc"))
        dma_out = DmaLane(sem("s_out"))
        dma_kept = DmaLane(sem("s_kept"))
        residual_kept = []

        psum = Ring(banks)
        wring = Ring(WS)

        def pe(call, *a, after=(), **kw):
            return lane_pe.put(call, a, kw, after)

        def dve(call, *a, after=(), **kw):
            return lane_dve.put(call, a, kw, after)

        def act(call, *a, after=(), **kw):
            return lane_act.put(call, a, kw, after)

        def pool(call, *a, after=(), **kw):
            return lane_pool.put(call, a, kw, after)

        def dma(dst, src, lane, after=()):
            step = Step(lane, 0)
            lane.count += 16
            step.value = lane.count
            for s in after:
                if s is not None:
                    s.lane.waited_for.add(s.index)
            lane_sp.items.append((nc.sync.dma_start, (dst, src), {}, [s for s in after if s is not None], step))
            return step

        V, S, G, E = nc.vector, nc.scalar, nc.gpsimd, nc.tensor

        def last(lane):
            return lane.items[-1][4] if lane.items else None

        def boundary():
            ends = []
            for ln in lanes:
                for item in reversed(ln.items):
                    if item[0] is not None:
                        ends.append(item[4])
                        break
            for ln in lanes + [lane_sp]:
                for s in ends:
                    s.lane.waited_for.add(s.index)
                ln.items.append((None, (), {}, list(ends), Step(ln, -1)))
            for ln in lanes:
                if not ln.in_order:
                    ln.items[-1] = (None, (), {}, list(ends), [s for s in ends if s.lane is ln][0])
            return ends

        par_at = {}
        par_used = [0]

        def par(name, ap2, cols):
            at = par_used[0]
            par_used[0] += cols
            assert par_used[0] <= 512
            dma(PAR[:, at:at + cols], ap2, dma_par)
            par_at[name] = at

        def col(name, c):
            return PAR[:, par_at[name] + c:par_at[name] + c + 1]

        def cols(name, c0, n, m):
            a = PAR[:, par_at[name] + c0:par_at[name] + c0 + n]
            return a.unsqueeze(2).to_broadcast([P, n, m])

        def area(spec, base=None, size=WORK_N, start=0):
            base = WORK[:, :] if base is None else base
            at, r = start, {}
            for name, n in spec:
                r[name] = base[:, at:at + n]
                at += n
            assert at <= size, at
            return r

        H_AREA = H[:, :, :].rearrange("p t n -> p (t n)")

        x_in = [dma(H[:, t, :], T["x"][0, t * P:(t + 1) * P, :], dma_x_tile[t]) for t in range(NT)]
        par("columns", T["channel_columns"], T["channel_columns"].shape[1])
        for n, (first, _) in column_plan().items():
            par_at[n] = par_at["columns"] + first
        par("sinks", T["attn_sinks_2"][0].partition_broadcast(P), 8)
        par("lq", T["lambda_q_2"][0].rearrange("a n -> (a n)").partition_broadcast(P), P)
        par("lk", T["lambda_k_2"][0].rearrange("a n -> (a n)").partition_broadcast(P), P)
        bias_far_at = par_used[0]
        par("bias_far", T["att_bias_far"].partition_broadcast(P), 8)
        par_ready = Step(dma_par, 0)
        par_ready.value = dma_par.count

        pool(G.memset, ident[:, :], 0.0)
        pool(G.affine_select, out=ident[:, :], in_=ident[:, :], compare_op=ALU.not_equal, fill=1.0,
             base=0, pattern=[[-1, P]], channel_multiplier=1)
        pool(G.memset, head_ones[:, :], 0.0)
        pool(G.memset, head_ones[0:64, 0:64], 1.0)
        consts_ready = pool(G.memset, head_ones[64:128, 64:128], 1.0)

        def eye(n=P):
            return ident[0:n, 0:n]

        def load_w(pieces, kt):
            key = [(src.tensor.name, c0, w) for src, c0, w in pieces] + [kt]
            if loaded_early:
                early_key, loaded = loaded_early.pop()
                assert key == early_key
                return loaded
            return load_now(pieces, kt)

        loaded_early = []

        def load_early(pieces, kt):
            loaded_early.append(([(src.tensor.name, c0, w) for src, c0, w in pieces] + [kt], load_now(pieces, kt)))

        def load_now(pieces, kt):
            slot, free = wring.take()
            width = sum(w for _, _, w in pieces)
            view = slot[:, 0:kt * width].rearrange("p (k n) -> p k n", k=kt)
            at = 0
            for src, c0, w in pieces:
                step = dma(view[:, :, at:at + w], src.rearrange("(k p) n -> p k n", p=P)[:, :, c0:c0 + w],
                           w_lane[id(slot)], after=free)
                at += w
            return slot, view, step

        def done_w(slot):
            wring.give(slot, [last(lane_pe)])

        def product_T(*args, **kw):
            for _ in product_T_pieces(*args, **kw):
                pass

        def product_T_pieces(wv, wstep, src, kt, c0, evac, after=()):
            for half in range(2):
                bank, free = psum.take()
                for k in range(kt):
                    mm = pe(E.matmul, bank[:, :], wv[:, k, c0:c0 + P], src[:, k, half * HALF:(half + 1) * HALF],
                            start=k == 0, stop=k == kt - 1,
                            after=(list(free) + [wstep] + list(after)) if k == 0 else ())
                psum.give(bank, [evac(bank, half, mm)])
                yield

        def product_N(wv, wstep, src, kt, t, evac, after=(), n=HALF, c0=0):
            bank, free = psum.take()
            for k in range(kt):
                mm = pe(E.matmul, bank[:, 0:n], src[:, k, t * P:(t + 1) * P], wv[:, k, c0:c0 + n],
                        start=k == 0, stop=k == kt - 1,
                        after=(list(free) + [wstep] + list(after)) if k == 0 else ())
            psum.give(bank, [evac(bank, mm)])

        def transposes(srcs, after=()):
            bank, free = psum.take()
            for i, s in enumerate(srcs):
                st = pe(E.transpose, bank[:, i * P:(i + 1) * P], s, ident[:, :],
                        after=(list(free) + list(after) + [consts_ready]) if i == 0 else ())
            return bank, st

        turn = [0]

        def copy_out(dst, src, after):
            turn[0] += 1
            if turn[0] % 2:
                return act(S.activation, dst, src, ACT.Copy, after=after)
            return dve(V.tensor_copy, dst, src, after=after)

        def add_to_H(bank, t, c0, mm, after=()):
            return dve(V.tensor_tensor, H[:, t, c0:c0 + HALF], H[:, t, c0:c0 + HALF], bank[:, :], ALU.add,
                       after=[mm] + list(after))

        def rstd_of(dst, src, scale, eps):
            a = dve(V.tensor_scalar, dst, src, scale, eps, ALU.mult, ALU.add)
            b = act(S.activation, dst, dst, ACT.Sqrt, after=[a])
            return dve(V.reciprocal, dst, dst, after=[b])

        SS = STAT[:, 0:8]
        MV = STAT[:, 8:24].rearrange("p (t a) -> p t a", a=2)
        BST = STAT[:, 24:36]
        RS = STAT[:, 36:44]

        def vector_of(name):
            return T[name] if len(T[name].shape) == 1 else T[name][0]

        def H_to_XT(t, ready):
            for half in range(2):
                bank, tr = transposes([H[:, t, (half * 4 + i) * P:(half * 4 + i + 1) * P] for i in range(4)],
                                      after=[ready])
                src = bank[:, :].rearrange("p (c n) -> p c n", c=4)
                at = (slice(None), slice(half * 4, half * 4 + 4), slice(t * P, (t + 1) * P))
                if SPLIT:
                    a = act(S.activation, SPLIT["XH"][at], src, ACT.Copy, after=[tr])
                    e = dve(V.tensor_tensor, SPLIT["XL"][at], src, SPLIT["XH"][at], ALU.subtract, after=[a])
                else:
                    e = copy_out(XT[at], src, [tr])
                psum.give(bank, [e])
            return e

        SPLIT = {}

        def start_split():
            until_mlp.close()
            for name, shape in (("XH", [P, KD, SEQ]), ("XL", [P, KD, SEQ]), ("HH", [P, 2, SEQ]), ("HL", [P, 2, SEQ]),
                                ("WH0", [P, 2048]), ("WL0", [P, 2048]), ("WH1", [P, 2048]), ("WL1", [P, 2048])):
                SPLIT[name] = sb(name, shape, ctx, F32R)
            rows = sb("ROWS", [P, 2 * D])
            N_AREA["grow"], N_AREA["brow"] = rows[:, 0:D], rows[:, D:2 * D]

        split_w = Ring(["0", "1"])
        MIX_AREA = MIX[:, :, :].rearrange("p c n -> p (c n)")
        stage_w = Ring([0, 1])
        stage_lane = [DmaLane(sem(f"s_stage{i}")) for i in range(2)]

        def load_split(w, kt):
            i, free = stage_w.take()
            stage = MIX_AREA[:, 2048 * i:2048 * (i + 1)]
            loaded = dma(stage.rearrange("p (k n) -> p k n", k=kt), w.rearrange("(k p) n -> p k n", p=P),
                         stage_lane[i], after=free)
            pair, free = split_w.take()
            hi, lo = SPLIT["WH" + pair], SPLIT["WL" + pair]
            a = act(S.activation, hi[:, :], stage, ACT.Copy, after=[loaded] + free)
            b = pool(G.tensor_tensor, lo[:, :], stage, hi[:, :], ALU.subtract, after=[a])
            stage_w.give(i, [b])
            return pair, hi[:, :].rearrange("p (k n) -> p k n", k=kt), lo[:, :].rearrange("p (k n) -> p k n", k=kt), b

        def each_loaded(chunks):
            ahead = load_split(*chunks[0])
            for nxt in chunks[1:] + [None]:
                now, ahead = ahead, load_split(*nxt) if nxt else None
                yield now
                split_w.give(now[0], [last(lane_pe)])

        def product_split(n, kt, left, right, after):
            bank, free = psum.take()
            for k in range(kt):
                (lh, ll), (rh, rl) = left(k), right(k)
                for j, (l, r) in enumerate(((lh, rh), (lh, rl), (ll, rh))):
                    mm = pe(E.matmul, bank[:, 0:n], l, r, start=(k, j) == (0, 0), stop=k == kt - 1 and j == 2,
                            after=(list(free) + list(after)) if (k, j) == (0, 0) else ())
            return bank, mm

        def tile_pairs(buf):
            return buf.rearrange("p (t n) -> p t n", n=P)

        def both():
            return [last(lane_dve), last(lane_act)]

        N_AREA = {n: WORK[:, WORK_N - (i + 1) * D:WORK_N - i * D]
                  for i, n in enumerate(("grow", "brow", "row2", "junk", "xn0", "xn1"))}
        xn_ring = Ring([N_AREA["xn0"], N_AREA["xn1"]])

        def load_row(place, name, after=()):
            return dma(N_AREA[place], vector_of(name).partition_broadcast(P), dma_misc, after=after)

        def rms_scale(t, eps, ready):
            a = act(S.activation, N_AREA["junk"], H[:, t, :], ACT.Square, accum_out=SS[:, t:t + 1], after=[ready])
            d = dve(V.tensor_scalar, RS[:, t:t + 1], SS[:, t:t + 1], 1.0 / D, eps, ALU.mult, ALU.add, after=[a])
            a = act(S.activation, RS[:, t:t + 1], RS[:, t:t + 1], ACT.Sqrt, after=[d])
            return dve(V.reciprocal, RS[:, t:t + 1], RS[:, t:t + 1], after=[a])

        def rms_tile(gname):
            def tile(t, ready):
                r = rms_scale(t, 1e-6, ready)
                xn, free = xn_ring.take()
                a = act(S.activation, xn, H[:, t, :], ACT.Copy, scale=RS[:, t:t + 1], after=[r] + free)
                yield
                for half in range(2):
                    bank, tr = transposes([xn[:, (half * 4 + i) * P:(half * 4 + i + 1) * P] for i in range(4)],
                                          after=[a])
                    e = dve(V.tensor_tensor, XT[:, half * 4:half * 4 + 4, t * P:(t + 1) * P],
                            bank[:, :].rearrange("p (c n) -> p c n", c=4), cols(gname, half * 4, 4, P), ALU.mult,
                            after=[tr, par_ready])
                    psum.give(bank, [e])
                xn_ring.give(xn, [tr])
                yield
            return tile

        def final_rms_tile(row_ready, then):
            def tile(t, ready):
                r = rms_scale(t, 1e-6, ready)
                x = dve(V.scalar_tensor_tensor, H[:, t, :], H[:, t, :], RS[:, t:t + 1], N_AREA["row2"], ALU.mult,
                        ALU.mult, after=[row_ready])
                kept = dma(T["residual"][t * P:(t + 1) * P, :], H[:, t, :], dma_kept, after=[x])
                residual_kept.append(kept)
                yield from then(t, x)
            return tile

        def scale_shift(x, t, rows_ready):
            d = dve(V.tensor_scalar, RS[:, t:t + 1], MV[:, t, 1:2], 1e-5, None, ALU.add)
            a = act(S.activation, RS[:, t:t + 1], RS[:, t:t + 1], ACT.Sqrt, after=[d])
            dve(V.scalar_tensor_tensor, x, x, MV[:, t, 0:1], N_AREA["grow"], ALU.subtract, ALU.mult,
                after=[rows_ready])
            dve(V.reciprocal, RS[:, t:t + 1], RS[:, t:t + 1], after=[a])
            return dve(V.scalar_tensor_tensor, x, x, RS[:, t:t + 1], N_AREA["brow"], ALU.mult, ALU.add)

        def ln_tile(rows_ready, transposed=True, stored=False):
            def tile(t, ready):
                dve(V.bn_stats, BST[:, 0:6], H[:, t, 0:HALF], after=[ready])
                dve(V.bn_stats, BST[:, 6:12], H[:, t, HALF:D])
                dve(V.bn_aggr, MV[:, t, :], BST)
                b = scale_shift(H[:, t, :], t, rows_ready)
                yield
                if transposed:
                    H_to_XT(t, b)
                if stored:
                    outs.append(dma(out[0, t * P:(t + 1) * P, :], H[:, t, :], dma_out, after=[b]))
                yield
            return tile

        outs = []

        def follow(products, tile, lag=1):
            waiting = []
            for done in products:
                for g in list(waiting):
                    if next(g, "end") == "end":
                        waiting.remove(g)
                if done:
                    g = tile(*done)
                    next(g)
                    waiting.append(g)
            while waiting:
                for g in list(waiting):
                    if next(g, "end") == "end":
                        waiting.remove(g)

        def projected_out(w, src, kt, after, evac, behind_weights=None):
            loaded = load_w([(w, 0, HALF)], kt)
            if behind_weights:
                behind_weights()
            for c0 in range(0, D, HALF):
                slot, wv, ws = load_w([(w, c0, HALF)], kt) if c0 else loaded
                for t in range(NT):
                    product_N(wv, ws, src, kt, t, lambda b, mm, t=t: evac(b, t, c0, mm), after=after)
                    yield (t, last(lane_dve)) if c0 else None
                done_w(slot)

        gate_tmp = Ring([GTMP[:, 0:HALF], GTMP[:, HALF:2 * HALF]])

        def gate_T(*args, **kw):
            for _ in gate_T_pieces(*args, **kw):
                pass

        def gate_T_pieces(wdram, c_base, ys, func, after=(), width=HALF):
            for ct in range(4):
                c0 = ct * P % width
                if c0 == 0:
                    slot, wv, ws = load_w([(wdram, c_base + ct * P, min(width, HALF - ct * P))], KD)
                def evac(bank, half, mm, ct=ct):
                    g, free = gate_tmp.take()
                    a = act(S.activation, g, bank[:, :], func, after=[mm] + free)
                    y = ys(ct)[:, half * HALF:(half + 1) * HALF]
                    m = pool(G.tensor_tensor, y, y, g, ALU.mult, after=[a] + list(after))
                    gate_tmp.give(g, [m])
                    return a
                yield from product_T_pieces(wv, ws, XT, KD, c0, evac)
                if ct == 3 or (ct + 1) * P % width == 0:
                    done_w(slot)

        def rwkv():
            KAPPA = math.exp(-0.5)
            B4 = 1024
            spec = [("LT", B4), ("RAW", 1025), ("R", B4), ("K", B4), ("A", B4), ("SIG", B4), ("CS", B4), ("EX", B4),
                    ("KK", B4), ("T1", B4), ("BT", B4), ("KTL", B4), ("VN", B4), ("RA", 2 * B4), ("ROWS", B4),
                    ("LVL", 7 * P), ("MASK2", 2 * P), ("W2", 512),
                    ("ST", P), ("WC", 16), ("BON", 16)]
            w = area(spec)
            RA = w["RA"].rearrange("p (t b n) -> p t b n", b=2, n=P)
            row_mask = w["ROWS"]
            LT, RAW = w["LT"], w["RAW"]
            pool(G.memset, row_mask, 1.0)
            pool(G.memset, row_mask.rearrange("p (c n) -> p c n", n=64)[:, :, 0:1], 0.0)
            pool(G.memset, RAW[:, 0:1], 0.0)
            lvl = w["LVL"].rearrange("p (m n) -> p m n", n=P)
            for i in range(6):
                m = 1 << i
                ng = P // (2 * m)
                pool(G.memset, lvl[:, i, :], 0.0)
                even = lvl[:, i, :].rearrange("p (g a b) -> p g a b", a=2, b=m)[:, :, 0, :]
                pool(G.memset, even, 1.0)
                pool(G.affine_select, out=even, in_=even, compare_op=ALU.is_ge, fill=0.0, base=-m,
                     pattern=[[-2 * m, ng], [0, m]], channel_multiplier=1)
                pool(G.affine_select, out=even, in_=even, compare_op=ALU.is_ge, fill=0.0, base=2 * m - 1,
                     pattern=[[2 * m, ng], [0, m]], channel_multiplier=-1)
            pool(G.memset, lvl[:, 6, :], 0.0)
            odd = lvl[:, 6, :].rearrange("p (g a) -> p g a", a=2)[:, :, 1]
            pool(G.affine_select, out=odd, in_=odd, compare_op=ALU.not_equal, fill=1.0, base=0,
                 pattern=[[-2, P // 2]], channel_multiplier=1)
            mask2 = w["MASK2"].rearrange("p (m n) -> p m n", n=P)
            pool(G.memset, w["MASK2"], 1.0)
            for i in range(2):
                pool(G.affine_select, out=mask2[:, i, :], in_=mask2[:, i, :], compare_op=ALU.is_ge, fill=0.0,
                     base=i - 1, pattern=[[1, P]], channel_multiplier=-1)
            masks_ready = pool(G.memset, mask2[0:64, :, 64:128], 0.0)
            WIN = T["w_in_e"][0]
            w2s = dma(w["W2"][0:64, :], T["rw_w2"][0], dma_misc)
            w2s = dma(w["W2"][64:128, :], T["rw_a2"][0], dma_misc)
            W2 = w["W2"]

            def shift_evac(dst, mu_col, tmp):
                def evac(bank, half, mm):
                    return act(S.activation, RAW[:, 1 + half * HALF:1 + (half + 1) * HALF], bank[:, :], ACT.Copy,
                               after=[mm, last(lane_dve), last(lane_pool)])
                def finish():
                    a = pool(G.tensor_tensor, tmp, RAW[:, 0:SEQ], RAW[:, 1:SEQ + 1], ALU.subtract,
                             after=[last(lane_act), masks_ready, last(lane_dve)])
                    return dve(V.scalar_tensor_tensor, dst, tmp, mu_col, RAW[:, 1:SEQ + 1], ALU.mult, ALU.add,
                               after=[a])
                return evac, finish

            slot, wv, ws = load_w([(WIN, 1536, P)], KD)
            evac, finish = shift_evac(LT, col("shift_mu", 12), w["EX"])
            product_T(wv, ws, XT, KD, 0, evac)
            done_w(slot)
            f = finish()
            lt_ready = act(S.activation, LT[0:64, :], LT[0:64, :], ACT.Tanh, after=[f])
            R, K, A, SIG, CS, EX, KK, T1 = (w[n] for n in ("R", "K", "A", "SIG", "CS", "EX", "KK", "T1"))
            BT, KTL, VN = (w[n] for n in ("BT", "KTL", "VN"))
            BN, KN, AN = RAW[:, 1:SEQ + 1], T1, KK
            ST, WC, BON = w["ST"], w["WC"], w["BON"]
            pair_end = []
            for c in range(4):
                yield
                YN = tile_pairs(MIX[:, c, :])
                slot, wv, ws = load_w([(WIN, g * 512 + c * P, P) for g in range(3)], KD)
                done = []
                for g, dst in ((0, R), (1, K), (2, T1)):
                    evac, finish = shift_evac(dst, col("shift_mu", g * 4 + c), EX)
                    yield from product_T_pieces(wv, ws, XT, KD, g * P, evac, after=[last(lane_dve)] + pair_end)
                    done.append(finish())
                done_w(slot)
                yield
                for hf in range(2):
                    bank, tr = transposes([T1[:, (hf * 4 + i) * P:(hf * 4 + i + 1) * P] for i in range(4)], after=done)
                    psum.give(bank, [copy_out(VN[:, hf * HALF:(hf + 1) * HALF], bank[:, :], [tr])])
                for hf in range(2):
                    sl = slice(hf * HALF, (hf + 1) * HALF)
                    bank, free = psum.take()
                    mm = pe(E.matmul, bank[:, :], W2[0:64, c * P:(c + 1) * P], LT[0:64, sl], start=True, stop=True,
                            after=free + [lt_ready, w2s])
                    psum.give(bank, [act(S.activation, SIG[:, sl], bank[:, :], ACT.Sigmoid,
                                         bias=col("rw_w0", c), after=[mm, par_ready])])
                    bank, free = psum.take()
                    mm = pe(E.matmul, bank[:, :], W2[64:128, c * P:(c + 1) * P], LT[64:128, sl], start=True, stop=True,
                            after=free)
                    psum.give(bank, [act(S.activation, A[:, sl], bank[:, :], ACT.Sigmoid,
                                         bias=col("rw_a0", c), after=[mm])])
                a_ready = last(lane_act)
                yield
                cs = dve(V.tensor_tensor_scan, CS, row_mask, SIG, 0.0, ALU.mult, ALU.add, after=[a_ready, masks_ready])
                x = dve(V.tensor_scalar, KK, K, col("rw_kk", c), None, ALU.mult)
                x = act(S.activation, T1, KK, ACT.Square, after=[x, last(lane_pe)])
                yield
                for hf in range(2):
                    sl = slice(hf * HALF, (hf + 1) * HALF)
                    bank, free = psum.take()
                    mm = pe(E.matmul, bank[:, :], head_ones[:, :], T1[:, sl], start=True, stop=True, after=free + [x])
                    psum.give(bank, [act(S.activation, EX[:, sl], bank[:, :], ACT.Sqrt,
                                         after=[mm, last(lane_dve)])])
                x = dve(V.tensor_scalar, EX, EX, 1e-12, None, ALU.max, after=[last(lane_act)])
                x = dve(V.reciprocal, EX, EX)
                x = dve(V.tensor_tensor, KK, KK, EX, ALU.mult)
                yield
                dve(V.tensor_scalar, T1, A, 1.0, col("rw_ka", c), ALU.subtract, ALU.mult)
                x = dve(V.scalar_tensor_tensor, K, T1, 1.0, K, ALU.add, ALU.mult)
                y = dve(V.scalar_tensor_tensor, T1, R, col("rw_rk", c), K, ALU.mult, ALU.mult)
                bank, free = psum.take()
                for t in range(NT):
                    mm = pe(E.matmul, bank[:, 2 * t:2 * t + 2], T1[:, t * P:(t + 1) * P],
                            head_ones[:, 0:P:64], start=True, stop=True, after=(free + [y]) if t == 0 else ())
                psum.give(bank, [dve(V.tensor_copy, BON, bank[:, 0:16], after=[mm])])
                yield
                b = dve(V.tensor_tensor, T1, KK, A, ALU.mult)
                ex = act(S.activation, EX, CS, ACT.Exp, scale=-KAPPA, after=[b])
                dve(V.tensor_tensor, RA[:, :, 1, :], tile_pairs(R), tile_pairs(EX), ALU.mult, after=[ex])
                wc = dve(V.tensor_copy, WC, EX.rearrange("p (c n) -> p c n", n=64)[:, :, 63])
                dve(V.tensor_tensor, SIG, CS, SIG, ALU.subtract)
                ex = act(S.activation, EX, SIG, ACT.Exp, scale=-KAPPA, after=[last(lane_dve)])
                dve(V.scalar_tensor_tensor, RA[:, :, 0, :], tile_pairs(KK), -1.0, tile_pairs(EX), ALU.mult, ALU.mult,
                    after=[ex])
                ex = act(S.activation, EX, CS, ACT.Exp, scale=KAPPA, after=[last(lane_dve)])
                dve(V.tensor_tensor, BT, T1, EX, ALU.mult, after=[ex])
                dve(V.tensor_tensor, KTL, K, EX, ALU.mult)
                yield
                wcb = WC.unsqueeze(2).to_broadcast([P, 16, 64])
                dve(V.tensor_tensor, SIG.rearrange("p (c n) -> p c n", n=64), BT.rearrange("p (c n) -> p c n", n=64),
                    wcb, ALU.mult)
                ops = dve(V.tensor_tensor, A.rearrange("p (c n) -> p c n", n=64),
                          KTL.rearrange("p (c n) -> p c n", n=64), wcb, ALU.mult)
                yield
                for src, dst in ((tile_pairs(SIG), BN), (tile_pairs(A), KN), (RA[:, :, 0, :], AN)):
                    yield
                    for hf in range(2):
                        bank, tr = transposes([src[:, hf * 4 + i, :] for i in range(4)], after=[ops])
                        psum.give(bank, [copy_out(dst[:, hf * HALF:(hf + 1) * HALF], bank[:, :], [tr])])
                x = dve(V.memset, ST, 0.0)
                mat = lambda b, i: b[:, i * HALF:(i + 1) * HALF]
                Am, AL, Fm, Gm, Ym = mat(R, 0), mat(R, 1), mat(K, 0), mat(K, 1), mat(A, 0)
                X0, UU = mat(A, 1)[:, 0:256], mat(SIG, 0)[:, 0:256]
                by4 = lambda b: b.rearrange("p (b m n) -> p b m n", b=4, m=2)
                handed = [(mat(A, 1)[:, 256:512], mat(SIG, 0)[:, 256:512], by4(CS), by4(EX)),
                          (mat(SIG, 1)[:, 0:256], mat(SIG, 1)[:, 256:512], by4(WS[0][:, 3072:4096]),
                           by4(WS[1][:, 3072:4096]))]
                wt_ready, st_ready = {}, [x]
                blk = lambda b: b.rearrange("p (b n) -> p b n", b=4)

                def factor(grp):
                    U0, WT, AKT, ABT = handed[grp % 2]
                    tiles = [(2 * grp + i, h) for h in range(2) for i in range(2)]
                    at = lambda t, h: (t - 2 * grp) * P + h * 64
                    before = both()
                    for hf in range(2):
                        bank, free = psum.take()
                        for q, (t, h) in enumerate(tiles[2 * hf:2 * hf + 2]):
                            pr = slice(h * 64, h * 64 + 64)
                            mm = pe(E.matmul, bank[:, q * P:(q + 1) * P], RA[pr, t, 0, :], BT[pr, t * P:(t + 1) * P],
                                    start=True, stop=True, after=(free + before) if q == 0 else ())
                        am = act(S.activation, Am[:, hf * 256:hf * 256 + 256], bank[:, 0:256], ACT.Copy, after=[mm] + before)
                        psum.give(bank, [am])
                    for dst, lhs in ((AKT, KTL), (ABT, BT)):
                        for hf in range(2):
                            bank, free = psum.take()
                            for q, (t, h) in enumerate(tiles[2 * hf:2 * hf + 2]):
                                pr = slice(h * 64, h * 64 + 64)
                                mm = pe(E.matmul, bank[:, q * 256:(q + 1) * 256], lhs[pr, t * P:(t + 1) * P],
                                        RA[pr, t, :, :], start=True, stop=True, after=free if q == 0 else ())
                            e = dve(V.tensor_tensor, dst[:, 2 * hf:2 * hf + 2, :, :],
                                    bank[:, :].rearrange("p (b m n) -> p b m n", b=2, m=2),
                                    mask2.unsqueeze(1).to_broadcast([P, 2, 2, P]), ALU.mult, after=[mm, masks_ready])
                            psum.give(bank, [e])
                    idb = ident[:, :].unsqueeze(1).to_broadcast([P, 4, P])
                    lv = lambda i: lvl[:, i, :].unsqueeze(1).to_broadcast([P, 4, P])
                    dve(V.tensor_tensor, blk(Fm), ABT[:, :, 0, :], lv(6), ALU.mult)
                    dve(V.tensor_tensor, blk(Fm), blk(Fm), idb, ALU.add)
                    dve(V.tensor_tensor, blk(Gm), blk(Am), lv(0), ALU.mult, after=[am])
                    fg = dve(V.tensor_tensor, blk(Gm), blk(Gm), idb, ALU.add)
                    al = pool(G.tensor_tensor, blk(AL), blk(Am), lv(1), ALU.mult, after=[am])
                    for i in range(1, 6):
                        yield
                        bank, free = psum.take()
                        for q in range(4):
                            sl = slice(q * P, (q + 1) * P)
                            mm = pe(E.matmul, bank[:, sl], AL[:, sl], Fm[:, sl], start=True, stop=True,
                                    after=(free + [al, fg]) if q == 0 else ())
                        ym = act(S.activation, Ym, bank[:, :], ACT.Copy, after=[mm])
                        psum.give(bank, [ym])
                        if i < 5:
                            al = pool(G.tensor_tensor, blk(AL), blk(Am), lv(i + 1), ALU.mult, after=[mm])
                        yield
                        bank, free = psum.take()
                        for q in range(4):
                            sl = slice(q * P, (q + 1) * P)
                            mm = pe(E.matmul, bank[:, sl], Gm[:, sl], Ym[:, sl], start=True, stop=True,
                                    after=(free + [ym]) if q == 0 else ())
                        bank2, free = psum.take()
                        if i < 5:
                            for q in range(4):
                                sl = slice(q * P, (q + 1) * P)
                                mm2 = pe(E.matmul, bank2[:, sl], Ym[:, sl], Gm[:, sl], start=True, stop=True,
                                         after=free if q == 0 else ())
                        fg = dve(V.tensor_tensor, Fm, Fm, bank[:, :], ALU.add, after=[mm])
                        psum.give(bank, [fg])
                        if i < 5:
                            fg = dve(V.tensor_tensor, Gm, Gm, bank2[:, :], ALU.add, after=[mm2])
                        psum.give(bank2, [fg] + list(free))
                    yield
                    bank, free = psum.take()
                    for q, (t, h) in enumerate(tiles):
                        mm = pe(E.matmul, bank[:, at(t, h):at(t, h) + 64], AKT[:, q, 0, :],
                                VN[:, t * P + h * 64:t * P + h * 64 + 64], start=True, stop=True,
                                after=(free + [fg]) if q == 0 else ())
                    x0 = act(S.activation, X0, bank[:, 0:256], ACT.Copy, after=[mm])
                    psum.give(bank, [x0])
                    yield
                    bank, free = psum.take()
                    for q, (t, h) in enumerate(tiles):
                        mm = pe(E.matmul, bank[:, at(t, h):at(t, h) + 64], Fm[:, q * P:(q + 1) * P],
                                X0[:, at(t, h):at(t, h) + 64], start=True, stop=True,
                                after=(free + [x0]) if q == 0 else ())
                    psum.give(bank, [act(S.activation, U0, bank[:, 0:256], ACT.Copy, after=[mm])])
                    bank, free = psum.take()
                    for i in range(2):
                        t = 2 * grp + i
                        for h in range(2):
                            mm = pe(E.matmul, bank[:, (2 * i + h) * P:(2 * i + h + 1) * P],
                                    AN[:, t * P:(t + 1) * P], Fm[:, (2 * h + i) * P:(2 * h + i + 1) * P],
                                    start=True, stop=True, after=free if (i, h) == (0, 0) else ())
                    bv = bank[:, :].rearrange("p (i h n) -> p i h n", i=2, h=2)
                    wtv = WT.rearrange("p (i n) -> p i n", i=2)
                    act(S.activation, wtv[0:64], bv[0:64, :, 0, :], ACT.Copy, after=[mm])
                    wt = act(S.activation, wtv[64:128], bv[64:128, :, 1, :], ACT.Copy)
                    psum.give(bank, [wt])
                    wt_ready[grp] = wt
                    yield

                def chunks(grp):
                    U0, WT, AKT, ABT = handed[grp % 2]
                    wt = wt_ready[grp]
                    for i in range(2):
                        t = 2 * grp + i
                        tc = slice(t * P, (t + 1) * P)
                        ui = UU[:, i * P:(i + 1) * P]
                        for ch in range(2):
                            yield
                            rows = slice(ch * 64, ch * 64 + 64)
                            bank, free = psum.take()
                            mm = pe(E.matmul, bank[:, 0:P], WT[:, i * P:(i + 1) * P], ST, start=True, stop=True,
                                    after=free + [wt] + st_ready)
                            ybank, free = psum.take()
                            mm2 = pe(E.matmul, ybank[:, 0:P], RA[:, t, 1, :], ST, start=True, stop=True, after=free)
                            u = dve(V.tensor_tensor, ui[rows, :], bank[rows, 0:P], U0[rows, i * P:(i + 1) * P],
                                    ALU.add, after=[mm, wt])
                            ycp = act(S.activation, YN[rows, t, :], ybank[rows, 0:P], ACT.Copy, after=[mm2])
                            psum.give(bank, [u])
                            psum.give(ybank, [ycp])
                            yield
                            bank, free = psum.take()
                            pe(E.matmul, bank[:, 0:P], KN[rows, tc], VN[rows, tc], start=True, stop=False, after=free)
                            mm = pe(E.matmul, bank[:, 0:P], BN[rows, tc], ui[rows, :], start=False, stop=True,
                                    after=[u])
                            n = 2 * t + ch
                            for h in range(2):
                                pr = slice(h * 64, h * 64 + 64)
                                s = dve(V.scalar_tensor_tensor, ST[pr, pr], ST[pr, pr], WC[pr, n:n + 1],
                                        bank[pr, pr], ALU.mult, ALU.add, after=[mm, mm2])
                            psum.give(bank, [s])
                            st_ready[:] = [s]
                        bank, free = psum.take()
                        for h in range(2):
                            hs = slice(h * 64, h * 64 + 64)
                            pe(E.matmul, bank[:, hs], ABT[:, 2 * h + i, 1, :], ui[:, hs], start=True, stop=False,
                               after=free + [u] if h == 0 else ())
                            mm = pe(E.matmul, bank[:, hs], AKT[:, 2 * h + i, 1, :], VN[:, t * P + h * 64:t * P + h * 64 + 64],
                                    start=False, stop=True)
                        psum.give(bank, [dve(V.tensor_tensor, YN[:, t, :], YN[:, t, :], bank[:, 0:P], ALU.add,
                                             after=[mm, ycp])])

                yield from factor(0)
                for grp in range(4):
                    if grp < 3:
                        yield from weave(chunks(grp), factor(grp + 1))
                    else:
                        yield from chunks(grp)
                yield
                gn = lambda b: b.rearrange("p (g n) -> p g n", n=64)
                Y2 = MIX[:, c, :]
                sm = STAT[:, 48:64]
                sv = STAT[:, 64:80]
                dve(V.tensor_reduce, sm, gn(Y2), AX.X, ALU.add)
                dve(V.tensor_scalar, sm, sm, 1.0 / 64, None, ALU.mult)
                smb = sm.unsqueeze(2).to_broadcast([P, 16, 64])
                dve(V.tensor_tensor, gn(Y2), gn(Y2), smb, ALU.subtract)
                x = act(S.activation, R, Y2, ACT.Square, after=[last(lane_dve), last(lane_pe)])
                dve(V.tensor_reduce, sv, gn(R), AX.X, ALU.add, after=[x])
                rstd_of(sv, sv, 1.0 / 64, 64e-5)
                dve(V.tensor_tensor, gn(Y2), gn(Y2), sv.unsqueeze(2).to_broadcast([P, 16, 64]), ALU.mult)
                g = dma(K[:, 0:P], T["rw_lnx_g"][0, c * P:(c + 1) * P].partition_broadcast(P), dma_misc,
                        after=both() + [last(lane_pe)])
                g = dma(K[:, P:2 * P], T["rw_lnx_b"][0, c * P:(c + 1) * P].partition_broadcast(P), dma_misc)
                dve(V.tensor_tensor, YN, YN, K[:, 0:P].unsqueeze(1).to_broadcast([P, NT, P]), ALU.mult, after=[g])
                dve(V.tensor_tensor, YN, YN, K[:, P:2 * P].unsqueeze(1).to_broadcast([P, NT, P]), ALU.add)
                dve(V.tensor_tensor, gn(R), gn(VN), BON.unsqueeze(2).to_broadcast([P, 16, 64]), ALU.mult)
                x = dve(V.tensor_tensor, Y2, Y2, R, ALU.add)
                pair_end = [x]
                yield
                for hf in range(2):
                    bank, tr = transposes([YN[:, hf * 4 + i, :] for i in range(4)], after=[x])
                    e = copy_out(MIX[:, c, hf * HALF:(hf + 1) * HALF], bank[:, :], [tr])
                    psum.give(bank, [e])
                    pair_end += [e, tr]

        def band_attention():
            w = area([("QT", 1024), ("KT", 1024), ("VN", 1024), ("BIAS", 2048), ("FAR", 384), ("S0", 640), ("S1", 640),
                      ("PT0", 640), ("PT1", 640), ("O", P)], base=H_AREA, size=8192)
            QT, KT = w["QT"], w["KT"]
            VN = w["VN"].rearrange("p (t n) -> p t n", t=NT)
            BIAS = w["BIAS"].rearrange("p (h n) -> p h n", h=8)
            src = T["att_bias_wide"]
            diag = bass.AP(tensor=src.tensor, offset=P - 1, ap=[[8 * 384 - 1, P], [384, 8], [1, 256]])
            d2 = dma(BIAS, diag, dma_misc)
            b = pool(G.memset, BIAS[0:64, :, 192:256], NEG, after=[d2])
            pool(G.memset, w["FAR"], 0.0)
            bias_ready = pool(G.memset, w["FAR"][64:128, 0:64], NEG)
            WIN = T["w_in_e"][0]
            s_ring, pt_ring = Ring([w["S0"], w["S1"]]), Ring([w["PT0"], w["PT1"]])
            stat = STAT[:, 80:112].rearrange("p (a h) -> p a h", a=4)
            o_free, qkv_free = [], []
            for c in range(4):
              slot, wv, ws = load_w([(WIN, 2176 + g * HALF + c * P, P) for g in range(3)], KD)
              for g, dst, scale in ((0, QT, 0.125), (1, KT, 1.0)):
                  yield from product_T_pieces(wv, ws, XT, KD, g * P, lambda b, half, mm: act(
                      S.activation, dst[:, half * HALF:(half + 1) * HALF], b[:, :], ACT.Copy, scale=scale,
                      after=[mm] + qkv_free))
              for t in range(NT):
                  product_N(wv, ws, XT, KD, t, lambda b, mm, t=t: copy_out(VN[:, t, :], b[:, 0:P], [mm]), n=P, c0=2 * P)
                  if t % 4 == 3:
                      yield
              done_w(slot)
              qkv_ready = both()
              for i in range(NT):
                obank, ofree = psum.take()
                for h in (2 * c, 2 * c + 1):
                    hl = h - 2 * c
                    pr = slice(64 * hl, 64 * hl + 64)
                    near, far = min(i, 1) + 1, max(min(i, 4) - 1, 0)
                    nk = near + far
                    k0 = i + 1 - nk
                    Sb, sfree = s_ring.take()
                    q = QT[pr, i * P:(i + 1) * P]
                    if far:
                        bank, free = psum.take()
                        mm = pe(E.matmul, bank[:, 0:far * P], q, KT[pr, k0 * P:(k0 + far) * P], start=True,
                                stop=True, after=free + qkv_ready)
                        off = (3 - far) * P
                        e = dve(V.scalar_tensor_tensor, Sb[:, 0:far * P], bank[:, 0:far * P],
                                PAR[:, bias_far_at + h:bias_far_at + h + 1], w["FAR"][:, off:off + far * P]
                                if far == 3 else w["FAR"][:, P:P + far * P], ALU.add, ALU.add,
                                after=[mm, bias_ready, par_ready] + sfree)
                        psum.give(bank, [e])
                    bank, free = psum.take()
                    mm = pe(E.matmul, bank[:, 0:near * P], q, KT[pr, (k0 + far) * P:(i + 1) * P], start=True,
                            stop=True, after=free + qkv_ready)
                    e = dve(V.tensor_tensor, Sb[:, far * P:nk * P], bank[:, 0:near * P],
                            BIAS[:, h, (2 - near) * P:256], ALU.add, after=[mm, bias_ready] + sfree)
                    psum.give(bank, [e])
                    x = dve(V.tensor_reduce, stat[:, 0, h:h + 1], Sb[:, 0:nk * P], AX.X, ALU.max, negate=True)
                    x = act(S.activation, Sb[:, 0:nk * P], Sb[:, 0:nk * P], ACT.Exp, bias=stat[:, 0, h:h + 1],
                            accum_out=stat[:, 1, h:h + 1], after=[x])
                    yield
                    PT, pfree = pt_ring.take()
                    for a0 in range(0, nk, 4):
                        n = min(4, nk - a0)
                        bank, tr = transposes([Sb[:, (a0 + j) * P:(a0 + j + 1) * P] for j in range(n)], after=[x])
                        e = copy_out(PT[:, a0 * P:(a0 + n) * P], bank[:, 0:n * P], [tr] + pfree)
                        psum.give(bank, [e])
                        es = both()
                    s_ring.give(Sb, [tr])
                    yield
                    for j in range(nk):
                        mm = pe(E.matmul, obank[:, hl * 64:(hl + 1) * 64], PT[:, j * P:(j + 1) * P],
                                VN[:, k0 + j, hl * 64:(hl + 1) * 64], start=j == 0, stop=j == nk - 1,
                                after=(es + (ofree if hl == 0 else [])) if j == 0 else ())
                    pt_ring.give(PT, [mm])
                hs = slice(2 * c, 2 * c + 2)
                dve(V.reciprocal, stat[:, 2, hs], stat[:, 1, hs], after=[x])
                x = dve(V.tensor_tensor, w["O"].rearrange("p (h n) -> p h n", h=2),
                        obank[:, 0:P].rearrange("p (h n) -> p h n", h=2),
                        stat[:, 2, hs].unsqueeze(2).to_broadcast([P, 2, 64]), ALU.mult, after=[mm] + o_free)
                psum.give(obank, [x])
                yield
                bank, tr = transposes([w["O"]], after=[x])
                o_free = [tr]
                e = copy_out(MIX[:, 4 + c, i * P:(i + 1) * P], bank[:, 0:P], [tr])
                psum.give(bank, [e])
              qkv_free = [mm, tr, e]
            yield from gate_T_pieces(T["w_in_e"][0], 3712, lambda ct: MIX[:, 4 + ct, :], ACT.Silu, after=both(),
                                     width=3 * P)

        def odd_layer():
            w = area([("VN", 8192), ("SGW", 1024), ("SGT", 1024), ("SGB", 1024)])
            w["grow"], w["brow"] = N_AREA["grow"], N_AREA["brow"]
            sgw = dma(w["SGW"].rearrange("p (g j) -> p g j", g=8), T["sg_w"][0].rearrange("g i j -> i g j"), dma_misc)
            sgw = dma(w["SGB"], T["sg_b"][0].rearrange("g i -> (g i)").partition_broadcast(P), dma_misc)
            sgw = dma(w["grow"], T["sg_ln_g"][0].partition_broadcast(P), dma_misc)
            sgw = dma(w["brow"], T["sg_ln_b"][0].partition_broadcast(P), dma_misc)
            for hf in range(2):
                bank, tr = transposes([w["SGW"][:, (hf * 4 + i) * P:(hf * 4 + i + 1) * P] for i in range(4)], after=[sgw])
                psum.give(bank, [copy_out(w["SGT"][:, hf * HALF:(hf + 1) * HALF], bank[:, :], [tr])])
            sgt = w["SGT"].rearrange("p (g i) -> p g i", g=8)
            sgt_ready = pool(G.memset, sgt[64:128, :, 0:64], 0.0, after=both())
            WIN = T["w_in_o"][0]
            VN = w["VN"].rearrange("p (t n) -> p t n", t=NT)

            def values():
                for c0 in (0, HALF):
                    slot, wv, ws = load_w([(WIN, D + c0, HALF)], KD)
                    for t in range(NT):
                        product_N(wv, ws, XT, KD, t, lambda b, mm: act(
                            S.activation, VN[:, t, c0:c0 + HALF], b[:, :], ACT.Gelu_apprx_tanh, after=[mm]))
                        yield (t, last(lane_act)) if c0 else None
                    done_w(slot)

            def mixed(t, ready):
                dve(V.bn_stats, BST[:, 0:6], VN[:, t, 0:HALF], after=[ready])
                dve(V.bn_stats, BST[:, 6:12], VN[:, t, HALF:D])
                dve(V.bn_aggr, MV[:, t, :], BST)
                b = scale_shift(VN[:, t, :], t, sgw)
                yield
                for hf in range(2):
                    bank, free = psum.take()
                    for g in range(4):
                        gg = hf * 4 + g
                        mm = pe(E.matmul, bank[:, g * P:(g + 1) * P], VN[:, t, gg * P:(gg + 1) * P], sgt[:, gg, :],
                                start=True, stop=True, after=(free + [b, sgt_ready]) if g == 0 else ())
                    e = dve(V.tensor_tensor, MIX[:, hf * 4:hf * 4 + 4, t * P:(t + 1) * P],
                            bank[:, :].rearrange("p (c n) -> p c n", c=4),
                            w["SGB"][:, hf * HALF:(hf + 1) * HALF].rearrange("p (c n) -> p c n", c=4), ALU.add,
                            after=[mm])
                    psum.give(bank, [e])
                yield

            follow(values(), mixed)
            for base, func in ((0, ACT.Gelu_apprx_tanh), (2 * D, ACT.Silu)):
                for c0 in (0, HALF):
                    gate_T(WIN, base + c0, lambda ct: MIX[:, c0 // P + ct, :], func, after=[last(lane_dve)])
            row = load_row("row2", "final_g", after=[last(lane_dve), last(lane_act)])
            follow(projected_out(T["w_out_o"][0], MIX, KD, [last(lane_pool)], add_to_H),
                   final_rms_tile(row, rms_tile("norm_g_2")))
            if 2 in BLOCKS:
                load_early([(T["w_in_2"][0], 0, HALF)], KD)
            boundary()

        Z2 = T["w_in_2"][0]
        AQ, AK, AV, AG, BG1, BG2, BG, CQ, CK, CV, CG, MG = (0, 512, 640, 768, 1280, 1792, 2304, 2816, 3328, 3840, 4352,
                                                            4864)

        def head_norm_evac(dst, bank, mm, gname, scale, tmp):
            (raw, sq), free = tmp.take()
            a = act(S.activation, raw, bank[:, :], ACT.Copy, after=[mm] + free)
            a = act(S.activation, sq, raw, ACT.Square, after=[a])
            b2, free = psum.take()
            m2 = pe(E.matmul, b2[:, :], head_ones[:, :], sq, start=True, stop=True, after=free + [a, consts_ready])
            d = dve(V.tensor_scalar, sq, b2[:, :], 1.0 / (64 * scale * scale), 1e-6 / (scale * scale), ALU.mult,
                    ALU.add, after=[m2])
            psum.give(b2, [d])
            a = act(S.activation, sq, sq, ACT.Sqrt, after=[d])
            d = dve(V.reciprocal, sq, sq, after=[a])
            d = dve(V.scalar_tensor_tensor, dst, raw, col(gname, 0), sq, ALU.mult, ALU.mult)
            tmp.give((raw, sq), [d])
            return a

        def merge(branch, w_o, Y, after):
            for c0 in (0, HALF):
                slot, wv, ws = load_w([(w_o, c0, HALF)], 4)
                slot2, wv2, ws2 = load_w([(Z2, MG + branch * D + c0, HALF)], KD)
                for ct in range(4):
                    mt = c0 // P + ct
                    held = {}

                    def evac_gate(bank, half, mm):
                        g, free = gate_tmp.take()
                        a = act(S.activation, g, bank[:, :], ACT.Sigmoid, after=[mm] + free)
                        held[half] = (g, a)
                        return a

                    def evac_y(bank, half, mm):
                        g, a = held[half]
                        dst = MIX[:, mt, half * HALF:(half + 1) * HALF]
                        if branch == 0:
                            d = dve(V.tensor_tensor, dst, g, bank[:, :], ALU.mult, after=[mm, a])
                            gate_tmp.give(g, [d])
                            return d
                        d = dve(V.tensor_tensor, g, g, bank[:, :], ALU.mult, after=[mm, a])
                        m = pool(G.tensor_tensor, dst, dst, g, ALU.add, after=[d])
                        gate_tmp.give(g, [m])
                        return d

                    yield from product_T_pieces(wv2, ws2, XT, KD, ct * P, evac_gate)
                    yield from product_T_pieces(wv, ws, Y, 4, ct * P, evac_y, after=after)
                done_w(slot)
                done_w(slot2)

        def window_attention():
            w = area([("KT", 2048), ("VN", 1024), ("MW", 256),
                      ("S0", 512), ("S1", 512), ("PT0", 512), ("PT1", 512), ("O0", 512), ("O1", 512)],
                     base=H_AREA, size=8192)
            QT = WORK[:, 0:4096].rearrange("p (c n) -> p c n", c=4)
            KT = w["KT"].rearrange("p (c n) -> p c n", c=2)
            VN = w["VN"].rearrange("p (t n) -> p t n", t=NT)
            Y = QT
            tmp = Ring([(w["S0"], w["S1"]), (w["PT0"], w["PT1"])])
            MW = w["MW"]
            pool(G.memset, MW, 0.0)
            pool(G.affine_select, out=MW, in_=MW, compare_op=ALU.is_ge, fill=NEG, base=P, pattern=[[-1, 256]],
                 channel_multiplier=1)
            mask = pool(G.affine_select, out=MW, in_=MW, compare_op=ALU.is_ge, fill=NEG, base=-1, pattern=[[1, 256]],
                        channel_multiplier=-1)
            slot, wv, ws = load_w([(Z2, AQ, HALF)], KD)
            for ct in range(4):
                yield from product_T_pieces(wv, ws, XT, KD, ct * P, lambda b, half, mm, ct=ct: head_norm_evac(
                    QT[:, ct, half * HALF:(half + 1) * HALF], b, mm, "attn_q_norm_g_2", 0.125, tmp))
            done_w(slot)
            slot, wv, ws = load_w([(Z2, AK, 64), (Z2, AK, 64), (Z2, AK + 64, 64), (Z2, AK + 64, 64), (Z2, AV, P)], KD)
            for kv in range(2):
                yield from product_T_pieces(wv, ws, XT, KD, kv * P, lambda b, half, mm, kv=kv: head_norm_evac(
                    KT[:, kv, half * HALF:(half + 1) * HALF], b, mm, "attn_k_norm_g_2", 1.0, tmp))
            for t in range(NT):
                product_N(wv, ws, XT, KD, t, lambda b, mm, t=t: copy_out(VN[:, t, :], b[:, 0:P], [mm]), n=P, c0=256)
            done_w(slot)
            ready = both()
            sinks = PAR[:, par_at["sinks"]:par_at["sinks"] + 8]

            def stream(tiles, k):
              Sb, PT, O = w[f"S{k}"], w[f"PT{k}"], w[f"O{k}"]
              st = STAT[:, 48 + 48 * k:96 + 48 * k].rearrange("p (a h) -> p a h", a=6)
              sfree, pfree, o_free = [], [], []
              for i in tiles:
                obank, ofree = psum.take()
                nk = min(i, 1) + 1
                n = nk * P
                for hp in range(4):
                    yield
                    S2 = Sb.rearrange("p (h n) -> p h n", h=2)
                    for h in range(2):
                        pr = slice(64 * h, 64 * h + 64)
                        bank, free = psum.take()
                        mm = pe(E.matmul, bank[:, 0:n], QT[pr, hp, i * P:(i + 1) * P],
                                KT[pr, hp // 2, (i + 1 - nk) * P:(i + 1) * P], start=True, stop=True,
                                after=free + ready)
                        e = dve(V.tensor_tensor, S2[:, h, 0:n], bank[:, 0:n], MW[:, 256 - n:256], ALU.add,
                                after=[mm, mask] + sfree)
                        psum.give(bank, [e])
                    hs = slice(2 * hp, 2 * hp + 2)
                    dve(V.tensor_reduce, st[:, 0, hs], S2[:, :, 0:n], AX.X, ALU.max)
                    dve(V.tensor_tensor, st[:, 0, hs], st[:, 0, hs], sinks[:, hs], ALU.max, after=[par_ready])
                    x = dve(V.tensor_scalar, st[:, 1, hs], st[:, 0, hs], -1.0, None, ALU.mult)
                    for h in range(2):
                        hh = 2 * hp + h
                        e = act(S.activation, S2[:, h, 0:n], S2[:, h, 0:n], ACT.Exp, bias=st[:, 1, hh:hh + 1],
                                accum_out=st[:, 2, hh:hh + 1], after=[x])
                    yield
                    bank, tr = transposes([S2[:, h, j * P:(j + 1) * P] for h in range(2) for j in range(nk)], after=[e])
                    cp = copy_out(PT[:, 0:2 * n], bank[:, 0:2 * n], [tr] + pfree)
                    psum.give(bank, [cp])
                    sfree = [tr]
                    yield
                    for h in range(2):
                        hh = 2 * hp + h
                        for j in range(nk):
                            mm = pe(E.matmul, obank[:, hh * 64:(hh + 1) * 64], PT[:, (h * nk + j) * P:(h * nk + j + 1) * P],
                                    VN[:, i + 1 - nk + j, (hp // 2) * 64:(hp // 2) * 64 + 64], start=j == 0,
                                    stop=j == nk - 1, after=([cp] + ofree) if j == 0 else ())
                    pfree = [mm]
                d = dve(V.tensor_tensor, st[:, 3, :], sinks, st[:, 0, :], ALU.subtract)
                a = act(S.activation, st[:, 4, :], st[:, 3, :], ACT.Exp, after=[d])
                dve(V.tensor_tensor, st[:, 4, :], st[:, 4, :], st[:, 2, :], ALU.add, after=[a])
                dve(V.reciprocal, st[:, 4, :], st[:, 4, :])
                x = dve(V.tensor_tensor, O.rearrange("p (h n) -> p h n", h=8),
                        obank[:, :].rearrange("p (h n) -> p h n", h=8),
                        st[:, 4, :].unsqueeze(2).to_broadcast([P, 8, 64]), ALU.mult, after=[mm] + o_free)
                psum.give(obank, [x])
                bank, tr = transposes([O[:, j * P:(j + 1) * P] for j in range(4)], after=[x])
                o_free = [tr]
                psum.give(bank, [copy_out(Y[:, :, i * P:(i + 1) * P], bank[:, :].rearrange("p (c n) -> p c n", c=4),
                                          [tr])])

            yield from weave(stream([7, 5, 3, 1], 0), stream([6, 4, 2, 0], 1))

        def conformer():
            W0 = 1056
            w = area([("ACC", 4096), ("U", 4 * W0), ("t0", 512), ("t1", 512), ("SQ", 2048), ("MU", 1024),
                      ("RSD", 1024)], start=4096)
            U = w["U"].rearrange("p (c n) -> p c n", c=4)
            ACC = w["ACC"].rearrange("p (c n) -> p c n", c=4)
            Y = ACC
            pad = dve(V.memset, U[:, :, 0:30], 0.0)
            sg = Ring([w["t0"], w["t1"]])
            for ct in range(4):
                if ct % 2 == 0:
                    slot, wv, ws = load_w([(Z2, BG1 + ct * P, 2 * P), (Z2, BG2 + ct * P, 2 * P)], KD)
                held = {}

                def evac_b(bank, half, mm):
                    g, free = sg.take()
                    a = act(S.activation, g, bank[:, :], ACT.Sigmoid, after=[mm] + free)
                    held[half] = (g, a)
                    return a

                def evac_a(bank, half, mm):
                    g, a = held[half]
                    d = dve(V.tensor_tensor, U[:, ct, 30 + half * HALF:30 + (half + 1) * HALF], g, bank[:, :],
                            ALU.mult, after=[mm, a])
                    sg.give(g, [d])
                    return d

                product_T(wv, ws, XT, KD, (2 + ct % 2) * P, evac_b)
                product_T(wv, ws, XT, KD, (ct % 2) * P, evac_a)
                if ct % 2:
                    done_w(slot)
            u_ready = last(lane_dve)
            taps = lambda j: col("conv_w_2", 3 * 31 + j)
            pool(G.tensor_scalar, ACC[:, 3, :], U[:, 3, 0:SEQ], taps(0), col("conv_b_2", 3), ALU.mult, ALU.add,
                 after=[u_ready])
            for j in range(1, 31):
                pool(G.tensor_scalar, GTMP[:, 0:SEQ], U[:, 3, j:j + SEQ], taps(j), None, ALU.mult)
                conv3 = pool(G.tensor_tensor, ACC[:, 3, :], ACC[:, 3, :], GTMP[:, 0:SEQ], ALU.add)
            for ct in range(3):
                tap = lambda j: col("conv_w_2", ct * 31 + j)
                dve(V.tensor_scalar, ACC[:, ct, :], U[:, ct, 0:SEQ], tap(0), col("conv_b_2", ct), ALU.mult, ALU.add)
                for j in range(1, 31):
                    if j % 3 == 0:
                        yield
                    dve(V.scalar_tensor_tensor, ACC[:, ct, :], U[:, ct, j:j + SEQ], tap(j), ACC[:, ct, :], ALU.mult,
                        ALU.add)
            on = dve(V.memset, w["t0"][:, 0:P], 1.0)
            ones = w["t0"][:, 0:P]
            MU, RSD = w["MU"], w["RSD"]
            for half in range(2):
                yield
                sl = slice(half * HALF, (half + 1) * HALF)
                SQ = w["SQ"].rearrange("p (c n) -> p c n", c=4)
                bank, free = psum.take()
                for ct in range(4):
                    mm = pe(E.matmul, bank[:, :], ones, ACC[:, ct, sl], start=ct == 0, stop=ct == 3,
                            after=(free + [on, conv3]) if ct == 0 else ())
                d = dve(V.tensor_scalar, MU[:, sl], bank[:, :], 1.0 / 512, None, ALU.mult, after=[mm])
                psum.give(bank, [d])
                d = dve(V.tensor_tensor, ACC[:, :, sl], ACC[:, :, sl], MU[:, sl].unsqueeze(1).to_broadcast([P, 4, HALF]),
                        ALU.subtract)
                a = act(S.activation, SQ, ACC[:, :, sl], ACT.Square, after=[d, last(lane_pe)])
                bank, free = psum.take()
                for ct in range(4):
                    mm = pe(E.matmul, bank[:, :], ones, SQ[:, ct, :], start=ct == 0, stop=ct == 3,
                            after=(free + [a]) if ct == 0 else ())
                d = dve(V.tensor_scalar, RSD[:, sl], bank[:, :], 1.0 / 512, 1e-6, ALU.mult, ALU.add, after=[mm])
                psum.give(bank, [d])
                a = act(S.activation, RSD[:, sl], RSD[:, sl], ACT.Sqrt, after=[d])
                dve(V.reciprocal, RSD[:, sl], RSD[:, sl], after=[a])
                d = dve(V.tensor_tensor, ACC[:, :, sl], ACC[:, :, sl], RSD[:, sl].unsqueeze(1).to_broadcast([P, 4, HALF]),
                        ALU.mult)
            for ct in range(4):
                a = act(S.activation, Y[:, ct, :], ACC[:, ct, :], ACT.Silu, scale=col("conv_norm_g_2", ct),
                        bias=col("conv_norm_b_2", ct), after=[d])

        def causal_mask(dst, fill_kept, fill_masked, strict):
            pool(G.memset, dst, fill_kept)
            return pool(G.affine_select, out=dst, in_=dst, compare_op=ALU.is_ge, fill=fill_masked,
                        base=-1 if strict else 0, pattern=[[-1, P]], channel_multiplier=1)

        def differential():
            w = area([("VN", 4096), ("MC", P), ("L", 384), ("t0", 512), ("t1", 512), ("P0", 1024), ("P1", 1024),
                      ("PT", 1024), ("O", 512)], start=8192)
            QT = H_AREA[:, 0:4096].rearrange("p (c n) -> p c n", c=4)
            KT = H_AREA[:, 4096:8192].rearrange("p (c n) -> p c n", c=4)
            VN = w["VN"].rearrange("p (t n) -> p t n", t=NT)
            tmp = Ring([(w["t0"], w["t1"])])
            mask = causal_mask(w["MC"], 0.0, NEG, False)
            lam_init = 0.8 - 0.6 * math.exp(-0.3 * 0)
            L = w["L"]
            lq = PAR[:, par_at["lq"]:par_at["lq"] + P]
            lk = PAR[:, par_at["lk"]:par_at["lk"] + P]
            d = dve(V.tensor_tensor, L[:, 0:P], lq, lk, ALU.mult, after=[par_ready])
            d = dve(V.tensor_reduce, L[:, P:P + 2], L[:, 0:P].rearrange("p (a n) -> p a n", a=2), AX.X, ALU.add)
            a = act(S.activation, L[:, P:P + 2], L[:, P:P + 2], ACT.Exp, after=[d])
            d = dve(V.tensor_tensor, L[:, 130:131], L[:, 129:130], L[:, 128:129], ALU.subtract, after=[a])
            d = dve(V.tensor_scalar, L[:, 130:131], L[:, 130:131], lam_init, None, ALU.subtract)
            neg_lam = L[:, 130:131]
            for c0, dst, gn, sc in ((CQ, QT, "diff_q_norm_g_2", 0.125), (CK, KT, "diff_k_norm_g_2", 1.0)):
                slot, wv, ws = load_w([(Z2, c0, HALF)], KD)
                for ct in range(4):
                    product_T(wv, ws, XT, KD, ct * P, lambda b, half, mm, ct=ct: head_norm_evac(
                        dst[:, ct, half * HALF:(half + 1) * HALF], b, mm, gn, sc, tmp))
                done_w(slot)
            slot, wv, ws = load_w([(Z2, CV, HALF)], KD)
            for t in range(NT):
                product_N(wv, ws, XT, KD, t, lambda b, mm, t=t: copy_out(VN[:, t, :], b[:, :], [mm]))
            done_w(slot)
            ready = both()
            yield "projected"
            st = STAT[:, 48:112].rearrange("p (a n) -> p a n", a=8)
            PP = [w["P0"], w["P1"]]
            PT = w["PT"]
            pt_free, pp_free = [], []
            for i in range(NT):
                obank, ofree = psum.take()
                n = (i + 1) * P
                for h in range(4):
                    yield
                    for c in range(2):
                        pr = slice(64 * c, 64 * c + 64)
                        q = QT[pr, h, i * P:(i + 1) * P]
                        parts = []
                        for k0 in range(0, n, HALF):
                            kn = min(HALF, n - k0)
                            bank, free = psum.take()
                            mm = pe(E.matmul, bank[:, 0:kn], q, KT[pr, h, k0:k0 + kn], start=True, stop=True,
                                    after=free + ready)
                            parts.append((bank, k0, kn, mm))
                        bank, k0, kn, mm = parts[-1]
                        dve(V.tensor_tensor, bank[:, kn - P:kn], bank[:, kn - P:kn], w["MC"], ALU.add,
                            after=[mm, mask])
                        for j, (bank, k0, kn, mm) in enumerate(parts):
                            d = dve(V.tensor_reduce, st[:, 0, j:j + 1], bank[:, 0:kn], AX.X, ALU.max, negate=True,
                                    after=[mm])
                        if len(parts) == 2:
                            d = dve(V.tensor_tensor, st[:, 0, 0:1], st[:, 0, 0:1], st[:, 0, 1:2], ALU.min)
                        for j, (bank, k0, kn, mm) in enumerate(parts):
                            a = act(S.activation, PP[c][:, k0:k0 + kn], bank[:, 0:kn], ACT.Exp, bias=st[:, 0, 0:1],
                                    accum_out=st[:, 1 + c, j:j + 1], after=[d] + pp_free)
                            psum.give(bank, [a])
                        if len(parts) == 2:
                            dve(V.tensor_tensor, st[:, 1 + c, 0:1], st[:, 1 + c, 0:1], st[:, 1 + c, 1:2], ALU.add,
                                after=[a])
                        dve(V.reciprocal, st[:, 3 + c, h:h + 1], st[:, 1 + c, 0:1], after=[a])
                    x = dve(V.tensor_scalar, st[:, 5, 0:1], st[:, 4, h:h + 1], st[:, 1, 0:1], neg_lam, ALU.mult, ALU.mult)
                    x = dve(V.scalar_tensor_tensor, PP[0][:, 0:n], PP[1][:, 0:n], st[:, 5, 0:1], PP[0][:, 0:n],
                            ALU.mult, ALU.add)
                    yield
                    for a0 in range(0, i + 1, 4):
                        m = min(4, i + 1 - a0)
                        bank, tr = transposes([PP[0][:, (a0 + j) * P:(a0 + j + 1) * P] for j in range(m)], after=[x])
                        e = copy_out(PT[:, a0 * P:(a0 + m) * P], bank[:, 0:m * P], [tr] + pt_free)
                        psum.give(bank, [e])
                    pp_free = [tr]
                    es = both()
                    yield
                    for j in range(i + 1):
                        mm = pe(E.matmul, obank[:, h * P:(h + 1) * P], PT[:, j * P:(j + 1) * P],
                                VN[:, j, h * P:(h + 1) * P], start=j == 0, stop=j == i,
                                after=(es + ofree) if j == 0 else ())
                    pt_free = [mm]
                O = w["O"].rearrange("p (h n) -> p h n", h=4)
                x = dve(V.tensor_tensor, O, obank[:, :].rearrange("p (h n) -> p h n", h=4),
                        st[:, 3, 0:4].unsqueeze(2).to_broadcast([P, 4, P]), ALU.mult, after=[mm, last(lane_pe)])
                psum.give(obank, [x])
                a = act(S.activation, w["t0"], w["O"], ACT.Square, after=[x])
                x = dve(V.tensor_reduce, st[:, 6, 0:4], w["t0"].rearrange("p (h n) -> p h n", h=4), AX.X, ALU.add,
                        after=[a])
                keep = 1.0 - lam_init
                x = rstd_of(st[:, 6, 0:4], st[:, 6, 0:4], 1.0 / (P * keep * keep), 1e-6 / (keep * keep))
                x = dve(V.tensor_tensor, O, O, st[:, 6, 0:4].unsqueeze(2).to_broadcast([P, 4, P]), ALU.mult)
                bank, tr = transposes([w["O"][:, j * P:(j + 1) * P] for j in range(4)], after=[x])
                e = dve(V.tensor_scalar, QT[:, :, i * P:(i + 1) * P], bank[:, :].rearrange("p (c n) -> p c n", c=4),
                        col("diff_subln_g_2", 0), None, ALU.mult, after=[tr])
                psum.give(bank, [e])


        ALPHA = float(2 ** 0.25)

        def residual_evac(bank, t, c0, mm, n=HALF):
            return dve(V.scalar_tensor_tensor, H[:, t, c0:c0 + n], H[:, t, c0:c0 + n], ALPHA, bank[:, 0:n],
                       ALU.mult, ALU.add, after=[mm])

        def stick_and_pool():
            U0 = 1040
            w = area([("QT", 4096), ("KT", 4096), ("U", 4 * U0), ("S", U0), ("S2", U0), ("CNT", 64), ("WP", 512),
                      ("MN", P), ("ONE", 1), ("O0", 512), ("O1", 512), ("T0", 512), ("T1", 512)])
            QT = w["QT"].rearrange("p (c n) -> p c n", c=4)
            KT = w["KT"].rearrange("p (c n) -> p c n", c=4)
            U = w["U"].rearrange("p (c n) -> p c n", c=4)
            CNT = w["CNT"].rearrange("p (g n) -> p g n", g=4)
            VN = w["U"][:, 0:4096].rearrange("p (t n) -> p t n", t=NT)
            causal_mask(w["MN"], 0.0, NEG, True)
            pool(G.memset, w["ONE"], 1.0)
            for b in (U, w["S"].unsqueeze(1), w["S2"].unsqueeze(1)):
                pad = pool(G.memset, b[:, :, 0:16], 0.0)
            for g in range(4):
                win = 2 << g
                pool(G.memset, CNT[:, g, :], 1.0)
                for t in range(win - 1):
                    pool(G.memset, CNT[:, g, t:t + 1], float(np.float32(win / (t + 1))))
            consts = last(lane_pool)
            wp = dma(w["WP"].rearrange("p (g d) -> p g d", g=4), T["w_pool_3"][0].rearrange("g c d -> c g d"), dma_misc)
            WIN = T["w_in_3"][0]
            slot, wv, ws = load_w([(WIN, 1536, HALF)], KD)
            for ct in range(4):
                product_T(wv, ws, XT, KD, ct * P, lambda b, half, mm, ct=ct: act(
                    S.activation, U[:, ct, 16 + half * HALF:16 + (half + 1) * HALF], b[:, :], ACT.Copy,
                    after=[mm, pad]))
            done_w(slot)
            u_ready = last(lane_act)

            def pooled():
                for g in range(4):
                    cur = U[:, g, :]
                    for lvl in range(g + 1):
                        sh = 1 << lvl
                        nxt = (w["S"], w["S2"])[lvl % 2]
                        d = dve(V.tensor_tensor, nxt[:, 16:16 + SEQ], cur[:, 16:16 + SEQ],
                                cur[:, 16 - sh:16 - sh + SEQ], ALU.add, after=[u_ready, consts, last(lane_pe)])
                        cur = nxt
                    dst = (w["S"], w["S2"])[(g + 1) % 2][:, 16:16 + SEQ]
                    dve(V.tensor_scalar, dst, cur[:, 16:16 + SEQ], 1.0 / (2 << g), None, ALU.mult)
                    dve(V.tensor_tensor, dst[:, 0:16], dst[:, 0:16], CNT[:, g, :], ALU.mult)
                    d = dve(V.tensor_tensor, dst, dst, U[:, g, 16:16 + SEQ], ALU.subtract)
                    yield
                    for half in range(2):
                        bank, free = psum.take()
                        mm = pe(E.matmul, bank[:, :], w["WP"][:, g * P:(g + 1) * P],
                                dst[:, half * HALF:(half + 1) * HALF], start=True, stop=True, after=free + [d, wp])
                        psum.give(bank, [act(S.activation, MIX[:, 4 + g, half * HALF:(half + 1) * HALF], bank[:, :],
                                             ACT.Copy, scale=col("pool_scale_3", g), after=[mm])])

            def queries_keys():
                for c0, dst, scale in ((0, QT, 0.125), (512, KT, 1.0)):
                    slot, wv, ws = load_w([(WIN, c0, HALF)], KD)
                    for ct in range(4):
                        product_T(wv, ws, XT, KD, ct * P, lambda b, half, mm, ct=ct: act(
                            S.activation, dst[:, ct, half * HALF:(half + 1) * HALF], b[:, :], ACT.Copy, scale=scale,
                            after=[mm]))
                        yield
                    done_w(slot)

            run(weave(queries_keys(), pooled()))
            slot, wv, ws = load_w([(WIN, 1024, HALF)], KD)
            u_done = both()
            for t in range(NT):
                product_N(wv, ws, XT, KD, t, lambda b, mm, t=t: copy_out(VN[:, t, :], b[:, :], [mm] + u_done))
            done_w(slot)
            ready = both() + [last(lane_pe)]
            XF = XT[:, :, :].rearrange("p c n -> p (c n)")

            def stream(tiles, k):
                base = k * 3080
                A, C, B = XF[:, base:base + 1024], XF[:, base + 1024:base + 2049], XF[:, base + 2056:base + 3080]
                PT, O, TT = B, w[f"O{k}"], w[f"T{k}"]
                st = STAT[:, 48 + 8 * k:56 + 8 * k]
                pt_free, a_free = [], []
                for i in tiles:
                    obank, ofree = psum.take()
                    n = (i + 1) * P
                    for h in range(8):
                        pr, ct = slice(64 * (h % 2), 64 * (h % 2) + 64), h // 2
                        q = QT[pr, ct, i * P:(i + 1) * P]
                        parts = []
                        for k0 in range(0, n, HALF):
                            kn = min(HALF, n - k0)
                            bank, free = psum.take()
                            mm = pe(E.matmul, bank[:, 0:kn], q, KT[pr, ct, k0:k0 + kn], start=True, stop=True,
                                    after=free + ready)
                            parts.append((bank, k0, kn, mm))
                        bank, k0, kn, mm = parts[-1]
                        d = dve(V.tensor_tensor, bank[:, kn - P:kn], bank[:, kn - P:kn], w["MN"], ALU.add,
                                after=[mm, consts])
                        for bank, k0, kn, mm in parts:
                            act(S.activation, B[:, k0:k0 + kn], bank[:, 0:kn], ACT.Sigmoid, scale=-1.0,
                                after=[d] + pt_free)
                            a = act(S.activation, A[:, k0:k0 + kn], bank[:, 0:kn], ACT.Sigmoid, after=a_free)
                            psum.give(bank, [a])
                        dve(V.memset, C[:, n:n + 1], 1.0, after=a_free)
                        c = dve(V.tensor_tensor_scan, C[:, 0:n][:, ::-1], B[:, 0:n][:, ::-1],
                                w["ONE"].to_broadcast([P, n]), 1.0, ALU.mult, ALU.mult, after=[a])
                        x = dve(V.tensor_tensor, A[:, 0:n], A[:, 0:n], C[:, 1:n + 1], ALU.mult)
                        yield
                        es = []
                        for a0 in range(0, i + 1, 4):
                            m = min(4, i + 1 - a0)
                            bank, tr = transposes([A[:, (a0 + j) * P:(a0 + j + 1) * P] for j in range(m)], after=[x])
                            e = copy_out(PT[:, a0 * P:(a0 + m) * P], bank[:, 0:m * P], [tr, c])
                            psum.give(bank, [e])
                            es.append(e)
                        a_free = [tr]
                        yield
                        for j in range(i + 1):
                            mm = pe(E.matmul, obank[:, h * 64:(h + 1) * 64], PT[:, j * P:(j + 1) * P],
                                    VN[:, j, h * 64:(h + 1) * 64], start=j == 0, stop=j == i,
                                    after=(es + ofree) if j == 0 else ())
                        pt_free = [mm]
                    O3 = O.rearrange("p (h n) -> p h n", h=8)
                    a = act(S.activation, O, obank[:, :], ACT.Copy, after=[mm])
                    psum.give(obank, [a])
                    dve(V.tensor_tensor, TT, O, O, ALU.mult, after=[a])
                    dve(V.tensor_reduce, st, TT.rearrange("p (h n) -> p h n", h=8), AX.X, ALU.add)
                    rstd_of(st, st, 1.0 / 64, 1e-6)
                    x = dve(V.tensor_tensor, O3, O3, st.unsqueeze(2).to_broadcast([P, 8, 64]), ALU.mult)
                    yield
                    bank, tr = transposes([O[:, j * P:(j + 1) * P] for j in range(4)], after=[x])
                    e = dve(V.tensor_tensor, MIX[:, 0:4, i * P:(i + 1) * P],
                            bank[:, :].rearrange("p (c n) -> p c n", c=4), cols("attn_out_g_3", 0, 4, P), ALU.mult,
                            after=[tr])
                    psum.give(bank, [e])

            run(weave(stream([7, 4, 3, 0], 0), stream([6, 5, 2, 1], 1)))

        def out_projection():
            Q = 2 * P
            views = [WS[0][:, 2048 * i:2048 * (i + 1)].rearrange("p (k n) -> p k n", k=KD) for i in range(2)]
            free = [[], []]

            def load(quarter):
                return dma(views[quarter % 2], T["w_out_3"][0].rearrange("(k p) n -> p k n", p=P)
                           [:, :, quarter * Q:(quarter + 1) * Q], stage_lane[quarter % 2], after=free[quarter % 2])

            def products(quarter, t, loaded):
                product_N(views[quarter % 2], loaded, MIX, KD, t, lambda b, mm: residual_evac(
                    b, t, quarter * Q, mm, Q), n=Q)

            first = [load(0), load(1)]
            for quarter in range(2):
                for t in range(NT):
                    products(quarter, t, first[quarter])
                    yield None
                free[quarter] = [last(lane_pe)]
            second = [load(2), load(3)]
            for t in range(NT):
                products(2, t, second[0])
                products(3, t, second[1])
                yield t, last(lane_dve)

        def mlp():
            FF = T["w_up_3"].shape[2]
            Q = 2 * P
            XH, XL, HH, HL = (SPLIT[n] for n in ("XH", "XL", "HH", "HL"))
            relu_ring = Ring([WS[0][:, i * HALF:(i + 1) * HALF] for i in range(4)])
            chunks = []
            for c in range(0, FF, Q):
                chunks += [(T["w_up_3"][0][:, c:c + Q], KD), (T["w_down_3"][0][c:c + Q, :], 2)]
            loaded = each_loaded(chunks)
            inner_free = []
            for c in range(0, FF, Q):
                _, wh, wl, w_ready = next(loaded)
                for half in range(2):
                    toks = slice(half * HALF, (half + 1) * HALF)
                    for ct in range(2):
                        cs = slice(ct * P, (ct + 1) * P)
                        bank, mm = product_split(HALF, KD, lambda k: (wh[:, k, cs], wl[:, k, cs]),
                                                 lambda k: (XH[:, k, toks], XL[:, k, toks]), [w_ready])
                        r, free = relu_ring.take()
                        a = act(S.activation, r, bank[:, :], ACT.Relu, after=[mm] + free)
                        psum.give(bank, [a])
                        sq = pool(G.tensor_tensor, r, r, r, ALU.mult, after=[a])
                        a = act(S.activation, HH[:, ct, toks], r, ACT.Copy, after=[sq] + inner_free)
                        inner = dve(V.tensor_tensor, HL[:, ct, toks], r, HH[:, ct, toks], ALU.subtract, after=[a])
                        relu_ring.give(r, [inner])
                    if half == 0:
                        first_inner = inner
                _, wh, wl, w_ready = next(loaded)
                for t in range(NT):
                    ts = slice(t * P, (t + 1) * P)
                    for c0 in (0, HALF):
                        bank, mm = product_split(HALF, 2, lambda k: (HH[:, k, ts], HL[:, k, ts]),
                                                 lambda k: (wh[:, k, c0:c0 + HALF], wl[:, k, c0:c0 + HALF]),
                                                 [w_ready, first_inner if t < NT // 2 else inner])
                        psum.give(bank, [(add_to_H if c else residual_evac)(bank, t, c0, mm)])
                    yield (t, last(lane_dve)) if c + Q == FF else None
                inner_free = [last(lane_pe)]
            next(loaded, None)

        def gate_quarter(quarter):
            Q = 2 * P
            return load_split(T["w_ple_gate_3"][0][:, quarter * Q:(quarter + 1) * Q], KD)

        def embed_gate(loaded):
            Q = 2 * P
            XH, XL = SPLIT["XH"], SPLIT["XL"]
            PN = MIX[:, 4:6, :].rearrange("p c (t n) -> p (c t) n", n=Q)
            PTT = MIX[:, 6:8, :]
            WP = WS[0][:, 0:2048].rearrange("p (k n) -> p k n", k=2)
            pl = dma(PN, T["p_3"][0, 0].rearrange("(t p) n -> p t n", p=P), dma_misc)
            pl = dma(WP, T["w_ple_3"][0].rearrange("(k p) n -> p k n", p=P), dma_misc)
            for c in range(2):
                for hf in range(2):
                    bank, tr = transposes([PN[:, hf * 4 + i, c * P:(c + 1) * P] for i in range(4)], after=[pl])
                    psum.give(bank, [copy_out(PTT[:, c, hf * HALF:(hf + 1) * HALF], bank[:, :], [tr])])
            ready = both()
            ring = Ring([WS[0][:, 2048 + i * Q:2048 + (i + 1) * Q] for i in range(8)])

            def products(quarter, t):
                _, wh, wl, w_ready = loaded[quarter]
                ts = slice(t * P, (t + 1) * P)
                c0 = quarter * Q
                bank, mm = product_split(Q, KD, lambda k: (XH[:, k, ts], XL[:, k, ts]),
                                         lambda k: (wh[:, k, :], wl[:, k, :]), [w_ready])
                g, free = ring.take()
                a = act(S.activation, g, bank[:, 0:Q], ACT.Sigmoid, after=[mm] + free)
                psum.give(bank, [a])

                def evac_p(b, mm):
                    d = dve(V.tensor_tensor, g, g, b[:, 0:Q], ALU.mult, after=[mm, a])
                    h = H[:, t, c0:c0 + Q]
                    ring.give(g, [dve(V.scalar_tensor_tensor, h, h, ALPHA, g, ALU.mult, ALU.add)])
                    return d

                product_N(WP, pl, PTT, 2, t, evac_p, after=ready, n=Q, c0=c0)

            for quarter in range(2):
                for t in range(NT):
                    products(quarter, t)
                    yield None
                split_w.give(loaded[quarter][0], [last(lane_pe)])
                loaded.append(gate_quarter(quarter + 2))
            for t in range(NT):
                products(2, t)
                products(3, t)
                yield t, last(lane_dve)

        def weave(*gens, pieces=None):
            gens = list(zip(gens, pieces or [1] * len(gens)))
            while gens:
                for g in list(gens):
                    for _ in range(g[1]):
                        if next(g[0], "end") == "end":
                            gens.remove(g)
                            break
                yield

        def run(gen):
            for _ in gen:
                pass

        def store_H(ready, src=None):
            if not outs:
                for t in range(NT):
                    outs.append(dma(out[0, t * P:(t + 1) * P, :], H[:, t, :], dma_out, after=ready))
            st = outs[-1]
            lane_sp.items.append((None, (), {}, [st], Step(lane_sp, -1)))

        def block1():
            follow(((t, x_in[t]) for t in range(NT)), rms_tile("norm_g"))
            boundary()
            run(weave(rwkv(), band_attention(), pieces=(1, 1)))
            boundary()
            gate = gate_T_pieces(T["w_in_e"][0], 1664, lambda ct: MIX[:, ct, :], ACT.Silu)
            next(gate)
            for t in range(NT):
                x_again = dma(H[:, t, :], T["x"][0, t * P:(t + 1) * P, :], dma_x)
            lane_dve.items.append((None, (), {}, [x_again], last(lane_dve)))
            run(gate)
            follow(projected_out(T["w_out_e"][0], MIX, KD, [last(lane_pool)], add_to_H), rms_tile("norm_g'"))
            load_early([(T["w_in_o"][0], D, HALF)], KD)
            boundary()
            odd_layer()

        def block2():
            if 1 not in BLOCKS:
                follow(((t, x_in[t]) for t in range(NT)), rms_tile("norm_g_2"))
                boundary()
            for ln in (lane_dve, lane_act, lane_pool):
                ln.items.append((None, (), {}, residual_kept[-1:], last(ln)))
            run(weave(window_attention(), conformer()))
            load_early([(Z2, CQ, HALF)], KD)
            boundary()
            Y0 = WORK[:, 0:4096].rearrange("p (c n) -> p c n", c=4)
            Y1 = WORK[:, 4096:8192].rearrange("p (c n) -> p c n", c=4)
            Y2 = H_AREA[:, 0:4096].rearrange("p (c n) -> p c n", c=4)

            def join(branch, gate_at, w_o, Y):
                yield from gate_T_pieces(Z2, gate_at, lambda ct: Y[:, ct, :], ACT.Silu)
                yield from merge(branch, w_o, Y, [last(lane_pool)])

            def first_joins():
                yield from join(0, AG, T["w_o_attn_2"][0], Y0)
                yield from join(1, BG, T["w_o_conv_2"][0], Y1)

            diff = differential()
            next(diff)
            run(weave(diff, first_joins(), pieces=(1, 1)))
            load_early([(Z2, CG, HALF)], KD)
            boundary()
            run(join(2, CG, T["w_o_diff_2"][0], Y2))
            load_early([(T["w_out_2"][0], 0, HALF)], KD)
            boundary()
            h_again = []

            def residual_back():
                for t in range(NT):
                    h_again.append(dma(H[:, t, :], residual_src(t), dma_x_tile[t], after=residual_kept))

            load_row("grow", "emb_ln_g_3")
            rows = load_row("brow", "emb_ln_b_3")
            follow(projected_out(T["w_out_2"][0], MIX, KD, [],
                                 lambda b, t, c0, mm: add_to_H(b, t, c0, mm, [] if c0 else [h_again[t]]),
                                 residual_back), ln_tile(rows) if 3 in BLOCKS else no_tile)
            if 3 in BLOCKS:
                load_early([(T["w_in_3"][0], 1536, HALF)], KD)
            boundary()

        def block3():
            if 2 not in BLOCKS:
                load_row("grow", "emb_ln_g_3")
                rows = load_row("brow", "emb_ln_b_3")
                follow(((t, x_in[t]) for t in range(NT)), ln_tile(rows))
                boundary()
            stick_and_pool()
            boundary()
            start_split()
            load_row("grow", "ln1_g_3")
            rows = load_row("brow", "ln1_b_3")
            follow(out_projection(), ln_tile(rows))
            boundary()
            load_row("grow", "ln2_g_3")
            rows = load_row("brow", "ln2_b_3")
            follow(mlp(), ln_tile(rows))
            first_quarters = [gate_quarter(0), gate_quarter(1)]
            boundary()
            load_row("grow", "ln3_g_3")
            rows = load_row("brow", "ln3_b_3")
            follow(embed_gate(first_quarters), ln_tile(rows, transposed=False, stored=True))

        def no_tile(t, ready):
            yield

        def residual_src(t):
            if 1 in BLOCKS:
                return T["residual"][t * P:(t + 1) * P, :]
            return T["x"][0, t * P:(t + 1) * P, :]

        for n in BLOCKS:
            (block1, block2, block3)[n - 1]()
        store_H([last(lane_dve), last(lane_act), last(lane_pool)])

        for ln in lanes + [lane_sp]:
            count_values(ln)
        block = ctx.enter_context(nc.Block())

        @block.sync
        def _(eng):
            emit(lane_sp, eng)

        @block.tensor
        def _(eng):
            emit(lane_pe, eng)

        @block.vector
        def _(eng):
            emit(lane_dve, eng)

        @block.scalar
        def _(eng):
            emit(lane_act, eng)

        @block.gpsimd
        def _(eng):
            emit(lane_pool, eng)


_NAMES = """x norm_g w_in_e shift_mu rw_w0 rw_w2 rw_a0 rw_a2 rw_kk rw_ka rw_rk rw_lnx_g rw_lnx_b att_bias w_out_e
w_in_o sg_ln_g sg_ln_b sg_w sg_b w_out_o final_g norm_g_2 w_in_2 attn_q_norm_g_2 attn_k_norm_g_2 attn_sinks_2
w_o_attn_2 conv_w_2 conv_b_2 conv_norm_g_2 conv_norm_b_2 w_o_conv_2 diff_q_norm_g_2 diff_k_norm_g_2 lambda_q_2
lambda_k_2 diff_subln_g_2 w_o_diff_2 w_out_2 p_3 emb_ln_g_3 emb_ln_b_3 w_in_3 attn_out_g_3 w_pool_3 pool_scale_3
w_out_3 ln1_g_3 ln1_b_3 w_up_3 w_down_3 ln2_g_3 ln2_b_3 w_ple_3 w_ple_gate_3 ln3_g_3 ln3_b_3""".split()


def kernel(**inputs):
    import concourse.bacc as bacc
    from concourse.bass_utils import run_bass_kernel_spmd

    nc = bacc.Bacc("TRN2", target_bir_lowering=False, num_devices=1)
    arrays, T = {}, {}
    arrays = {n: np.ascontiguousarray(inputs[n]) for n in _NAMES}
    arrays["channel_columns"] = channel_columns(inputs)
    rev = inputs["att_bias"][0][:, ::-1]
    wide = np.concatenate([np.repeat(rev[:, :1], P - 1, axis=1), rev], axis=1)
    arrays["att_bias_wide"] = np.ascontiguousarray(np.broadcast_to(wide, (P,) + wide.shape))
    arrays["att_bias_far"] = np.ascontiguousarray(rev[:, 0])
    for n, a in arrays.items():
        T[n] = nc.dram_tensor(n, a.shape, F32, kind="ExternalInput").ap()
    T["residual"] = nc.dram_tensor("residual", (SEQ, D), F32, kind="Internal").ap()
    out = nc.dram_tensor("out", (1, SEQ, D), F32, kind="ExternalOutput").ap()
    build(nc, T, out)
    return run_bass_kernel_spmd(nc, [arrays], core_ids=[0]).results[0]["out"]
```
